# Optimizing a Trainium2 kernel written in Bass

```python
import jax, jax.numpy as jnp
from jax import lax
import numpy as np
import math

D_MODEL = 1024
BATCH = 1
SEQ = 256
DEPTH = 1

GRID_W = 64
CTX_LEN = 256

RET_HEADS = 8
RET_QK_DIM = 128
RET_V_DIM = 256
RET_QK = RET_HEADS * RET_QK_DIM
RET_V = RET_HEADS * RET_V_DIM
RET_CHUNK = 128
ROPE_BASE = 10000.0

CONV_DIM = D_MODEL
CONV_WIDTH = 31
N_BRANCHES = 2

N_GROUPS = 4
EXPERTS_PER_GROUP = 8
N_EXPERTS = N_GROUPS * EXPERTS_PER_GROUP
EXPERT_TOP_K = 2
EXPERT_FF = 512

LN_EPS = 1e-5
ALPHA = (2.0 * DEPTH) ** 0.25
BETA = (8.0 * DEPTH) ** -0.25

Q_OFF = 0
K_OFF = Q_OFF + RET_QK
V_OFF = K_OFF + RET_QK
G_OFF = V_OFF + RET_V
GLU_OFF = G_OFF + RET_V
GATE_OFF = GLU_OFF + 2 * CONV_DIM
IN_COLS = GATE_OFF + N_BRANCHES * D_MODEL


def _layernorm(x, g, b):
    xf = x.astype(jnp.float32)
    mu = xf.mean(-1, keepdims=True)
    var = jnp.square(xf - mu).mean(-1, keepdims=True)
    return (xf - mu) * lax.rsqrt(var + LN_EPS) * g + b

def _head_norm(o):
    of = o.astype(jnp.float32)
    mu = of.mean(-1, keepdims=True)
    var = jnp.square(of - mu).mean(-1, keepdims=True)
    return (of - mu) * lax.rsqrt(var + LN_EPS)

def _modulate(h, shift, scale):
    return h * (1.0 + scale) + shift

def _rope_2d(rows):
    r, col = jnp.meshgrid(jnp.arange(rows), jnp.arange(GRID_W), indexing='ij')
    r = r.reshape(-1).astype(jnp.float32)
    col = col.reshape(-1).astype(jnp.float32)
    n_freq = RET_QK_DIM // 4
    inv = ROPE_BASE ** (-jnp.arange(n_freq, dtype=jnp.float32) / n_freq)
    ang = jnp.concatenate([r[:, None] * inv, col[:, None] * inv], axis=-1)
    ang = jnp.concatenate([ang, ang], axis=-1)
    return jnp.cos(ang), jnp.sin(ang)

def _apply_rope(t, cos, sin):
    t1, t2 = jnp.split(t, 2, axis=-1)
    rot = jnp.concatenate([-t2, t1], axis=-1)
    return t * cos[None, :, None, :] + rot * sin[None, :, None, :]

def _split_proj(proj):
    b_, l_ = proj.shape[:2]
    q = proj[..., Q_OFF:K_OFF].reshape(b_, l_, RET_HEADS, RET_QK_DIM)
    k = proj[..., K_OFF:V_OFF].reshape(b_, l_, RET_HEADS, RET_QK_DIM) * RET_QK_DIM ** -0.5
    v = proj[..., V_OFF:G_OFF].reshape(b_, l_, RET_HEADS, RET_V_DIM)
    g = proj[..., G_OFF:GLU_OFF]
    glu = proj[..., GLU_OFF:GATE_OFF]
    gates = proj[..., GATE_OFF:]
    return q, k, v, g, glu, gates

def _retention_chunked(q, k, v, log_gamma, s0):
    b_, l_, h_, _ = q.shape
    dv = v.shape[-1]
    n_chunks = l_ // RET_CHUNK
    pos = jnp.arange(RET_CHUNK, dtype=jnp.float32)
    diff = pos[:, None] - pos[None, :]
    intra = jnp.where(diff >= 0, jnp.exp(jnp.maximum(diff, 0.0)[None] * log_gamma[:, None, None]), 0.0)
    q_dec = jnp.exp((pos[:, None] + 1.0) * log_gamma[None, :])
    k_dec = jnp.exp((RET_CHUNK - 1.0 - pos)[:, None] * log_gamma[None, :])
    c_dec = jnp.exp(RET_CHUNK * log_gamma)

    def to_chunks(t):
        return jnp.moveaxis(t.reshape(b_, n_chunks, RET_CHUNK, h_, t.shape[-1]), 1, 0)

    def step(s, qkv):
        qc, kc, vc = qkv
        scores = jnp.einsum('bihd,bjhd->bhij', qc, kc) * intra
        o = (jnp.einsum('bhij,bjhv->bihv', scores, vc)
             + jnp.einsum('bihd,bhdv->bihv', qc * q_dec[None, :, :, None], s))
        s = s * c_dec[None, :, None, None] + jnp.einsum('bjhd,bjhv->bhdv', kc * k_dec[None, :, :, None], vc)
        return s, o

    s_fin, o = lax.scan(step, s0, (to_chunks(q), to_chunks(k), to_chunks(v)))
    o = jnp.moveaxis(o, 0, 1).reshape(b_, l_, h_, dv)
    return o, s_fin

def _retention_bidir(q, k, v, lg_f, lg_b, s0_f, s0_b):
    o_f, s_f = _retention_chunked(q, k, v, lg_f, s0_f)
    o_b, s_b = _retention_chunked(q[:, ::-1], k[:, ::-1], v[:, ::-1], lg_b, s0_b)
    return o_f + o_b[:, ::-1], s_f, s_b

def _retention_final_state(k, v, log_gamma):
    l_ = k.shape[1]
    w = jnp.exp((l_ - 1.0 - jnp.arange(l_, dtype=jnp.float32))[:, None] * log_gamma[None, :])
    return jnp.einsum('blhd,blhv->bhdv', k * w[None, :, :, None], v)

def _depthwise_conv(z, w, b):
    out = lax.conv_general_dilated(
        z, w[:, None, :].astype(z.dtype), window_strides=(1,),
        padding=[(CONV_WIDTH // 2, CONV_WIDTH // 2)],
        dimension_numbers=('NWC', 'WIO', 'NWC'), feature_group_count=z.shape[-1])
    return out + b

def _merge_branches(o_ret, g, glu, gates, p):
    b_, l_ = g.shape[:2]
    ret = jax.nn.silu(g.astype(jnp.float32)) * _head_norm(o_ret).reshape(b_, l_, RET_V)
    y_a = ret @ p['w_ret_out']
    za, zb = jnp.split(glu, 2, axis=-1)
    z = za * jax.nn.sigmoid(zb)
    z = _depthwise_conv(z, p['conv_dw'], p['conv_dw_b'])
    z = jax.nn.silu(_layernorm(z, p['conv_ln_g'], p['conv_ln_b']))
    y_b = z @ p['w_conv_out'] + p['b_conv_out']
    ga, gb = jnp.split(jax.nn.sigmoid(gates.astype(jnp.float32)), 2, axis=-1)
    return (ga * y_a + gb * y_b) @ p['w_mix_out'] + p['b_mix_out']

def _hier_moe(u, p):
    b_, l_, d_ = u.shape
    t = u.reshape(b_ * l_, d_)
    grp_p = jax.nn.softmax((t @ p['w_router_grp'] + p['b_router_grp']).astype(jnp.float32), axis=-1)
    grp_w, grp_idx = lax.top_k(grp_p, 1)
    exp_logits = (t @ p['w_router_exp'] + p['b_router_exp']).astype(jnp.float32)
    exp_logits = exp_logits.reshape(-1, N_GROUPS, EXPERTS_PER_GROUP)
    in_grp = jnp.take_along_axis(exp_logits, grp_idx[:, :, None], axis=1)[:, 0]
    top_w, top_i = lax.top_k(jax.nn.softmax(in_grp, axis=-1), EXPERT_TOP_K)
    top_w = top_w / top_w.sum(-1, keepdims=True) * grp_w
    eid = grp_idx * EXPERTS_PER_GROUP + top_i
    combine = jnp.einsum('nk,nke->ne', top_w, jax.nn.one_hot(eid, N_EXPERTS, dtype=jnp.float32))
    y = jnp.zeros(t.shape, jnp.float32)
    for e in range(N_EXPERTS):
        h = jax.nn.silu(t @ p['w_exp_gate'][e]) * (t @ p['w_exp_up'][e])
        y = y + combine[:, e:e + 1] * (h @ p['w_exp_down'][e])
    return y.reshape(b_, l_, d_)

def _layer(h_lat, h_ctx, s_lat, s_ctx, p, cos, sin, update_ctx):
    mod_lat = s_lat @ p['w_ada'] + p['b_ada']
    mod_ctx = s_ctx @ p['w_ada'] + p['b_ada']
    sh_m, sc_m, gt_m, sh_f, sc_f, gt_f = jnp.split(mod_lat[:, None, :], 6, axis=-1)
    csh_m, csc_m, cgt_m, csh_f, csc_f, cgt_f = jnp.split(mod_ctx, 6, axis=-1)
    lg_f = jax.nn.log_sigmoid(p['ret_decay_fwd'].astype(jnp.float32))
    lg_b = jax.nn.log_sigmoid(p['ret_decay_bwd'].astype(jnp.float32))
    b_ = h_lat.shape[0]

    u_ctx = _modulate(h_ctx, csh_m, csc_m)
    if update_ctx:
        q_c, k_c, v_c, g_c, glu_c, gates_c = _split_proj(u_ctx @ p['w_in'] + p['b_in'])
        zeros = jnp.zeros((b_, RET_HEADS, RET_QK_DIM, RET_V_DIM), jnp.float32)
        o_c, s_f, s_b = _retention_bidir(q_c, k_c, v_c, lg_f, lg_b, zeros, zeros)
    else:
        kv = u_ctx @ p['w_in'][:, K_OFF:G_OFF] + p['b_in'][K_OFF:G_OFF]
        k_c = kv[..., :RET_QK].reshape(b_, -1, RET_HEADS, RET_QK_DIM) * RET_QK_DIM ** -0.5
        v_c = kv[..., RET_QK:].reshape(b_, -1, RET_HEADS, RET_V_DIM)
        s_f = _retention_final_state(k_c, v_c, lg_f)
        s_b = _retention_final_state(k_c[:, ::-1], v_c[:, ::-1], lg_b)

    u_lat = _modulate(h_lat, sh_m, sc_m)
    q, k, v, g, glu, gates = _split_proj(u_lat @ p['w_in'] + p['b_in'])
    q = _apply_rope(q, cos, sin)
    k = _apply_rope(k, cos, sin)
    o, _, _ = _retention_bidir(q, k, v, lg_f, lg_b, s_f, s_b)
    mix = _merge_branches(o, g, glu, gates, p)
    h_lat = _layernorm(ALPHA * h_lat + gt_m * mix, p['ln1_g'], p['ln1_b'])
    moe = _hier_moe(_modulate(h_lat, sh_f, sc_f), p)
    h_lat = _layernorm(ALPHA * h_lat + gt_f * moe, p['ln2_g'], p['ln2_b'])

    if update_ctx:
        mix_c = _merge_branches(o_c, g_c, glu_c, gates_c, p)
        h_ctx = _layernorm(ALPHA * h_ctx + cgt_m * mix_c, p['ln1_g'], p['ln1_b'])
        moe_c = _hier_moe(_modulate(h_ctx, csh_f, csc_f), p)
        h_ctx = _layernorm(ALPHA * h_ctx + cgt_f * moe_c, p['ln2_g'], p['ln2_b'])
    return h_lat, h_ctx

def first_inputs(seed: int = 0) -> dict:
    key = jax.random.key(seed)
    ks = jax.random.split(key, 32)
    f32 = jnp.float32
    D = D_MODEL

    def nrm(k, shape, scale):
        return jax.random.normal(k, shape, f32) * scale

    gamma0 = 1.0 - 2.0 ** (-5.0 - np.arange(RET_HEADS))
    logit0 = jnp.asarray(np.log(gamma0 / (1.0 - gamma0)), f32)
    return {
        'x': nrm(ks[0], (BATCH, SEQ, D), 1.0),
        'c': nrm(ks[1], (BATCH, D), 1.0),
        'ctx': nrm(ks[2], (BATCH, CTX_LEN, D), 1.0),
        'c_ctx': nrm(ks[3], (D,), 1.0),
        'w_ada': nrm(ks[4], (DEPTH, D, 6 * D), 0.5 * D ** -0.5),
        'b_ada': nrm(ks[5], (DEPTH, 6 * D), 0.01),
        'w_in': nrm(ks[6], (DEPTH, D, IN_COLS), D ** -0.5),
        'b_in': nrm(ks[7], (DEPTH, IN_COLS), 0.01),
        'ret_decay_fwd': logit0 + nrm(ks[8], (DEPTH, RET_HEADS), 0.1),
        'ret_decay_bwd': logit0 + nrm(ks[9], (DEPTH, RET_HEADS), 0.1),
        'w_ret_out': nrm(ks[10], (DEPTH, RET_V, D), RET_V ** -0.5),
        'conv_dw': nrm(ks[11], (DEPTH, CONV_WIDTH, CONV_DIM), CONV_WIDTH ** -0.5),
        'conv_dw_b': nrm(ks[12], (DEPTH, CONV_DIM), 0.01),
        'conv_ln_g': 1.0 + nrm(ks[13], (DEPTH, CONV_DIM), 0.02),
        'conv_ln_b': nrm(ks[14], (DEPTH, CONV_DIM), 0.01),
        'w_conv_out': nrm(ks[15], (DEPTH, CONV_DIM, D), CONV_DIM ** -0.5),
        'b_conv_out': nrm(ks[16], (DEPTH, D), 0.01),
        'w_mix_out': nrm(ks[17], (DEPTH, D, D), BETA * D ** -0.5),
        'b_mix_out': nrm(ks[18], (DEPTH, D), 0.01),
        'ln1_g': 1.0 + nrm(ks[19], (DEPTH, D), 0.02),
        'ln1_b': nrm(ks[20], (DEPTH, D), 0.01),
        'w_router_grp': nrm(ks[21], (DEPTH, D, N_GROUPS), D ** -0.5),
        'b_router_grp': nrm(ks[22], (DEPTH, N_GROUPS), 0.01),
        'w_router_exp': nrm(ks[23], (DEPTH, D, N_EXPERTS), D ** -0.5),
        'b_router_exp': nrm(ks[24], (DEPTH, N_EXPERTS), 0.01),
        'w_exp_gate': nrm(ks[25], (DEPTH, N_EXPERTS, D, EXPERT_FF), D ** -0.5),
        'w_exp_up': nrm(ks[26], (DEPTH, N_EXPERTS, D, EXPERT_FF), D ** -0.5),
        'w_exp_down': nrm(ks[27], (DEPTH, N_EXPERTS, EXPERT_FF, D), BETA * EXPERT_FF ** -0.5),
        'ln2_g': 1.0 + nrm(ks[28], (DEPTH, D), 0.02),
        'ln2_b': nrm(ks[29], (DEPTH, D), 0.01),
    }

def first_block(x, c, ctx, c_ctx, w_ada, b_ada, w_in, b_in, ret_decay_fwd, ret_decay_bwd, w_ret_out,
              conv_dw, conv_dw_b, conv_ln_g, conv_ln_b, w_conv_out, b_conv_out, w_mix_out, b_mix_out,
              ln1_g, ln1_b, w_router_grp, b_router_grp, w_router_exp, b_router_exp,
              w_exp_gate, w_exp_up, w_exp_down, ln2_g, ln2_b):
    rows = x.shape[1] // GRID_W
    cos, sin = _rope_2d(rows)
    s_lat = jax.nn.silu(c)
    s_ctx = jax.nn.silu(c_ctx)
    h_lat, h_ctx = x, ctx
    for layer in range(DEPTH):
        p = dict(
            w_ada=w_ada[layer], b_ada=b_ada[layer], w_in=w_in[layer], b_in=b_in[layer],
            ret_decay_fwd=ret_decay_fwd[layer], ret_decay_bwd=ret_decay_bwd[layer],
            w_ret_out=w_ret_out[layer], conv_dw=conv_dw[layer], conv_dw_b=conv_dw_b[layer],
            conv_ln_g=conv_ln_g[layer], conv_ln_b=conv_ln_b[layer], w_conv_out=w_conv_out[layer],
            b_conv_out=b_conv_out[layer], w_mix_out=w_mix_out[layer], b_mix_out=b_mix_out[layer],
            ln1_g=ln1_g[layer], ln1_b=ln1_b[layer], w_router_grp=w_router_grp[layer],
            b_router_grp=b_router_grp[layer], w_router_exp=w_router_exp[layer],
            b_router_exp=b_router_exp[layer], w_exp_gate=w_exp_gate[layer], w_exp_up=w_exp_up[layer],
            w_exp_down=w_exp_down[layer], ln2_g=ln2_g[layer], ln2_b=ln2_b[layer])
        h_lat, h_ctx = _layer(h_lat, h_ctx, s_lat, s_ctx, p, cos, sin, layer + 1 < DEPTH)
    return h_lat


EPS = 1e-6
CHUNK = 128
GM_GROUPS = 8
GM_GROUP_DIM = 64
GM_WIDTH = GM_GROUPS * GM_GROUP_DIM
WINDOW = 128
Q_HEADS = 8
KV_HEADS = 2
Q_PER_KV = Q_HEADS // KV_HEADS
HEAD_DIM = 64
ATTN_WIDTH = Q_HEADS * HEAD_DIM
KV_WIDTH = KV_HEADS * HEAD_DIM
REL_BUCKETS = 32
REL_MAX_EXACT = REL_BUCKETS // 2
REL_MAX_DIST = 128
N_GROUPS_MOE = 4
EXPERTS_PER_GROUP_2 = 4
N_EXPERTS_2 = N_GROUPS_MOE * EXPERTS_PER_GROUP_2
TOP_K = 2
MASK_VALUE = -1e30

SPLIT_SIZES = (GM_WIDTH, GM_WIDTH, ATTN_WIDTH, KV_WIDTH, KV_WIDTH, D_MODEL, D_MODEL)
SPLIT_POINTS = tuple(int(v) for v in np.cumsum(SPLIT_SIZES)[:-1])
IN_WIDTH = int(sum(SPLIT_SIZES))


def rms_norm(x, g):
    xf = x.astype(jnp.float32)
    y = xf * lax.rsqrt(jnp.mean(xf * xf, axis=-1, keepdims=True) + EPS)
    return (y * g.astype(jnp.float32)).astype(x.dtype)

def layer_norm(x, g):
    xf = x.astype(jnp.float32)
    mu = jnp.mean(xf, axis=-1, keepdims=True)
    xc = xf - mu
    y = xc * lax.rsqrt(jnp.mean(xc * xc, axis=-1, keepdims=True) + EPS)
    return (y * g.astype(jnp.float32)).astype(x.dtype)

def t5_causal_bucket(dist):
    is_small = dist < REL_MAX_EXACT
    nf = jnp.maximum(dist, 1).astype(jnp.float32)
    large = REL_MAX_EXACT + (
        jnp.log(nf / REL_MAX_EXACT) / math.log(REL_MAX_DIST / REL_MAX_EXACT)
        * (REL_BUCKETS - REL_MAX_EXACT)).astype(jnp.int32)
    large = jnp.minimum(large, REL_BUCKETS - 1)
    return jnp.where(is_small, dist, large)

def gmlp_chunk_mixer(u_raw, v_raw, v_norm_g, w_s, b_s):
    B, S, _ = u_raw.shape
    u = jax.nn.gelu(u_raw)
    v = layer_norm(jax.nn.gelu(v_raw), v_norm_g)
    v = v.reshape(B, S // CHUNK, CHUNK, GM_GROUPS, GM_GROUP_DIM)
    causal = jnp.tril(jnp.ones((CHUNK, CHUNK), dtype=bool))
    ws = jnp.where(causal[None], w_s, jnp.zeros((), w_s.dtype)).astype(v.dtype)
    sv = jnp.einsum("gts,bcsgd->bctgd", ws, v)
    sv = sv + b_s.T.astype(v.dtype)[None, None, :, :, None]
    return u * sv.reshape(B, S, GM_WIDTH)

def swa_sink_attention(q, k, v, sinks, rel_bias):
    B, S, _ = q.shape
    nb = S // WINDOW
    q = q.reshape(B, nb, WINDOW, KV_HEADS, Q_PER_KV, HEAD_DIM)
    k = k.reshape(B, nb, WINDOW, KV_HEADS, HEAD_DIM)
    v = v.reshape(B, nb, WINDOW, KV_HEADS, HEAD_DIM)
    k_prev = jnp.concatenate([jnp.zeros_like(k[:, :1]), k[:, :-1]], axis=1)
    v_prev = jnp.concatenate([jnp.zeros_like(v[:, :1]), v[:, :-1]], axis=1)
    kb = jnp.concatenate([k_prev, k], axis=2)
    vb = jnp.concatenate([v_prev, v], axis=2)

    scores = jnp.einsum("bnqkgd,bnskd->bnkgqs", q, kb,
                        preferred_element_type=jnp.float32) * (HEAD_DIM ** -0.5)

    qi = jnp.arange(WINDOW, dtype=jnp.int32)[:, None]
    sj = jnp.arange(2 * WINDOW, dtype=jnp.int32)[None, :]
    dist = qi + WINDOW - sj
    in_window = (dist >= 0) & (dist < WINDOW)
    bucket = t5_causal_bucket(jnp.clip(dist, 0, WINDOW - 1))
    bias = rel_bias.astype(jnp.float32)[bucket]
    bias = bias.transpose(2, 0, 1).reshape(KV_HEADS, Q_PER_KV, WINDOW, 2 * WINDOW)
    blk = jnp.arange(nb, dtype=jnp.int32)[:, None, None]
    valid = in_window[None] & ((blk > 0) | (sj[None] >= WINDOW))

    scores = scores + bias[None, None]
    scores = jnp.where(valid[None, :, None, None], scores, MASK_VALUE)
    sink = sinks.astype(jnp.float32).reshape(KV_HEADS, Q_PER_KV)[None, None, :, :, None, None]
    m = jnp.maximum(jnp.max(scores, axis=-1, keepdims=True), sink)
    p = jnp.exp(scores - m)
    denom = jnp.sum(p, axis=-1, keepdims=True) + jnp.exp(sink - m)
    probs = (p / denom).astype(vb.dtype)
    out = jnp.einsum("bnkgqs,bnskd->bnqkgd", probs, vb)
    return out.reshape(B, S, ATTN_WIDTH)

def hierarchical_moe(h, rg_w, rg_b, re_w, re_b, w_gate, w_up, w_down):
    B, S, D = h.shape
    t = h.reshape(-1, D)
    g_logits = jnp.dot(t, rg_w, preferred_element_type=jnp.float32) + rg_b.astype(jnp.float32)
    g_probs = jax.nn.softmax(g_logits, axis=-1)
    g_top_p, g_top_i = lax.top_k(g_probs, 1)
    e_all = jnp.einsum("td,gde->tge", t, re_w,
                       preferred_element_type=jnp.float32) + re_b.astype(jnp.float32)
    e_logits = jnp.take_along_axis(e_all, g_top_i[:, :, None], axis=1)[:, 0]
    e_top_v, e_top_i = lax.top_k(e_logits, TOP_K)
    w_top = jax.nn.softmax(e_top_v, axis=-1) * g_top_p
    expert_id = g_top_i * EXPERTS_PER_GROUP_2 + e_top_i
    combine = jnp.einsum("tk,tke->te", w_top,
                         jax.nn.one_hot(expert_id, N_EXPERTS_2, dtype=jnp.float32))
    combine = combine.astype(t.dtype)
    out = jnp.zeros_like(t)
    for e in range(N_EXPERTS_2):
        hid = jax.nn.silu(t @ w_gate[e]) * (t @ w_up[e])
        out = out + combine[:, e:e + 1] * (hid @ w_down[e])
    return out.reshape(B, S, D)

def second_inputs(seed: int = 0) -> dict:
    key = jax.random.key(seed)
    ks = jax.random.split(key, 20)
    f32 = jnp.float32
    nrm = lambda k, shape, scale: jax.random.normal(k, shape, f32) * scale
    L = DEPTH
    return {
        "x": jax.random.normal(ks[0], (BATCH, SEQ, D_MODEL), f32),
        "attn_norm_g": 1.0 + nrm(ks[1], (L, D_MODEL), 0.02),
        "w_in": nrm(ks[2], (L, D_MODEL, IN_WIDTH), D_MODEL ** -0.5),
        "gm_v_norm_g": 1.0 + nrm(ks[3], (L, GM_WIDTH), 0.02),
        "gm_w_spatial": nrm(ks[4], (L, GM_GROUPS, CHUNK, CHUNK), CHUNK ** -0.5),
        "gm_b_spatial": 1.0 + nrm(ks[5], (L, GM_GROUPS, CHUNK), 0.02),
        "attn_sinks": nrm(ks[6], (L, Q_HEADS), 0.5),
        "rel_bias": nrm(ks[7], (REL_BUCKETS, Q_HEADS), 0.5),
        "w_proj_a": nrm(ks[8], (L, GM_WIDTH, D_MODEL), GM_WIDTH ** -0.5),
        "w_proj_b": nrm(ks[9], (L, ATTN_WIDTH, D_MODEL), ATTN_WIDTH ** -0.5),
        "w_out": nrm(ks[10], (L, D_MODEL, D_MODEL), D_MODEL ** -0.5),
        "ffn_norm_g": 1.0 + nrm(ks[11], (L, D_MODEL), 0.02),
        "router_group_w": nrm(ks[12], (L, D_MODEL, N_GROUPS_MOE), D_MODEL ** -0.5),
        "router_group_b": nrm(ks[13], (L, N_GROUPS_MOE), 0.01),
        "router_expert_w": nrm(ks[14], (L, N_GROUPS_MOE, D_MODEL, EXPERTS_PER_GROUP_2), D_MODEL ** -0.5),
        "router_expert_b": nrm(ks[15], (L, N_GROUPS_MOE, EXPERTS_PER_GROUP_2), 0.01),
        "expert_w_gate": nrm(ks[16], (L, N_EXPERTS_2, D_MODEL, EXPERT_FF), D_MODEL ** -0.5),
        "expert_w_up": nrm(ks[17], (L, N_EXPERTS_2, D_MODEL, EXPERT_FF), D_MODEL ** -0.5),
        "expert_w_down": nrm(ks[18], (L, N_EXPERTS_2, EXPERT_FF, D_MODEL), EXPERT_FF ** -0.5),
        "final_norm_g": 1.0 + nrm(ks[19], (D_MODEL,), 0.02),
    }

def second_block(x, attn_norm_g, w_in, gm_v_norm_g, gm_w_spatial, gm_b_spatial, attn_sinks,
              rel_bias, w_proj_a, w_proj_b, w_out, ffn_norm_g, router_group_w, router_group_b,
              router_expert_w, router_expert_b, expert_w_gate, expert_w_up, expert_w_down,
              final_norm_g):
    h = x
    for l in range(DEPTH):
        hn = rms_norm(h, attn_norm_g[l])
        proj = hn @ w_in[l]
        u_raw, v_raw, q, k, v, gate_a, gate_b = jnp.split(proj, SPLIT_POINTS, axis=-1)
        a = gmlp_chunk_mixer(u_raw, v_raw, gm_v_norm_g[l], gm_w_spatial[l], gm_b_spatial[l])
        b = swa_sink_attention(q, k, v, attn_sinks[l], rel_bias)
        merged = (jax.nn.sigmoid(gate_a) * (a @ w_proj_a[l])
                  + jax.nn.sigmoid(gate_b) * (b @ w_proj_b[l]))
        h = h + merged @ w_out[l]
        hn = rms_norm(h, ffn_norm_g[l])
        h = h + hierarchical_moe(hn, router_group_w[l], router_group_b[l], router_expert_w[l],
                                 router_expert_b[l], expert_w_gate[l], expert_w_up[l],
                                 expert_w_down[l])
    return rms_norm(h, final_norm_g)


def setup_inputs(seed=0):
    out = dict(first_inputs(seed))
    for name, value in second_inputs(seed + 1).items():
        if name != "x":
            out[name + "_2"] = value
    return out


def reference(
    x, c, ctx, c_ctx, w_ada, b_ada, w_in, b_in, ret_decay_fwd, ret_decay_bwd, w_ret_out,
    conv_dw, conv_dw_b, conv_ln_g, conv_ln_b, w_conv_out, b_conv_out, w_mix_out, b_mix_out,
    ln1_g, ln1_b, w_router_grp, b_router_grp, w_router_exp, b_router_exp, w_exp_gate, w_exp_up,
    w_exp_down, ln2_g, ln2_b, attn_norm_g_2, w_in_2, gm_v_norm_g_2, gm_w_spatial_2,
    gm_b_spatial_2, attn_sinks_2, rel_bias_2, w_proj_a_2, w_proj_b_2, w_out_2, ffn_norm_g_2,
    router_group_w_2, router_group_b_2, router_expert_w_2, router_expert_b_2, expert_w_gate_2,
    expert_w_up_2, expert_w_down_2, final_norm_g_2,
):
    x = first_block(
        x, c, ctx, c_ctx, w_ada, b_ada, w_in, b_in, ret_decay_fwd, ret_decay_bwd, w_ret_out,
        conv_dw, conv_dw_b, conv_ln_g, conv_ln_b, w_conv_out, b_conv_out, w_mix_out, b_mix_out,
        ln1_g, ln1_b, w_router_grp, b_router_grp, w_router_exp, b_router_exp, w_exp_gate,
        w_exp_up, w_exp_down, ln2_g, ln2_b,
    )
    return second_block(
        x, attn_norm_g_2, w_in_2, gm_v_norm_g_2, gm_w_spatial_2, gm_b_spatial_2, attn_sinks_2,
        rel_bias_2, w_proj_a_2, w_proj_b_2, w_out_2, ffn_norm_g_2, router_group_w_2,
        router_group_b_2, router_expert_w_2, router_expert_b_2, expert_w_gate_2, expert_w_up_2,
        expert_w_down_2, final_norm_g_2,
    )


_drawn_inputs = setup_inputs


def setup_inputs(seed=0):
    import zlib

    import numpy as np

    out = dict(_drawn_inputs(seed))
    spreads = {}
    factors = {'b_ada': 6.688,
     'b_in': 5.553,
     'conv_dw_b': 8.0,
     'conv_ln_g': 26.888,
     'conv_ln_b': 50.034,
     'b_conv_out': 39.945,
     'b_mix_out': 13.141,
     'b_router_grp': 23.813,
     'b_router_exp': 27.188,
     'ln2_b': 2.965,
     'attn_norm_g_2': 3.647,
     'gm_v_norm_g_2': 31.41,
     'gm_b_spatial_2': 20.75,
     'attn_sinks_2': 34.176,
     'router_group_b_2': 26.672,
     'router_expert_b_2': 31.264,
     'ln1_b': 3.247,
     'ffn_norm_g_2': 8.0,
     'router_group_w_2': 3.119,
     'router_expert_w_2': 3.538,
     'expert_w_gate_2': 2.738}
    for name, (base, spread) in spreads.items():
        noise = np.random.default_rng([zlib.crc32(name.encode()), seed]).standard_normal(out[name].shape)
        drawn = base * np.exp(spread * noise) if base else spread * noise
        out[name] = __import__('jax').numpy.asarray(drawn.astype(out[name].dtype))
    for name, factor in factors.items():
        out[name] = (out[name] * factor).astype(out[name].dtype)
    return out
```

```python
from contextlib import ExitStack

import numpy as np

import concourse.bass as bass
from concourse import mybir

F32 = mybir.dt.float32
ALU = mybir.AluOpType
ACT = mybir.ActivationFunctionType
AX = mybir.AxisListType

P = 128
D = 1024
L = 256
DT = D // P
LT = L // P
HEADS, DV = 8, 256
TAPS = 31
HALO = TAPS // 2
RING = 3
BLK = 4096
LN_EPS, RMS_EPS = 1e-5, 1e-6
KSCALE = 128 ** -0.5
ALPHA = 2.0 ** 0.25
GROUPS = 4
EXPERTS = (32, 16)
SLOTS = 64
QH, HD = 8, 64
MASKED = -1e30


def columns(*parts):
    at, out = 0, {}
    for name, n in parts:
        out[name] = at
        at += n
    return out, at


VCOLS, NV = columns(("b_ada", 48), ("b_q", 8), ("b_k", 8), ("b_za", 8), ("b_zb", 8), ("b_gates", 16),
                    ("conv_b", 8), ("conv_g", 8), ("conv_lb", 8), ("b_conv", 8), ("b_mix", 8), ("ln1_g", 8),
                    ("ln1_b", 8), ("ln2_g", 8), ("ln2_b", 8), ("attn_g", 8), ("ffn_g", 8), ("final_g", 8),
                    ("taps", 8 * TAPS))
RCOLS, NR = columns(("decay", 16), ("rb0", 36), ("rb1", 20), ("sinks", 8), ("gm_g", 512))
CCOLS, NC = columns(("ident", 128), ("ones", 128), ("rot", 128), ("cos", 256), ("sin", 256), ("dpos", 512),
                    ("dneg", 512), ("ln2", 512), ("nfb", 512), ("mctx", 4), ("causal", 128), ("iota", 32), ("tri", 128), ("pcol", 1))


def make_jobs():
    jobs, srcs = [], []
    for src, n, kinds in (("ada", 12, ["ada"]), ("glu", 4, ["cm8"]), ("k", 2, ["cm8", "tm8c"]),
                          ("v", 4, ["tm8", "tm8c"]), ("q", 2, ["cm8"]), ("g", 4, ["tm8"]), ("gates", 4, ["cm8"]),
                          ("ret", 4, ["cm16"]), ("cout", 2, ["cm8"]), ("mix", 2, ["cm8"]),
                          ("u2", 1, ["cm8"]), ("v2", 1, ["tm8"]), ("q2", 1, ["cm8"]), ("kv2", 1, ["kv"]),
                          ("gates2", 4, ["cm8"]), ("pa", 1, ["cm4", "cm4"]), ("pb", 1, ["cm4", "cm4"]),
                          ("out2", 2, ["cm8"])):
        for b in range(n):
            for half, kind in enumerate(kinds):
                i = len(jobs)
                jobs.append(dict(src=src, b=b, kind=kind, half=half, w=len(srcs), i=i, pair=i % 2, use=i // 2))
            srcs.append((src, b))
    last_of = {j["w"]: j["i"] for j in jobs}
    return jobs, {(j["src"], j["b"], j["half"]): j for j in jobs}, srcs, last_of


def build(nc, a):
    jobs, J, srcs, last_of = make_jobs()
    moe_w = [srcs.index(("u2", 0)), len(srcs)]
    with ExitStack() as ctx:
        def sb(name, shape):
            return ctx.enter_context(nc.sbuf_tensor(name, shape, F32))

        def sem(name):
            return ctx.enter_context(nc.semaphore(name))

        ring = sb("ring", [P, RING, BLK])
        const = sb("const", [P, NC])
        vec = sb("vec", [P, NV])
        row = sb("row", [P, NR])
        wr = [sb("wr0", [P, DT, 36]), sb("wr1", [P, DT, 20])]
        hT = sb("hT", [P, DT, L])
        uT = sb("uT", [P, DT, L])
        RA = sb("RA", [P, 2 * DT, L])
        kT = sb("kT", [P, DT, L])
        qT = sb("qT", [P, DT, L])
        Kc = sb("Kc", [P, DT, L])
        Vc = sb("Vc", [P, 2 * DT, L])
        V = sb("V", [P, 2 * DT, L])
        biasr = sb("biasr", [P, 2, 512])
        zpad = sb("zpad", [P, DT, L + 2 * HALO])
        conv = sb("conv", [P, DT, L])
        raw = sb("raw", [P, 4, L])
        Eqd = sb("Eqd", [P, 4, L])
        qd = sb("qd", [P, 4, L])
        Ddec = sb("Ddec", [P, 4, L])
        kw = sb("kw", [P, 4, L])
        S0s = sb("S0s", [P, 4, L])
        Ph = sb("Ph", [P, 4, L])
        adaS = sb("adaS", [P, 2, P])
        modT = sb("modT", [P, 2, 48])
        sT = sb("sT", [P, DT, 32])
        cin = sb("cin", [P, DT, 2])
        lgs = sb("lgs", [P, 6, 16])
        wctx = sb("wctx", [P, LT, 2, 8])
        mv = sb("mv", [P, LT, HEADS, 2])
        rstd = sb("rstd", [P, LT * HEADS])
        bst = sb("bst", [P, LT, 6])
        rs = sb("rs", [P, L])
        rt = biasr[:, :, :].rearrange("p a n -> p (a n)")

        def flat(t):
            return t[:, :, :].rearrange("p a n -> p (a n)")
        xg, ys = flat(raw)[:, 0:512], flat(Ph)[:, 0:512]
        xts = flat(qd)[:, 0:512].rearrange("p (c m) -> p c m", c=4)
        hid, sg = qd[:, 2, :], Eqd[:, 0, :]
        hts = qd[:, 3, :].rearrange("p (c m) -> p c m", c=2)
        yg = flat(V).rearrange("p (a n) -> p a n", a=4)
        hot, rel = flat(Vc)[0:32, 0:384], flat(Vc)[0:32, 512:512 + QH]
        outside, relb = flat(Vc)[0:QH, 1024:1408], flat(Vc)[0:QH, 1536:1920]
        pT = flat(zpad)
        gu, aT, bT = conv[:, 0:4, :], conv[:, 4:8, :], Eqd
        q2, k2, v2 = RA[:, 0:4, :], RA[:, 4, :], RA[:, 5, :]
        ws = flat(S0s).rearrange("p (g t) -> p g t", g=8)
        tab = adaS[:, :, :].rearrange("p a n -> p (a n)").bitcast(mybir.dt.int32)
        idx = lgs[:, :, :].rearrange("p a n -> p (a n)").bitcast(mybir.dt.uint32)
        ctxT, ucT = RA[:, 0:DT], RA[:, DT:2 * DT]
        Kct = flat(Kc).rearrange("p (a n) -> p a n", a=LT)
        Vct = flat(Vc).rearrange("p (a n) -> p a n", a=LT)
        Vt = flat(V).rearrange("p (a n) -> p a n", a=LT)
        On = flat(RA).rearrange("p (a n) -> p a n", a=LT)
        retT, gT, mT, SQ = Vc, V, kT, qT
        raw2 = flat(raw).rearrange("p (a n) -> p a n", a=LT)
        PP = [ctx.enter_context(nc.psum_tensor(f"PP{i}", [P, 4, L], F32)) for i in range(2)]
        MB = [ctx.enter_context(nc.psum_tensor(f"MB{i}", [P, 2, L], F32)) for i in range(4)]
        PPt = [p[:, :, :].rearrange("p a n -> p (a n)").rearrange("p (a n) -> p a n", a=LT) for p in PP]

        xs_d = [nc.dram_tensor(f"xs_d{n}", [2 * L + SLOTS, D], F32, kind="Internal").ap() for n in range(2)]
        ys_d = [nc.dram_tensor(f"ys_d{n}", [(E + 2 * L // SLOTS) * 2 * SLOTS, D // 2], F32, kind="Internal").ap()
                for n, E in enumerate(EXPERTS)]
        relb_d = nc.dram_tensor("relb_d", [QH, P, 384], F32, kind="Internal")

        RT, _ = columns(("lt", 72), ("gd", 8), ("e2", 2), ("gm", 2), ("gw", 2), ("cm", 2), ("eq", 16), ("c", 16), ("hg", 8),
                        ("ml", 16), ("m1", 2), ("m2", 2), ("h1", 16), ("h2", 16), ("w1", 2), ("w2", 2), ("tmp", 64),
                        ("A1", 64), ("A2", 64), ("M", 64), ("rank", 64), ("rank2", 64), ("Sa", 96), ("Sb", 96),
                        ("vx", 64), ("q", 32), ("item", 2), ("pos", 12), ("mx", 8), ("sk", 8), ("den", 8))
        assert _ <= 1024
        widths = dict(zip(list(RT), [b - c for c, b in zip(list(RT.values()), list(RT.values())[1:] + [_])]))

        def r_(name):
            return rt[:, RT[name]:RT[name] + widths[name]]

        def cst(name, n):
            return const[:, CCOLS[name]:CCOLS[name] + n]

        def col(name, t):
            return vec[:, VCOLS[name] + t:VCOLS[name] + t + 1]

        def rowc(name, n):
            return row[:, RCOLS[name]:RCOLS[name] + n]
        ident, ones, rotm = cst("ident", P), cst("ones", P), cst("rot", P)
        lg = lgs[:, 5, :]

        ld_c, ld_small, ld_x = sem("ld_c"), sem("ld_small"), sem("ld_x")
        w_full = [sem(f"w_full{i}") for i in range(RING)]
        job_done = sem("job_done")
        pair_free = [sem("pair_free0"), sem("pair_free1")]
        dve_own, act_own = sem("dve_own"), sem("act_own")
        zeroed, silu_c, ada_turned, mod_part, u_mod, u_ready = (sem(n) for n in (
            "zeroed", "silu_c", "ada_turned", "mod_part", "u_mod", "u_ready"))
        lg_abs, lg_exp, lg_ready, wctx_exp = (sem(n) for n in ("lg_abs", "lg_exp", "lg_ready", "wctx_exp"))
        sig_ready, raw_rot, rope_done = sem("sig_ready"), sem("raw_rot"), sem("rope_done")
        bias_full = [sem("bias_full0"), sem("bias_full1")]
        dec_arg, dec_ready, prep, s0_ps, sc_ps, s0_sb, p_sb, o_ps, o_kept, o_stat = (sem(n) for n in (
            "dec_arg", "dec_ready", "head_prep", "s0_ps", "sc_ps", "s0_sb", "p_sb", "o_ps", "o_kept", "o_stat"))
        var_ready, std_ready, g_silu, ret_ready, ret_turned, ret_kept = (sem(n) for n in (
            "var_ready", "std_ready", "g_silu", "ret_ready", "ret_turned", "ret_kept"))
        conv_ready, mix_in, h_mid, h_ready = sem("conv_ready"), sem("mix_in"), sem("h_mid"), sem("h_ready")
        ln_pe, ln_dve, ln_act = sem("ln_pe"), sem("ln_dve"), sem("ln_act")
        out_done = sem("out_done")
        moe = []
        for n in range(2):
            moe.append({k: sem(f"{k}{n}") for k in (
                "uf_ready", "logits", "gexp_in", "eexp_in", "gexp_out", "eexp_out", "hot_ready", "ranks", "items_in", "items_ps", "items_ready",
                "idx_ready", "u_turned", "u_rows", "xs_done", "x_full", "wg_full", "wu_full", "wd_full", "xt_ps",
                "xts_ready", "gate_done", "up_done", "down_done", "sg_ready", "hid_ready", "ht_ps", "ht_ready", "y_kept",
                "ys_stored", "ys_free", "spare", "yg_full", "y_sum", "y_turned")})
        b2 = {k: sem(f"b2_{k}") for k in ("ld", "relb_ps", "relb_sb", "relb_dram", "relb_full", "gelu_u", "gelu_v", "vvar",
                                          "vstd", "v_ready", "qk_ready", "v2_ready", "ws_ready", "sp_ps", "a_ready",
                                          "sc_ps", "sc_sb", "p_exp", "p_ready", "p_turned", "p_kept", "b_ps", "b_ready",
                                          "m_ready")}

        LNS, tot = {}, [0, 0, 0]
        for name, mean in (("conv", 1), ("ln1", 1), ("ln2", 1), ("attn", 0), ("ffn", 0), ("final", 0)):
            LNS[name] = dict(mean=mean, pe=tot[0], dve=tot[1], act=tot[2])
            tot = [tot[0] + 1 + mean, tot[1] + 2 + mean, tot[2] + 3]
            LNS[name]["end"] = tot[2]

        def w_wait(eng, w):
            eng.wait_ge(w_full[w % RING], 16 * (w // RING + 1))

        def job_wait(eng, j):
            eng.wait_ge(job_done, j["i"] + 1)

        class Own:

            def __init__(self, eng, sem_):
                self.eng, self.sem, self.n = eng, sem_, 0

            def link(self, ins):
                self.n += 1
                ins.then_inc(self.sem, 1)
                self.eng.wait_ge(self.sem, self.n)

        def say(eng, ins, sem_, value):
            ins.then_inc(sem_, 1)
            eng.wait_ge(sem_, value)

        block = ctx.enter_context(nc.Block())

        @block.sync
        def _(sp):
            def load(w):
                src, b = srcs[w]
                if w >= RING and not moe_w[0] <= w < moe_w[0] + RING:
                    sp.wait_ge(job_done, last_of[w - RING] + 1)
                s = a["w_" + src]
                sp.dma_start(ring[:, w % RING, 0:s.shape[2]], s[b]).then_inc(w_full[w % RING], 16)

            def experts(n):
                m, s = moe[n], a[f"w_moe{n}"]
                part = (("wg_full", "gate_done"), ("wu_full", "up_done"), ("wd_full", "down_done"))
                for q in range(3):
                    sp.wait_ge(job_done, last_of[max(w for w in range(moe_w[n]) if w % RING == q)] + 1)
                    sp.dma_start(ring[:, q, :], s[q]).then_inc(m[part[q][0]], 16)
                sp.wait_ge(m["xs_done"], 80)
                for h in range(2):
                    sp.dma_start(xg[SLOTS * h:SLOTS * (h + 1), :], xs_d[n][0:SLOTS, h * 512:(h + 1) * 512]).then_inc(m["x_full"], 16)
                sp.wait_ge(m["items_ready"], 1)
                T = sp.value_load(tab[0:1, 128:129], min_val=EXPERTS[n], max_val=EXPERTS[n] + 8)
                with sp.Fori(1, T) as i:
                    e = sp.value_load(tab[0:1, bass.ds(i, 1)], min_val=0, max_val=EXPERTS[n] - 1)
                    r = sp.value_load(tab[0:1, bass.ds(i + 64, 1)], min_val=0, max_val=2 * L)
                    sp.wait_ge(m["xt_ps"], i)
                    for h in range(2):
                        sp.dma_start(xg[SLOTS * h:SLOTS * (h + 1), :], xs_d[n][bass.ds(r, SLOTS), h * 512:(h + 1) * 512]
                                     ).then_inc(m["x_full"], 16)
                    for q in range(3):
                        sp.wait_ge(m[part[q][1]], i)
                        sp.dma_start(ring[:, q, :], s[bass.ds(3 * e + q, 1)].rearrange("a p n -> p (a n)")
                                     ).then_inc(m[part[q][0]], 16)
                sp.wait_ge(m["xt_ps"], T)
                for h in range(2):
                    sp.dma_start(xg[SLOTS * h:SLOTS * (h + 1), :], xs_d[n][0:SLOTS, h * 512:(h + 1) * 512]).then_inc(m["x_full"], 16)
                return [(m[x[1]], T) for x in part]

            for w in range(moe_w[0]):
                load(w)
            used = experts(0)
            for w in range(moe_w[0], moe_w[1]):
                if w < moe_w[0] + RING:
                    sp.wait_ge(*used[w % RING])
                load(w)
            experts(1)
            sp.wait_ge(ln_act, LNS["final"]["end"])
            sp.dma_start(a["out"], uT[:, :, :]).then_inc(out_done, 16)
            sp.wait_ge(out_done, 16)
        def routed(pool, n):
            m = moe[n]
            pool.wait_ge(m["u_rows"], 1)
            pool.dma_start(xs_d[n][2 * L:2 * L + SLOTS, :], Kct[0:SLOTS, 0, :]).then_inc(m["xs_done"], 16)
            pool.dma_start(ys_d[n][EXPERTS[n] * 2 * SLOTS:, :].rearrange("(b p) c -> p b c", p=P),
                           Kct[:, 0, 0:512].unsqueeze(1).to_broadcast([P, 2 * L // SLOTS, 512])).then_inc(m["spare"], 16)
            pool.wait_ge(m["spare"], 16)
            pool.wait_ge(m["idx_ready"], 1)
            for k in range(2):
                for t in range(LT):
                    pool.indirect_dma_start(xs_d[n], bass.IndirectOffsetOnAxis(ap=idx[:, 2 * k + t:2 * k + t + 1], axis=0),
                                            Kct[:, t, :], None).then_inc(m["xs_done"], 16)
            pool.sem_inc(m["ys_free"], 1)
            pool.wait_ge(m["items_ready"], 1)
            T = pool.value_load(tab[0:1, 128:129], min_val=EXPERTS[n], max_val=EXPERTS[n] + 8)
            with pool.Fori(0, T) as i:
                pool.wait_ge(m["y_kept"], i + 2)
                pool.dma_start(ys_d[n][bass.ds(i * 2 * SLOTS, 2 * SLOTS), :], ys[:, :]).then_inc(m["ys_stored"], 16)
                pool.wait_ge(m["ys_stored"], i * 16 + 16)
                pool.sem_inc(m["ys_free"], 1)
            for k in range(2):
                for t in range(LT):
                    for h in range(2):
                        c = 4 + 4 * k + 2 * t + h
                        pool.indirect_dma_start(yg[:, 2 * k + t, h * 512:(h + 1) * 512], None, ys_d[n],
                                                bass.IndirectOffsetOnAxis(ap=idx[:, c:c + 1], axis=0)).then_inc(m["yg_full"], 16)

        @block.gpsimd
        def _(pool):
            nc.gpsimd.memset(sT[:, :, :], 0.0).then_inc(zeroed, 1)
            nc.gpsimd.memset(zpad[:, :, 0:HALO], 0.0).then_inc(zeroed, 1)
            nc.gpsimd.memset(zpad[:, :, L + HALO:L + 2 * HALO], 0.0).then_inc(zeroed, 1)
            for n in range(10):
                if n >= 2:
                    src, b = (("k", n - 2), ("v", n - 4), ("v", n - 4), ("g", n - 8))[min((n - 2) // 2, 3)]
                    j = J[src, b, 0 if src == "g" else 1]
                    pool.wait_ge(pair_free[j["pair"]], j["use"] + 1)
                pool.dma_start(biasr[:, n % 2, :], a["bias_rows"][:, n * 512:(n + 1) * 512].partition_broadcast(P)
                               ).then_inc(bias_full[n % 2], 16)
            routed(pool, 0)
            pool.wait_ge(moe[0]["y_turned"], 1)
            pool.dma_start(flat(S0s), a["ws"].rearrange("s g t -> s (g t)")).then_inc(b2["ld"], 16)
            for g in range(8):
                pool.dma_start(flat(Ph)[64 * (g % 2):64 * (g % 2) + 64, (g // 2) * P:(g // 2 + 1) * P],
                               a["gm_b"][:, g * P:(g + 1) * P].partition_broadcast(64)).then_inc(b2["ld"], 16)
            pool.dma_start(hot, a["hot"]).then_inc(b2["ld"], 16)
            pool.dma_start(rel, a["rel"]).then_inc(b2["ld"], 16)
            pool.dma_start(outside, a["outside"]).then_inc(b2["ld"], 16)
            pool.wait_ge(b2["relb_dram"], 16)
            for h in range(QH):
                pool.dma_start(RA[:, DT + h, :], bass.AP(tensor=relb_d, offset=h * P * 384 + 127, ap=[[383, P], [1, L]])
                               ).then_inc(b2["relb_full"], 16)
            routed(pool, 1)

        @block.scalar
        def _(act):
            own = Own(act, act_own)
            act.dma_start(cin[:, :, :], a["cT"]).then_inc(ld_c, 16)
            act.dma_start(vec[:, :], a["vec"]).then_inc(ld_small, 16)
            act.dma_start(const[:, :], a["const"]).then_inc(ld_small, 16)
            act.dma_start(row[:, :], a["rows"].partition_broadcast(P)).then_inc(ld_small, 16)
            act.dma_start(wr[0][:, :, :], a["wr0"]).then_inc(ld_small, 16)
            act.dma_start(wr[1][:, :, :], a["wr1"]).then_inc(ld_small, 16)
            act.dma_start(hT[:, :, :], a["xT"]).then_inc(ld_x, 16)
            act.dma_start(ctxT, a["ctxT"]).then_inc(ld_x, 16)
            act.wait_ge(ld_c, 16)
            act.wait_ge(zeroed, 1)
            nc.scalar.activation(sT[:, :, 0:2], cin[:, :, :], ACT.Silu).then_inc(silu_c, 1)
            act.wait_ge(lg_abs, 1)
            nc.scalar.activation(lgs[:, 1, :], lgs[:, 0, :], ACT.Exp, scale=-1.0).then_inc(lg_exp, 1)
            act.wait_ge(lg_ready, 1)
            nc.scalar.activation(wctx[:, :, :, :], wctx[:, :, :, :], ACT.Exp).then_inc(wctx_exp, 1)
            act.wait_ge(ld_x, 32)
            act.wait_ge(u_mod, 1)
            for r, (src, dst) in enumerate(((hT, uT), (ctxT, ucT))):
                for t in range(DT):
                    ins = nc.scalar.activation(dst[:, t, :], src[:, t, :], ACT.Identity, bias=modT[:, r, t:t + 1],
                                               scale=modT[:, r, 8 + t:9 + t])
                ins.then_inc(u_ready, 1)
            for b in range(4):
                j = J["glu", b, 0]
                job_wait(act, j)
                for i in range(2):
                    ins = nc.scalar.activation(raw[:, 2 * (b % 2) + i, :], PP[j["pair"]][:, 2 + i, :], ACT.Sigmoid,
                                               bias=col("b_zb", 2 * b + i))
                ins.then_inc(sig_ready, 1)

            def raw_copy(r, src, b, bias):
                j = J[src, b, 0]
                job_wait(act, j)
                if r:
                    act.wait_ge(rope_done, r)
                else:
                    act.wait_ge(pair_free[1], J["glu", 3, 0]["use"] + 1)
                for i in range(4):
                    ins = nc.scalar.activation(raw[:, i, :], PP[j["pair"]][:, i, :], ACT.Identity,
                                               bias=col(bias, 4 * b + i))
                ins.then_inc(pair_free[j["pair"]], 1)
            for r, (src, b, bias) in enumerate((("k", 0, "b_k"), ("k", 1, "b_k"), ("q", 0, "b_q"), ("q", 1, "b_q"))):
                raw_copy(r, src, b, bias)
            nfb = cst("nfb", 512)

            def exps(h):
                act.wait_ge(lg_ready, 1)
                act.wait_ge(rope_done, 4)
                if h >= 2:
                    act.wait_ge(prep, h - 1)
                for d in range(2):
                    nc.scalar.activation(Eqd[:, 2 * (h % 2) + d, :], nfb[:, d * L:(d + 1) * L], ACT.Exp,
                                         scale=lg[:, 8 * d + h:8 * d + h + 1])
                act.wait_ge(dec_arg, h + 1)
                dd = Ddec[:, 2 * (h % 2):2 * (h % 2) + 2, :]
                nc.scalar.activation(dd, dd, ACT.Exp).then_inc(dec_ready, 1)

            def s0_copy(h):
                act.wait_ge(s0_ps, h + 1)
                if h >= 2:
                    act.wait_ge(o_ps, h - 1)
                nc.scalar.activation(S0s[:, 2 * (h % 2):2 * (h % 2) + 2, :], MB[0][:, :, :], ACT.Copy).then_inc(s0_sb, 1)

            def o_copy(h):
                act.wait_ge(o_ps, h + 1)
                nc.scalar.activation(On[:, :, h * DV:(h + 1) * DV], MB[2 + h % 2][:, :, :], ACT.Copy).then_inc(o_kept, 1)
            exps(0)
            for h in range(HEADS):
                if h + 1 < HEADS:
                    exps(h + 1)
                s0_copy(h)
                if h:
                    o_copy(h - 1)
            o_copy(HEADS - 1)
            act.wait_ge(var_ready, 1)
            nc.scalar.activation(rstd[:, :], rstd[:, :], ACT.Sqrt).then_inc(std_ready, 1)

            def turned_copy(b):
                act.wait_ge(ret_turned, b + 1)
                for q in range(2):
                    ins = nc.scalar.activation(retT[:, 4 * b + 2 * q:4 * b + 2 * q + 2, :], MB[2 * (b % 2) + q][:, :, :],
                                               ACT.Copy)
                ins.then_inc(ret_kept, 1)
            for b in range(4):
                j = J["g", b, 0]
                act.wait_ge(pair_free[j["pair"]], j["use"] + 1)
                nc.scalar.activation(raw[:, :, :], raw[:, :, :], ACT.Silu).then_inc(g_silu, 1)
                if b:
                    turned_copy(b - 1)
            turned_copy(3)
            for b in range(4):
                j = J["gates", b, 0]
                job_wait(act, j)
                for i in range(4):
                    ins = nc.scalar.activation(gT[:, 4 * b + i, :], PP[j["pair"]][:, i, :], ACT.Sigmoid,
                                               bias=col("b_gates", 4 * b + i))
                ins.then_inc(pair_free[j["pair"]], 1)

            def norm(name, src, dst, func, g, b):
                n = LNS[name]
                m = n["mean"]
                act.wait_ge(ln_dve, n["dve"] + m) if n["dve"] + m else None
                if name == "attn":
                    act.wait_ge(ln_act, LNS["ln2"]["end"])
                if name in ("ffn", "final") and not m:
                    act.wait_ge(h_ready, 2 if name == "ffn" else 3)
                say(act, nc.scalar.activation(SQ[:, :, :], dst[:, :, :] if m else src[:, :, :], ACT.Square), ln_act,
                    n["act"] + 1)
                act.wait_ge(ln_dve, n["dve"] + m + 1)
                nc.scalar.activation(rs[:, :], rs[:, :], ACT.Sqrt).then_inc(ln_act, 1)
                act.wait_ge(ln_dve, n["dve"] + m + 2)
                for t in range(DT):
                    ins = nc.scalar.activation(dst[:, t, :], dst[:, t, :], func, scale=col(g, t), bias=col(b, t) if b else 0.0)
                say(act, ins, ln_act, n["act"] + 3)
            norm("conv", conv, conv, ACT.Silu, "conv_g", "conv_lb")
            norm("ln1", hT, hT, ACT.Identity, "ln1_g", "ln1_b")
            act.wait_ge(u_mod, 2)
            for t in range(DT):
                ins = nc.scalar.activation(uT[:, t, :], hT[:, t, :], ACT.Identity, bias=modT[:, 0, 24 + t:25 + t],
                                           scale=modT[:, 0, 32 + t:33 + t])
            ins.then_inc(moe[0]["uf_ready"], 1)

            def route_and_experts(n):
                m = moe[n]
                for t in range(LT):
                    act.wait_ge(m["u_turned"], t + 1)
                    ins = nc.scalar.activation(Kct[:, t, :], flat(PP[t]), ACT.Copy)
                ins.then_inc(m["u_rows"], 1)
                act.wait_ge(m["gexp_in"], 1)
                nc.scalar.activation(r_("gd"), r_("gd"), ACT.Exp).then_inc(m["gexp_out"], 1)
                act.wait_ge(m["eexp_in"], 1)
                nc.scalar.activation(r_("e2"), r_("e2"), ACT.Exp).then_inc(m["eexp_out"], 1)
                act.wait_ge(m["xt_ps"], 1)
                nc.scalar.activation(xts, MB[0][:, :, :].rearrange("p a (b m) -> p (a b) m", b=2), ACT.Copy).then_inc(m["xts_ready"], 1)
                act.wait_ge(m["items_ready"], 1)
                T = act.value_load(tab[0:1, 128:129], min_val=EXPERTS[n], max_val=EXPERTS[n] + 8)
                with act.Fori(0, T) as i:
                    act.wait_ge(m["gate_done"], i + 1)
                    act.wait_ge(m["hid_ready"], i + 1)
                    nc.scalar.activation(sg, PP[0][:, 0, :], ACT.Silu).then_inc(m["sg_ready"], 1)
                    act.wait_ge(m["xt_ps"], i + 2)
                    nc.scalar.activation(xts, MB[0][:, :, :].rearrange("p a (b m) -> p (a b) m", b=2), ACT.Copy
                                         ).then_inc(m["xts_ready"], 1)
                    act.wait_ge(m["ht_ps"], i + 1)
                    nc.scalar.activation(hts, MB[1][:, 0, :].rearrange("p (c m) -> p c m", c=2), ACT.Copy
                                         ).then_inc(m["ht_ready"], 1)
            route_and_experts(0)
            norm("ln2", hT, hT, ACT.Identity, "ln2_g", "ln2_b")
            norm("attn", hT, uT, ACT.Identity, "attn_g", None)
            act.wait_ge(b2["relb_sb"], 1)
            act.dma_start(relb_d.ap(), relb[:, None, :].broadcast_to([QH, P, 384])).then_inc(b2["relb_dram"], 16)

            def copy_job(src, out, func, b=0, **kw):
                j = J[src, b, 0]
                job_wait(act, j)
                say(act, nc.scalar.activation(out, PP[j["pair"]][:, :, :], func, **kw), pair_free[j["pair"]], j["use"] + 1)
            copy_job("u2", gu, ACT.Gelu_apprx_tanh)
            copy_job("v2", raw[:, :, :], ACT.Gelu_apprx_tanh)
            copy_job("q2", q2, ACT.Copy)
            act.wait_ge(b2["vvar"], 1)
            nc.scalar.activation(rs[:, 0:2], rs[:, 0:2], ACT.Sqrt).then_inc(b2["vstd"], 1)
            j = J["kv2", 0, 0]
            job_wait(act, j)
            nc.scalar.activation(k2, PP[j["pair"]][:, 0, :], ACT.Copy, scale=HD ** -0.5)
            say(act, nc.scalar.activation(v2, PP[j["pair"]][:, 2, :], ACT.Copy), pair_free[j["pair"]], j["use"] + 1)
            copy_job("gates2", gT[:, 0:4, :], ACT.Sigmoid, 0)
            for qb in range(2):
                act.wait_ge(b2["sc_sb"], qb + 1)
                w0 = 0 if qb else P
                nc.scalar.activation(Kc[:, :, w0:L], Kc[:, :, w0:L], ACT.Exp)
                nc.scalar.activation(r_("sk"), r_("sk"), ACT.Exp).then_inc(b2["p_exp"], 1)
                copy_job("gates2", gT[:, 4 + 8 * qb:8 + 8 * qb, :], ACT.Sigmoid, 1 + 2 * qb)
                act.wait_ge(b2["p_turned"], qb + 1)
                for q in range(4 if qb else 2):
                    ins = nc.scalar.activation(pT[:, q * 512:(q + 1) * 512], flat(MB[q]), ACT.Copy)
                ins.then_inc(b2["p_kept"], 1)
                if not qb:
                    copy_job("gates2", gT[:, 8:12, :], ACT.Sigmoid, 2)
            norm("ffn", hT, uT, ACT.Identity, "ffn_g", None)
            route_and_experts(1)
            norm("final", hT, uT, ACT.Identity, "final_g", None)

        @block.tensor
        def _(pe):
            def job(j):
                w_wait(pe, j["w"])
                if j["use"]:
                    pe.wait_ge(pair_free[j["pair"]], j["use"])
                W, out, kind = ring[:, j["w"] % RING, :], PP[j["pair"]], j["kind"]
                if kind == "ada":
                    for k in range(DT):
                        for c in range(4):
                            ins = pe.matmul(out[32 * c:32 * c + 32, 0, 0:P], sT[:, k, :],
                                            W[:, k * 512 + c * P:k * 512 + (c + 1) * P], start=k == 0, stop=k == DT - 1,
                                            tile_position=(0, 32 * c))
                elif kind in ("cm8", "cm4", "cm16"):
                    K = int(kind[2:])
                    X = {"cm8": {"mix": mT, "cout": conv, "out2": mT}.get(j["src"], uT), "cm16": retT,
                         "cm4": {"pa": conv[:, 4:8], "pb": Eqd}.get(j["src"])}[kind]
                    width = 4096 // K
                    for c in range(2 if K == 16 else 4):
                        at = c * P + (512 * j["half"] if K == 4 else 0)
                        for k in range(K):
                            ins = pe.matmul(out[:, c, :], W[:, k * width + at:k * width + at + P], X[:, k, :],
                                            start=k == 0, stop=k == K - 1)
                elif kind in ("tm8", "tm8c"):
                    X = ucT if kind == "tm8c" else uT
                    for t in range(LT):
                        for k in range(DT):
                            ins = pe.matmul(out[:, 2 * t:2 * t + 2, :].rearrange("p a n -> p (a n)"),
                                            X[:, k, t * P:(t + 1) * P], W[:, k * 512:(k + 1) * 512], start=k == 0,
                                            stop=k == DT - 1)
                elif kind == "kv":
                    for k in range(DT):
                        pe.matmul(out[:, 0, :], W[:, k * 256:k * 256 + P], uT[:, k, :], start=k == 0, stop=k == DT - 1)
                    for t in range(LT):
                        for k in range(DT):
                            ins = pe.matmul(out[:, 2, t * P:(t + 1) * P], uT[:, k, t * P:(t + 1) * P],
                                            W[:, k * 256 + P:(k + 1) * 256], start=k == 0, stop=k == DT - 1)
                ins.then_inc(job_done, 1)

            def turn_ada(b):
                j = J["ada", b, 0]
                pe.wait_ge(pair_free[j["pair"]], j["use"] + 1)
                if b >= 2:
                    pe.wait_ge(mod_part, b - 1)
                pe.transpose(MB[b % 2][:, 0, 0:P], adaS[:, b % 2, :], ident).then_inc(ada_turned, 1)
            pe.wait_ge(silu_c, 1)
            pe.wait_ge(ld_small, 80)
            for b in range(12):
                job(J["ada", b, 0])
                if b:
                    turn_ada(b - 1)
            turn_ada(11)
            pe.wait_ge(u_ready, 2)
            for b in range(4):
                job(J["glu", b, 0])

            def rotate(r):
                j = J["kq"[r // 2], r % 2, 0]
                pe.wait_ge(pair_free[j["pair"]], j["use"] + 1)
                pe.wait_ge(rope_done, r) if r else pe.wait_ge(mod_part, 12)
                for q in range(2):
                    ins = pe.matmul(MB[q][:, :, :].rearrange("p a n -> p (a n)"), rotm,
                                    raw[:, 2 * q:2 * q + 2, :].rearrange("p a n -> p (a n)"), start=True, stop=True)
                ins.then_inc(raw_rot, 1)
            for b in range(2):
                job(J["k", b, 0])
                job(J["k", b, 1])
                rotate(b)
            for b in range(4):
                job(J["v", b, 0])
                job(J["v", b, 1])
            job(J["q", 0, 0])
            rotate(2)
            job(J["q", 1, 0])
            rotate(3)

            def scores(h):
                pe.wait_ge(prep, h + 1)
                if h:
                    pe.wait_ge(s0_sb, h)
                else:
                    pe.wait_ge(rope_done, 4)
                k4 = kw[:, :, :].rearrange("p a n -> p (a n)").rearrange("p (a n) -> p a n", n=P)
                for d in range(2):
                    for m in range(LT):
                        ins = pe.matmul(MB[0][:, d, :], k4[:, 4 * (h % 2) + 2 * d + m, :], Vct[:, m, h * DV:(h + 1) * DV],
                                        start=m == 0, stop=m == LT - 1)
                ins.then_inc(s0_ps, 1)
                if h:
                    pe.wait_ge(p_sb, h)
                for m in range(LT):
                    ins = pe.matmul(MB[1][:, m, :], kT[:, h, m * P:(m + 1) * P], qT[:, h, :], start=True, stop=True)
                ins.then_inc(sc_ps, 1)

            def mix_head(h):
                pe.wait_ge(s0_sb, h + 1)
                pe.wait_ge(p_sb, h + 1)
                if h >= 2:
                    pe.wait_ge(o_kept, h - 1)
                o, q = MB[2 + h % 2], 2 * (h % 2)
                for t in range(LT):
                    for m in range(LT):
                        pe.matmul(o[:, t, :], Ph[:, q + m, t * P:(t + 1) * P], Vt[:, m, h * DV:(h + 1) * DV],
                                  start=m == 0, stop=False)
                    for d in range(2):
                        ins = pe.matmul(o[:, t, :], qd[:, q + d, t * P:(t + 1) * P], S0s[:, q + d, :], start=False,
                                        stop=d == 1)
                ins.then_inc(o_ps, 1)
            scores(0)
            for h in range(HEADS):
                if h + 1 < HEADS:
                    scores(h + 1)
                mix_head(h)

            def turn_ret(b):
                pe.wait_ge(ret_ready, b + 1)
                if b >= 2:
                    pe.wait_ge(ret_kept, b - 1)
                for i in range(4):
                    for t in range(LT):
                        ins = pe.transpose(MB[2 * (b % 2) + i // 2][:, i % 2, t * P:(t + 1) * P],
                                           On[:, t, b * 512 + i * P:b * 512 + (i + 1) * P], ident)
                ins.then_inc(ret_turned, 1)
            for b in range(4):
                job(J["g", b, 0])
                if b:
                    turn_ret(b - 1)
            job(J["gates", 0, 0])
            turn_ret(3)
            for b in range(1, 4):
                job(J["gates", b, 0])

            def sums(name, src, out, first):
                n = LNS[name]
                for k in range(DT):
                    ins = pe.matmul(out[:, 0, :], ones, src[:, k, :], start=k == 0, stop=k == DT - 1)
                ins.then_inc(ln_pe, 1)

            def norm(name, src):
                n = LNS[name]
                if n["mean"]:
                    sums(name, src, MB[0], True)
                pe.wait_ge(ln_act, n["act"] + 1)
                sums(name, SQ, MB[1], False)
            pe.wait_ge(ret_kept, 4)
            pe.wait_ge(conv_ready, 1)
            sums("conv", conv, MB[0], True)
            job(J["ret", 0, 0])
            job(J["ret", 1, 0])
            pe.wait_ge(ln_act, LNS["conv"]["act"] + 1)
            sums("conv", SQ, MB[1], False)
            job(J["ret", 2, 0])
            job(J["ret", 3, 0])
            pe.wait_ge(ln_act, LNS["conv"]["end"])
            for b in range(2):
                job(J["cout", b, 0])
            pe.wait_ge(mix_in, 2)
            for b in range(2):
                job(J["mix", b, 0])
            pe.wait_ge(h_mid, 2)
            norm("ln1", hT)

            def route_and_experts(n):
                m, E = moe[n], EXPERTS[n]
                cols = GROUPS + E
                for t in range(LT):
                    for k in range(DT):
                        ins = pe.matmul(MB[2][:, 0, t * 64:t * 64 + cols], uT[:, k, t * P:(t + 1) * P], wr[n][:, k, :],
                                        start=k == 0, stop=k == DT - 1)
                ins.then_inc(m["logits"], 1)
                for t in range(LT):
                    pe.wait_ge(pair_free[t], J_uses[n][t])
                    for k in range(DT):
                        ins = pe.transpose(flat(PP[t])[:, k * P:(k + 1) * P], uT[:, k, t * P:(t + 1) * P], ident)
                    ins.then_inc(m["u_turned"], 1)
                pe.wait_ge(m["hot_ready"], 1)
                M, tri = r_("M"), cst("tri", P)
                pe.matmul(MB[3][:, 0, 0:E], tri, M[:, 0:E], start=True, stop=True)
                pe.matmul(MB[3][:, 0, E:2 * E], tri, M[:, E:2 * E], start=True, stop=False)
                pe.matmul(MB[3][:, 0, E:2 * E], ones, M[:, 0:E], start=False, stop=True)
                for t in range(LT):
                    ins = pe.matmul(MB[3][:, 0, 2 * E:3 * E], ones, M[:, t * E:(t + 1) * E], start=t == 0, stop=t == 1)
                ins.then_inc(m["ranks"], 1)
                pe.wait_ge(m["items_in"], 1)
                for q in range(2):
                    ins = pe.transpose(MB[3][0:1, 1, q * P:(q + 1) * P], r_("item")[:, q:q + 1], ident)
                ins.then_inc(m["items_ps"], 1)

                def turn_rows(ins=None):
                    for c in range(4):
                        ins = pe.transpose(MB[0][:, c // 2, (c % 2) * P:(c % 2 + 1) * P], xg[:, c * P:(c + 1) * P], ident)
                    ins.then_inc(m["xt_ps"], 1)
                pe.wait_ge(m["x_full"], 32)
                turn_rows()
                pe.wait_ge(m["u_rows"], 1)
                pe.wait_ge(m["items_ready"], 1)
                T = pe.value_load(tab[0:1, 128:129], min_val=EXPERTS[n], max_val=EXPERTS[n] + 8)
                with pe.Fori(0, T) as i:
                    pe.wait_ge(m["xts_ready"], i + 1)
                    pe.wait_ge(m["hid_ready"], i + 1)
                    for q, (full, done) in enumerate((("wg_full", "gate_done"), ("wu_full", "up_done"))):
                        pe.wait_ge(m[full], i * 16 + 16)
                        for k in range(DT):
                            for g in range(2):
                                ins = pe.matmul(PP[0][SLOTS * g:SLOTS * (g + 1), 2 * q, :],
                                                xts[:, k % 4, SLOTS * (k // 4):SLOTS * (k // 4 + 1)],
                                                ring[:, q, k * 512 + g * 256:k * 512 + (g + 1) * 256], start=k == 0,
                                                stop=k == DT - 1, tile_position=(0, SLOTS * g))
                        ins.then_inc(m[done], 1)
                    pe.wait_ge(m["x_full"], i * 32 + 64)
                    turn_rows()
                    pe.wait_ge(m["hid_ready"], i + 2)
                    for c in range(2):
                        ins = pe.transpose(MB[1][:, 0, c * P:(c + 1) * P], hid[:, c * P:(c + 1) * P], ident)
                    ins.then_inc(m["ht_ps"], 1)
                    pe.wait_ge(m["wd_full"], i * 16 + 16)
                    pe.wait_ge(m["y_kept"], i + 1)
                    pe.wait_ge(m["ht_ready"], i + 1)
                    for k in range(4):
                        for g in range(2):
                            ins = pe.matmul(PP[1][SLOTS * g:SLOTS * (g + 1), 0:2, :].rearrange("p a n -> p (a n)"),
                                            hts[:, k % 2, SLOTS * (k // 2):SLOTS * (k // 2 + 1)],
                                            ring[:, 2, k * D + g * 512:k * D + (g + 1) * 512], start=k == 0, stop=k == 3,
                                            tile_position=(0, SLOTS * g))
                    ins.then_inc(m["down_done"], 1)
                pe.wait_ge(m["y_sum"], 1)
                for k in range(DT):
                    for t in range(LT):
                        ins = pe.transpose(MB[k // 2][:, k % 2, t * P:(t + 1) * P], yg[:, t, k * P:(k + 1) * P], ident)
                ins.then_inc(m["y_turned"], 1)
            J_uses = [[0, 0], [0, 0]]
            for n in range(2):
                for j in jobs:
                    if j["w"] < moe_w[n]:
                        J_uses[n][j["pair"]] = j["use"] + 1
            pe.wait_ge(moe[0]["uf_ready"], 1)
            route_and_experts(0)
            pe.wait_ge(h_ready, 1)
            norm("ln2", hT)
            norm("attn", hT)
            pe.wait_ge(b2["ld"], 16 * 12)
            pe.matmul(flat(MB[2])[0:QH, 0:384], rel, hot, start=True, stop=True).then_inc(b2["relb_ps"], 1)
            pe.wait_ge(ln_act, LNS["attn"]["end"])
            for n in ("u2", "v2", "q2", "kv2", "gates2"):
                job(J[n, 0, 0])
            pe.wait_ge(b2["v_ready"], 1)
            pe.wait_ge(b2["ws_ready"], 1)
            for g in range(8):
                for c in range(LT):
                    ins = pe.matmul(MB[g // 4][64 * (g % 2):64 * (g % 2) + 64, (g // 2) % 2, c * P:(c + 1) * P],
                                    raw2[:, c, g * 64:(g + 1) * 64], ws[:, g, :], start=True, stop=True,
                                    tile_position=(0, 64 * (g % 2)))
            ins.then_inc(b2["sp_ps"], 1)

            def attn_scores(qb):
                if qb:
                    pe.wait_ge(b2["b_ready"], 1)
                else:
                    pe.wait_ge(b2["a_ready"], 1)
                    j = J["kv2", 0, 0]
                    pe.wait_ge(pair_free[j["pair"]], j["use"] + 1)
                per = 2 if qb else 4
                for h in range(QH):
                    at = 64 * (h // 4)
                    ins = pe.matmul(flat(MB[h // per])[:, (h % per) * (512 // per):(h % per + 1) * (512 // per)],
                                    q2[at:at + 64, h % 4, qb * P:(qb + 1) * P], k2[at:at + 64, 0:(qb + 1) * P],
                                    start=True, stop=True, tile_position=(at, 0))
                ins.then_inc(b2["sc_ps"], 1)

            def attn_turn(qb):
                pe.wait_ge(b2["p_ready"], qb + 1)
                i = 0
                for h in range(QH):
                    for kb in range(0 if qb else 1, 2):
                        ins = pe.transpose(flat(MB[i // 4])[:, (i % 4) * P:(i % 4 + 1) * P], Kc[:, h, kb * P:(kb + 1) * P], ident)
                        i += 1
                ins.then_inc(b2["p_turned"], 1)

            def attn_out(qb):
                pe.wait_ge(b2["p_kept"], qb + 1)
                n = qb + 1
                for h in range(QH):
                    for kb in range(n):
                        ins = pe.matmul(flat(MB[0])[64 * (h % 2):64 * (h % 2) + 64, (h // 2) * P:(h // 2 + 1) * P],
                                        v2[:, kb * P + 64 * (h // 4):kb * P + 64 * (h // 4) + 64],
                                        pT[:, (h * n + kb) * P:(h * n + kb + 1) * P], start=kb == 0, stop=kb == n - 1,
                                        tile_position=(0, 64 * (h % 2)))
                ins.then_inc(b2["b_ps"], 1)
            attn_scores(0)
            job(J["gates2", 1, 0])
            attn_turn(0)
            job(J["gates2", 2, 0])
            attn_out(0)
            attn_scores(1)
            job(J["gates2", 3, 0])
            attn_turn(1)
            job(J["pa", 0, 0])
            job(J["pa", 0, 1])
            attn_out(1)
            pe.wait_ge(b2["b_ready"], 2)
            job(J["pb", 0, 0])
            job(J["pb", 0, 1])
            pe.wait_ge(b2["m_ready"], 2)
            for b in range(2):
                job(J["out2", b, 0])
            norm("ffn", hT)
            pe.wait_ge(ln_act, LNS["ffn"]["end"])
            route_and_experts(1)
            norm("final", hT)

        @block.vector
        def _(dve):
            V_ = nc.vector
            own = Own(dve, dve_own)
            link = own.link

            def evac(j, ins):
                say(dve, ins, pair_free[j["pair"]], j["use"] + 1)
            dve.wait_ge(ld_small, 80)
            x = rowc("decay", 16)
            say(dve, V_.scalar_tensor_tensor(lgs[:, 0, :], x, -1.0, x, ALU.mult, ALU.max), lg_abs, 1)
            dve.wait_ge(lg_exp, 1)
            link(V_.tensor_scalar(lgs[:, 2, :], lgs[:, 1, :], 2.0, None, ALU.add))
            link(V_.reciprocal(lgs[:, 2, :], lgs[:, 2, :]))
            link(V_.tensor_tensor(lgs[:, 1, :], lgs[:, 1, :], lgs[:, 2, :], ALU.mult))
            link(V_.tensor_tensor(lgs[:, 2, :], lgs[:, 1, :], lgs[:, 1, :], ALU.mult))
            link(V_.tensor_scalar(lgs[:, 3, :], lgs[:, 2, :], 1 / 17, None, ALU.mult))
            for c in (15, 13, 11, 9, 7, 5, 3):
                link(V_.scalar_tensor_tensor(lgs[:, 3, :], lgs[:, 3, :], 1 / c, lgs[:, 2, :], ALU.add, ALU.mult))
            link(V_.scalar_tensor_tensor(lgs[:, 3, :], lgs[:, 3, :], 1.0, lgs[:, 1, :], ALU.add, ALU.mult))
            link(V_.tensor_scalar(lgs[:, 4, :], x, 0.0, None, ALU.min))
            link(V_.scalar_tensor_tensor(lg, lgs[:, 3, :], -2.0, lgs[:, 4, :], ALU.mult, ALU.add))
            for m in range(LT):
                for d in range(2):
                    ins = V_.tensor_scalar(wctx[:, m, d, :], lg[:, 8 * d:8 * d + 8], cst("mctx", 4)[:, 2 * m + d:2 * m + d + 1],
                                           None, ALU.mult)
            say(dve, ins, lg_ready, 1)

            def modulation(b):
                dve.wait_ge(ada_turned, b + 1)
                T = MB[b % 2][:, 0, 0:P].rearrange("p (c r) -> p c r", r=32)
                for r in range(2):
                    ins = V_.tensor_tensor(modT[:, r, 4 * b:4 * b + 4], T[:, :, r], vec[:, 4 * b:4 * b + 4], ALU.add)
                say(dve, ins, mod_part, b + 1)
                if b == 3:
                    say(dve, V_.tensor_scalar(modT[:, :, 8:16], modT[:, :, 8:16], 1.0, None, ALU.add), u_mod, 1)
                if b == 11:
                    say(dve, V_.tensor_scalar(modT[:, 0, 32:40], modT[:, 0, 32:40], 1.0, None, ALU.add), u_mod, 2)
            for b in range(12):
                j = J["ada", b, 0]
                job_wait(dve, j)
                if b >= 2:
                    dve.wait_ge(ada_turned, b - 1)
                evac(j, V_.tensor_copy(adaS[:, b % 2, :], PP[j["pair"]][:, 0, 0:P]))
                if b:
                    modulation(b - 1)
            modulation(11)
            dve.wait_ge(zeroed, 3)
            for b in range(4):
                j = J["glu", b, 0]
                dve.wait_ge(sig_ready, b + 1)
                for i in range(2):
                    ins = V_.scalar_tensor_tensor(zpad[:, 2 * b + i, HALO:HALO + L], PP[j["pair"]][:, i, :],
                                                  col("b_za", 2 * b + i), raw[:, 2 * (b % 2) + i, :], ALU.add, ALU.mult)
                evac(j, ins)

            def rope(r):
                dst = (kT, qT)[r // 2][:, 4 * (r % 2):4 * (r % 2) + 4, :]
                cos4, sin2 = (cst(n, L).unsqueeze(1).to_broadcast([P, k, L]) for n, k in (("cos", 4), ("sin", 2)))
                dve.wait_ge(raw_rot, r + 1)
                V_.tensor_tensor(Eqd[:, :, :], raw[:, :, :], cos4, ALU.mult)
                for q in range(2):
                    ins = V_.tensor_tensor(dst[:, 2 * q:2 * q + 2, :], MB[q][:, :, :], sin2, ALU.mult)
                link(ins)
                say(dve, V_.tensor_tensor(dst, dst, Eqd[:, :, :], ALU.add), rope_done, r + 1)

            def with_bias(j, n, dst):
                job_wait(dve, j)
                dve.wait_ge(bias_full[n % 2], 16 * (n // 2 + 1))
                evac(j, V_.tensor_tensor(dst, PPt[j["pair"]], biasr[:, n % 2, :].unsqueeze(1).to_broadcast([P, LT, 512]), ALU.add))

            def convolve(t):
                tap = [col("taps", t * TAPS + k) for k in range(TAPS)]
                link(V_.tensor_scalar(conv[:, t, :], zpad[:, t, 0:L], tap[0], col("conv_b", t), ALU.mult, ALU.add))
                for k in range(1, TAPS):
                    ins = V_.scalar_tensor_tensor(conv[:, t, :], zpad[:, t, k:k + L], tap[k], conv[:, t, :], ALU.mult, ALU.add)
                    if k < TAPS - 1 or t < DT - 1:
                        link(ins)
                    else:
                        say(dve, ins, conv_ready, 1)
            for b in range(2):
                with_bias(J["k", b, 1], b, Kct[:, :, b * 512:(b + 1) * 512])
                rope(b)
            for b in range(4):
                with_bias(J["v", b, 0], 2 + b, Vt[:, :, b * 512:(b + 1) * 512])
                convolve(2 * b)
                with_bias(J["v", b, 1], 2 + b, Vct[:, :, b * 512:(b + 1) * 512])
                convolve(2 * b + 1)
            rope(2)
            rope(3)
            k4 = kw[:, :, :].rearrange("p a n -> p (a n)").rearrange("p (a n) -> p a n", n=P)

            def prepare(h):
                q = 2 * (h % 2)
                f = Ddec[:, q:q + 2, :].rearrange("p a n -> p (a n)")
                link(V_.scalar_tensor_tensor(f, cst("dpos", 512), lg[:, h:h + 1], cst("ln2", 512), ALU.mult, ALU.add))
                say(dve, V_.scalar_tensor_tensor(f, cst("dneg", 512), lg[:, 8 + h:9 + h], f, ALU.mult, ALU.add), dec_arg, h + 1)
                dve.wait_ge(wctx_exp, 1)
                if h >= 2:
                    dve.wait_ge(s0_ps, h - 1)
                    dve.wait_ge(o_ps, h - 1)
                for d in range(2):
                    for m in range(LT):
                        V_.tensor_scalar(k4[:, 4 * (h % 2) + 2 * d + m, :], Kct[:, m, h * P:(h + 1) * P], wctx[:, m, d, h:h + 1],
                                         KSCALE, ALU.mult, ALU.mult)
                dve.wait_ge(dec_ready, h + 1)
                say(dve, V_.tensor_tensor(qd[:, q:q + 2, :], Eqd[:, q:q + 2, :], qT[:, h, :].unsqueeze(1).to_broadcast([P, 2, L]),
                                          ALU.mult), prep, h + 1)

            def stats(h):
                dve.wait_ge(o_kept, h + 1)
                for t in range(LT):
                    ins = V_.bn_stats(bst[:, t, :], On[:, t, h * DV:(h + 1) * DV])
                link(ins)
                for t in range(LT):
                    ins = V_.bn_aggr(mv[:, t, h, :], bst[:, t, :])
                say(dve, ins, o_stat, h + 1)
            prepare(0)
            for h in range(HEADS):
                if h + 1 < HEADS:
                    prepare(h + 1)
                dve.wait_ge(sc_ps, h + 1)
                q = 2 * (h % 2)
                say(dve, V_.scalar_tensor_tensor(Ph[:, q:q + 2, :], MB[1][:, :, :], KSCALE, Ddec[:, q:q + 2, :], ALU.mult,
                                                 ALU.mult), p_sb, h + 1)
                if h:
                    stats(h - 1)
            stats(HEADS - 1)
            say(dve, V_.tensor_scalar(rstd[:, :].rearrange("p (t h) -> p t h", t=LT), mv[:, :, :, 1], LN_EPS, None, ALU.add),
                var_ready, 1)
            dve.wait_ge(std_ready, 1)
            link(V_.reciprocal(rstd[:, :], rstd[:, :]))
            for t in range(LT):
                for h in range(HEADS):
                    o = On[:, t, h * DV:(h + 1) * DV]
                    ins = V_.tensor_scalar(o, o, mv[:, t, h, 0:1], rstd[:, t * HEADS + h:t * HEADS + h + 1], ALU.subtract, ALU.mult)
            link(ins)
            for b in range(4):
                with_bias(J["g", b, 0], 6 + b, raw2)
                dve.wait_ge(g_silu, b + 1)
                o = On[:, :, b * 512:(b + 1) * 512]
                say(dve, V_.tensor_tensor(o, o, raw2, ALU.mult), ret_ready, b + 1)

            def centre(name, src, dst):
                n = LNS[name]
                dve.wait_ge(ln_pe, n["pe"] + 1)
                say(dve, V_.tensor_tensor(dst[:, :, :], src[:, :, :], MB[0][:, 0:1, :].to_broadcast([P, DT, L]), ALU.subtract),
                    ln_dve, n["dve"] + 1)

            def scale(name, src, dst, eps):
                n = LNS[name]
                m = n["mean"]
                dve.wait_ge(ln_pe, n["pe"] + m + 1)
                say(dve, V_.tensor_scalar(rs[:, :], MB[1][:, 0, :], eps, None, ALU.add), ln_dve, n["dve"] + m + 1)
                dve.wait_ge(ln_act, n["act"] + 2)
                link(V_.reciprocal(rs[:, :], rs[:, :]))
                say(dve, V_.tensor_tensor(dst[:, :, :], src[:, :, :], rs[:, :].unsqueeze(1).to_broadcast([P, DT, L]), ALU.mult),
                    ln_dve, n["dve"] + m + 2)

            def ret(b):
                j = J["ret", b, 0]
                job_wait(dve, j)
                g3 = J["gates", 3, 0]
                dve.wait_ge(pair_free[g3["pair"]], g3["use"] + 1)
                evac(j, V_.tensor_tensor(mT[:, 2 * b:2 * b + 2, :], PP[j["pair"]][:, 0:2, :], gT[:, 2 * b:2 * b + 2, :], ALU.mult))
            centre("conv", conv, conv)
            ret(0)
            ret(1)
            scale("conv", conv, conv, LN_EPS)
            ret(2)
            ret(3)
            for b in range(2):
                j = J["cout", b, 0]
                job_wait(dve, j)
                for i in range(4):
                    ins = V_.scalar_tensor_tensor(raw[:, i, :], PP[j["pair"]][:, i, :], col("b_conv", 4 * b + i),
                                                  gT[:, 8 + 4 * b + i, :], ALU.add, ALU.mult)
                evac(j, ins)
                m4 = mT[:, 4 * b:4 * b + 4, :]
                say(dve, V_.tensor_tensor(m4, m4, raw[:, :, :], ALU.add), mix_in, b + 1)
            for b in range(2):
                j = J["mix", b, 0]
                job_wait(dve, j)
                for i in range(4):
                    ins = V_.tensor_scalar(raw[:, i, :], PP[j["pair"]][:, i, :], col("b_mix", 4 * b + i),
                                           modT[:, 0, 16 + 4 * b + i:17 + 4 * b + i], ALU.add, ALU.mult)
                evac(j, ins)
                h4 = hT[:, 4 * b:4 * b + 4, :]
                say(dve, V_.scalar_tensor_tensor(h4, h4, ALPHA, raw[:, :, :], ALU.mult, ALU.add), h_mid, b + 1)
            def first_of(out, val, top, n):
                eq, c = (r_(x).rearrange("p (t n) -> p t n", t=LT)[:, :, 0:n] for x in ("eq", "c"))
                link(V_.tensor_tensor(eq, val, top.unsqueeze(2).to_broadcast([P, LT, n]), ALU.is_equal))
                link(V_.scalar_tensor_tensor(c, eq, -64.0, cst("iota", n).unsqueeze(1).to_broadcast([P, LT, n]), ALU.mult, ALU.add))
                link(V_.tensor_reduce(r_("cm"), c, AX.X, ALU.min))
                link(V_.tensor_tensor(out, c, r_("cm").unsqueeze(2).to_broadcast([P, LT, n]), ALU.is_equal))

            def route(n):
                m, E = moe[n], EXPERTS[n]
                EG = E // GROUPS
                t2 = lambda x, w: r_(x)[:, 0:LT * w].rearrange("p (t n) -> p t n", t=LT)
                t4 = lambda x: r_(x)[:, 0:LT * E].rearrange("p (t g n) -> p t g n", t=LT, g=GROUPS)
                dve.wait_ge(m["logits"], 1)
                lt = t2("lt", GROUPS + E)
                link(V_.tensor_tensor(lt, MB[2][:, 0, 0:128].rearrange("p (t c) -> p t c", t=LT)[:, :, 0:GROUPS + E],
                                      rowc(f"rb{n}", GROUPS + E).unsqueeze(1).to_broadcast([P, LT, GROUPS + E]), ALU.add))
                link(V_.tensor_reduce(r_("gm"), lt[:, :, 0:GROUPS], AX.X, ALU.max))
                say(dve, V_.tensor_tensor(t2("gd", GROUPS), lt[:, :, 0:GROUPS], r_("gm").unsqueeze(2).to_broadcast([P, LT, GROUPS]),
                                          ALU.subtract), m["gexp_in"], 1)
                first_of(t2("hg", GROUPS), lt[:, :, 0:GROUPS], r_("gm"), GROUPS)
                hg = t2("hg", GROUPS).unsqueeze(3).to_broadcast([P, LT, GROUPS, EG])
                tmp = r_("tmp")[:, 0:LT * E].rearrange("p (t g n) -> p t g n", t=LT, g=GROUPS)
                le = lt[:, :, GROUPS:GROUPS + E].rearrange("p t (g n) -> p t g n", g=GROUPS)
                link(V_.tensor_tensor(tmp, le, hg, ALU.mult))
                ml = t2("ml", EG)
                link(V_.tensor_reduce(ml, tmp.rearrange("p t g n -> p t n g"), AX.X, ALU.add))
                link(V_.tensor_reduce(r_("m1"), ml, AX.X, ALU.max))
                first_of(t2("h1", EG), ml, r_("m1"), EG)
                link(V_.scalar_tensor_tensor(ml, t2("h1", EG), MASKED, ml, ALU.mult, ALU.add))
                link(V_.tensor_reduce(r_("m2"), ml, AX.X, ALU.max))
                say(dve, V_.tensor_tensor(r_("e2"), r_("m2"), r_("m1"), ALU.subtract), m["eexp_in"], 1)
                first_of(t2("h2", EG), ml, r_("m2"), EG)
                for A, h in (("A1", "h1"), ("A2", "h2")):
                    link(V_.tensor_tensor(t4(A), t2(h, EG).unsqueeze(2).to_broadcast([P, LT, GROUPS, EG]), hg, ALU.mult))
                say(dve, V_.tensor_tensor(r_("M")[:, 0:2 * E], r_("A1")[:, 0:2 * E], r_("A2")[:, 0:2 * E], ALU.add), m["hot_ready"], 1)
                dve.wait_ge(m["gexp_out"], 1)
                link(V_.tensor_reduce(r_("gw"), t2("gd", GROUPS), AX.X, ALU.add))
                dve.wait_ge(m["eexp_out"], 1)
                link(V_.scalar_tensor_tensor(r_("w1"), r_("e2"), 1.0, r_("gw"), ALU.add, ALU.mult))
                link(V_.reciprocal(r_("w1"), r_("w1")))
                link(V_.tensor_tensor(r_("w2"), r_("w1"), r_("e2"), ALU.mult))
                Sa, Sb = (r_(x).rearrange("p (t n) -> p t n", t=2) for x in ("Sa", "Sb"))
                V_.memset(r_("Sa"), 0.0)
                link(V_.memset(r_("Sb"), 0.0))
                dve.wait_ge(m["ranks"], 1)
                cnt, items = Sa[:, 0, 16:16 + E], Sa[:, 1, 16:16 + E]
                link(V_.tensor_scalar(cnt, MB[3][:, 0, 2 * E:3 * E], float(D), None, ALU.mult))
                link(V_.tensor_scalar(r_("rank")[:, 0:2 * E], MB[3][:, 0, 0:2 * E], float(D), None, ALU.mult))
                link(V_.tensor_scalar(items, cnt, float(SLOTS), 1.0, ALU.is_gt, ALU.add))
                for c in (2, 3):
                    link(V_.scalar_tensor_tensor(items, cnt, float(c * SLOTS), items, ALU.is_gt, ALU.add))
                A, B, step = Sa, Sb, 1
                while step < E:
                    link(V_.tensor_tensor(B[:, :, 16:16 + E], A[:, :, 16:16 + E], A[:, :, 16 - step:16 + E - step], ALU.add))
                    A, B, step = B, A, 2 * step
                start, first, total = A[:, 0, 15:15 + E], A[:, 1, 15:15 + E], A[:, 1, 15 + E:16 + E]
                link(V_.scalar_tensor_tensor(r_("q")[:, 0:E], first, -float(SLOTS), start, ALU.mult, ALU.add))
                link(V_.tensor_tensor(r_("tmp")[:, 1:E], r_("q")[:, 1:E], r_("q")[:, 0:E - 1], ALU.subtract))
                link(V_.tensor_scalar(r_("vx")[:, 0:E], first, cst("pcol", 1), None, ALU.is_le))
                link(V_.tensor_reduce(r_("item")[:, 0:1], r_("vx")[:, 0:E], AX.X, ALU.add))
                link(V_.tensor_tensor(r_("tmp")[:, 1:E], r_("tmp")[:, 1:E], r_("vx")[:, 1:E], ALU.mult))
                link(V_.tensor_reduce(r_("item")[:, 1:2], r_("tmp")[:, 1:E], AX.X, ALU.add))
                link(V_.tensor_scalar(r_("item")[:, 0:1], r_("item")[:, 0:1], -1.0, None, ALU.add))
                say(dve, V_.scalar_tensor_tensor(r_("item")[:, 1:2], cst("pcol", 1), float(SLOTS), r_("item")[:, 1:2], ALU.mult,
                                                 ALU.add), m["items_in"], 1)
                vx, rank, rank2 = t2("vx", E), t2("rank", E), t2("rank2", E)
                over = lambda x: x.unsqueeze(1).to_broadcast([P, LT, E])
                link(V_.tensor_tensor(vx, rank, over(start), ALU.add))
                link(V_.tensor_scalar(rank2, rank, float(SLOTS), None, ALU.is_ge))
                for c in (2, 3):
                    link(V_.scalar_tensor_tensor(rank2, rank, float(c * SLOTS), rank2, ALU.is_ge, ALU.add))
                link(V_.scalar_tensor_tensor(rank2, rank2, float(SLOTS), rank, ALU.mult, ALU.add))
                link(V_.scalar_tensor_tensor(rank2, over(first), 2.0 * SLOTS, rank2, ALU.mult, ALU.add))
                pos = r_("pos")
                for k, A_ in enumerate(("A1", "A2")):
                    for v, to in ((vx, pos[:, 2 * k:2 * k + 2]),
                                  (rank2, pos[:, 4 + 4 * k:8 + 4 * k].rearrange("p (t h) -> p t h", h=2)[:, :, 0])):
                        link(V_.tensor_tensor(t2("tmp", E), t2(A_, E), v, ALU.mult))
                        link(V_.tensor_reduce(to, t2("tmp", E), AX.X, ALU.add))
                ev = pos[:, 4:12].rearrange("p (t h) -> p t h", h=2)
                link(V_.tensor_scalar(ev[:, :, 1], ev[:, :, 0], float(SLOTS), None, ALU.add))
                say(dve, V_.tensor_copy(idx[:, 0:12], pos), m["idx_ready"], 1)
                dve.wait_ge(m["items_ps"], 1)
                V_.tensor_copy(tab[0:1, 128:129], total[0:1])
                say(dve, V_.tensor_copy(tab[0:1, 0:128].rearrange("p (q n) -> p q n", q=2),
                                        MB[3][0:1, 1, :].rearrange("p (q n) -> p q n", q=2)[:, :, 0:64]), m["items_ready"], 1)
                dve.sem_inc(m["hid_ready"], 1)
                dve.sem_inc(m["y_kept"], 1)
                T = dve.value_load(tab[0:1, 128:129], min_val=E, max_val=E + 8)
                with dve.Fori(0, T) as i:
                    dve.wait_ge(m["sg_ready"], i + 1)
                    dve.wait_ge(m["up_done"], i + 1)
                    V_.tensor_tensor(hid, PP[0][:, 2, :], sg, ALU.mult).then_inc(m["hid_ready"], 1)
                    dve.wait_ge(m["down_done"], i + 1)
                    dve.wait_ge(m["ys_free"], i + 1)
                    V_.tensor_copy(ys, PP[1][:, 0:2, :].rearrange("p a n -> p (a n)")).then_inc(m["y_kept"], 1)
                dve.wait_ge(m["yg_full"], 128)
                for t in range(LT):
                    link(V_.tensor_scalar(yg[:, t, :], yg[:, t, :], r_("w1")[:, t:t + 1], None, ALU.mult))
                    ins = V_.scalar_tensor_tensor(yg[:, t, :], yg[:, 2 + t, :], r_("w2")[:, t:t + 1], yg[:, t, :], ALU.mult, ALU.add)
                say(dve, ins, m["y_sum"], 1)
                if n == 0:
                    link(V_.tensor_scalar(hT[:, :, :], hT[:, :, :], ALPHA, None, ALU.mult))
                dve.wait_ge(m["y_turned"], 1)
                for k in range(DT):
                    if n == 0:
                        ins = V_.scalar_tensor_tensor(hT[:, k, :], MB[k // 2][:, k % 2, :], modT[:, 0, 40 + k:41 + k], hT[:, k, :],
                                                      ALU.mult, ALU.add)
                    else:
                        ins = V_.tensor_tensor(hT[:, k, :], MB[k // 2][:, k % 2, :], hT[:, k, :], ALU.add)
                say(dve, ins, h_ready, 1 + 2 * n)
            centre("ln1", hT, hT)
            scale("ln1", hT, hT, LN_EPS)
            route(0)
            centre("ln2", hT, hT)
            scale("ln2", hT, hT, LN_EPS)
            scale("attn", hT, uT, RMS_EPS)
            dve.wait_ge(b2["relb_ps"], 1)
            dve.wait_ge(b2["ld"], 16 * 12)
            say(dve, V_.tensor_tensor(relb, flat(MB[2])[0:QH, 0:384], outside, ALU.add), b2["relb_sb"], 1)
            say(dve, V_.tensor_tensor(ws, ws, cst("causal", P).unsqueeze(1).to_broadcast([P, 8, P]), ALU.mult), b2["ws_ready"], 1)
            j = J["v2", 0, 0]
            dve.wait_ge(pair_free[j["pair"]], j["use"] + 1)
            for t in range(LT):
                ins = V_.bn_stats(bst[:, t, :], raw2[:, t, :])
            link(ins)
            for t in range(LT):
                ins = V_.bn_aggr(mv[:, t, 0, :], bst[:, t, :])
            link(ins)
            dve.wait_ge(ln_act, LNS["attn"]["end"])
            say(dve, V_.tensor_scalar(rs[:, 0:2], mv[:, :, 0, 1], RMS_EPS, None, ALU.add), b2["vvar"], 1)
            dve.wait_ge(b2["vstd"], 1)
            link(V_.reciprocal(rs[:, 0:2], rs[:, 0:2]))
            for t in range(LT):
                ins = V_.tensor_scalar(raw2[:, t, :], raw2[:, t, :], mv[:, t, 0, 0:1], rs[:, t:t + 1], ALU.subtract, ALU.mult)
            link(ins)
            say(dve, V_.tensor_tensor(raw2, raw2, rowc("gm_g", 512).unsqueeze(1).to_broadcast([P, LT, 512]), ALU.mult),
                b2["v_ready"], 1)
            dve.wait_ge(b2["sp_ps"], 1)
            for q in range(2):
                bias = flat(Ph)[:, 0:512].rearrange("p (a t) -> p a t", a=4)[:, 2 * q:2 * q + 2, :]
                ins = V_.tensor_tensor(aT[:, 2 * q:2 * q + 2, :].rearrange("p a (c t) -> p a c t", c=2),
                                       MB[q][:, :, :].rearrange("p a (c t) -> p a c t", c=2),
                                       bias.unsqueeze(2).to_broadcast([P, 2, LT, P]), ALU.add)
            link(ins)
            say(dve, V_.tensor_tensor(aT, aT, gu, ALU.mult), b2["a_ready"], 1)
            dve.wait_ge(b2["relb_full"], 16 * QH)
            for qb in range(2):
                dve.wait_ge(b2["sc_ps"], qb + 1)
                if qb:
                    dve.wait_ge(b2["p_turned"], 1)
                w0, per = (0, 2) if qb else (P, 4)
                sc = Kc[:, :, w0:L]
                for q in range(QH // per):
                    h = slice(q * per, (q + 1) * per)
                    ins = V_.tensor_tensor(Kc[:, h, w0:L], flat(MB[q]).rearrange("p (a n) -> p a n", a=per),
                                           RA[:, DT + q * per:DT + (q + 1) * per, w0:L], ALU.add)
                link(ins)
                link(V_.tensor_reduce(r_("mx"), sc, AX.X, ALU.max))
                link(V_.tensor_tensor(r_("mx"), r_("mx"), rowc("sinks", QH), ALU.max))
                V_.tensor_tensor(r_("sk"), rowc("sinks", QH), r_("mx"), ALU.subtract)
                say(dve, V_.tensor_tensor(sc, sc, r_("mx").unsqueeze(2).to_broadcast([P, QH, L - w0]), ALU.subtract),
                    b2["sc_sb"], qb + 1)
                dve.wait_ge(b2["p_exp"], qb + 1)
                link(V_.tensor_reduce(r_("den"), sc, AX.X, ALU.add))
                link(V_.tensor_tensor(r_("den"), r_("den"), r_("sk"), ALU.add))
                link(V_.reciprocal(r_("den"), r_("den")))
                say(dve, V_.tensor_tensor(sc, sc, r_("den").unsqueeze(2).to_broadcast([P, QH, L - w0]), ALU.mult),
                    b2["p_ready"], qb + 1)
                dve.wait_ge(b2["b_ps"], qb + 1)
                say(dve, V_.tensor_copy(bT[:, :, qb * P:(qb + 1) * P], flat(MB[0]).rearrange("p (a n) -> p a n", a=4)),
                    b2["b_ready"], qb + 1)
            g3 = J["gates2", 3, 0]
            dve.wait_ge(pair_free[g3["pair"]], g3["use"] + 1)
            for half in range(2):
                j = J["pa", 0, half]
                job_wait(dve, j)
                evac(j, V_.tensor_tensor(mT[:, 4 * half:4 * half + 4, :], PP[j["pair"]][:, :, :],
                                         gT[:, 4 * half:4 * half + 4, :], ALU.mult))
            for half in range(2):
                j = J["pb", 0, half]
                job_wait(dve, j)
                evac(j, V_.tensor_tensor(raw[:, :, :], PP[j["pair"]][:, :, :], gT[:, 8 + 4 * half:12 + 4 * half, :], ALU.mult))
                m4 = mT[:, 4 * half:4 * half + 4, :]
                say(dve, V_.tensor_tensor(m4, m4, raw[:, :, :], ALU.add), b2["m_ready"], half + 1)
            for b in range(2):
                j = J["out2", b, 0]
                job_wait(dve, j)
                h4 = hT[:, 4 * b:4 * b + 4, :]
                evac(j, V_.tensor_tensor(h4, PP[j["pair"]][:, :, :], h4, ALU.add))
            dve.sem_inc(h_ready, 1)
            scale("ffn", hT, uT, RMS_EPS)
            route(1)
            scale("final", hT, uT, RMS_EPS)


def blocks(w, width=512):
    K, N = w.shape
    return np.ascontiguousarray(w.reshape(K // P, P, N // width, width).transpose(2, 1, 0, 3)).reshape(N // width, P, -1)


def tiles(x):
    n = x.shape[-1] // P
    return np.ascontiguousarray(np.moveaxis(x.reshape(-1, n, P), (0, 1, 2), (2, 1, 0)))


def bucket(dist):
    large = 16 + (np.log(np.maximum(dist, 1).astype(np.float32) / np.float32(16)) / np.float32(np.log(8.0)) * np.float32(16)).astype(np.int32)
    return np.where(dist < 16, dist, np.minimum(large, 31))


def constants():
    f = np.float32
    c = np.zeros((P, NC), f)

    def put(name, value):
        value = np.asarray(value, f).reshape(P, -1)
        c[:, CCOLS[name]:CCOLS[name] + value.shape[1]] = value
    p = np.arange(P)
    put("ident", np.eye(P))
    put("ones", np.full((P, P), 1.0 / D))
    rot = np.zeros((P, P))
    rot[p[64:], p[:64]] = -1.0
    rot[p[:64], p[64:]] = 1.0
    put("rot", rot)
    pos = np.arange(L)
    inv = (f(10000.0) ** (-np.arange(32, dtype=f) / f(32))).astype(f)
    ang = np.concatenate([(pos // 64).astype(f)[:, None] * inv, (pos % 64).astype(f)[:, None] * inv], axis=1).astype(f)
    ang = np.concatenate([ang, ang], axis=1)
    put("cos", np.cos(ang).T)
    put("sin", np.sin(ang).T)
    m = p[:, None, None] + P * np.arange(LT)[None, :, None]
    n = pos[None, None, :]
    put("dpos", np.maximum(n - m, 0))
    put("dneg", np.maximum(m - n, 0))
    put("ln2", (m == n) * np.log(2.0))
    put("nfb", np.broadcast_to(np.concatenate([pos + 1, L - pos]), (P, 2 * L)))
    put("mctx", np.stack([L - 1 - m[:, :, 0], m[:, :, 0]], axis=2))
    put("causal", p[:, None] <= p[None, :])
    put("iota", np.broadcast_to(np.arange(32) + 64, (P, 32)))
    put("tri", (p[:, None] < p[None, :]) / D)
    put("pcol", p)
    return c


def layout(i):
    i = {k: np.asarray(v) for k, v in i.items()}
    d = {}
    w_in, b_in = i["w_in"][0], i["b_in"][0]
    cut = np.cumsum([0, 1024, 1024, 2048, 2048, 1024, 1024, 2048])
    q, k, v, g, za, zb, gates = (slice(cut[n], cut[n + 1]) for n in range(7))
    d["w_ada"] = blocks(i["w_ada"][0])
    d["w_q"], d["w_k"], d["w_v"], d["w_g"], d["w_gates"] = (blocks(w_in[:, s]) for s in (q, k, v, g, gates))
    d["w_glu"] = blocks(np.stack([w_in[:, za].reshape(D, 4, 256), w_in[:, zb].reshape(D, 4, 256)], axis=2).reshape(D, 2 * D))
    d["w_ret"] = blocks(i["w_ret_out"][0], 256)
    d["w_cout"], d["w_mix"] = blocks(i["w_conv_out"][0]), blocks(i["w_mix_out"][0])
    vecs = [i["b_ada"][0], b_in[q], b_in[k], b_in[za], b_in[zb], b_in[gates], i["conv_dw_b"][0], i["conv_ln_g"][0],
            i["conv_ln_b"][0], i["b_conv_out"][0], i["b_mix_out"][0], i["ln1_g"][0], i["ln1_b"][0], i["ln2_g"][0],
            i["ln2_b"][0], i["attn_norm_g_2"][0], i["ffn_norm_g_2"][0], i["final_norm_g_2"]]
    taps = i["conv_dw"][0].reshape(TAPS, DT, P).transpose(2, 1, 0).reshape(P, -1)
    d["vec"] = np.concatenate([tiles(x)[:, :, 0] for x in vecs] + [taps], axis=1)
    d["rows"] = np.concatenate([i["ret_decay_fwd"][0], i["ret_decay_bwd"][0], i["b_router_grp"][0], i["b_router_exp"][0],
                                i["router_group_b_2"][0], i["router_expert_b_2"][0].ravel(), i["attn_sinks_2"][0],
                                i["gm_v_norm_g_2"][0]])[None]
    d["bias_rows"] = np.concatenate([b_in[k], b_in[v], b_in[g]])[None]
    d["wr0"] = np.concatenate([i["w_router_grp"][0], i["w_router_exp"][0]], axis=1).reshape(DT, P, 36).transpose(1, 0, 2)
    d["wr1"] = np.concatenate([i["router_group_w_2"][0], i["router_expert_w_2"][0].transpose(1, 0, 2).reshape(D, 16)],
                              axis=1).reshape(DT, P, 20).transpose(1, 0, 2)
    d["xT"], d["ctxT"] = tiles(i["x"][0]), tiles(i["ctx"][0])
    d["cT"] = np.concatenate([tiles(i["c"]), tiles(i["c_ctx"][None])], axis=2)
    for n, (x, y, z) in enumerate((("w_exp_gate", "w_exp_up", "w_exp_down"), ("expert_w_gate_2", "expert_w_up_2", "expert_w_down_2"))):
        E = EXPERTS[n]
        s = np.empty((E, 3, P, BLK), np.float32)
        s[:, 0] = i[x][0].reshape(E, DT, P, 512).transpose(0, 2, 1, 3).reshape(E, P, BLK)
        s[:, 1] = i[y][0].reshape(E, DT, P, 512).transpose(0, 2, 1, 3).reshape(E, P, BLK)
        s[:, 2] = i[z][0].reshape(E, 4, P, D).transpose(0, 2, 1, 3).reshape(E, P, BLK)
        d[f"w_moe{n}"] = s.reshape(3 * E, P, BLK)
    w2 = i["w_in_2"][0]
    d["w_u2"], d["w_v2"] = blocks(w2[:, 0:512]), blocks(w2[:, 512:1024])
    d["w_q2"] = blocks(w2[:, 1024:1536].reshape(D, 2, 4, HD).transpose(0, 2, 1, 3).reshape(D, 512))
    d["w_kv2"] = blocks(w2[:, 1536:1792], 256)
    d["w_gates2"] = blocks(w2[:, 1792:3840])
    d["w_pa"], d["w_pb"] = blocks(i["w_proj_a_2"][0], 1024), blocks(i["w_proj_b_2"][0], 1024)
    d["w_out2"] = blocks(i["w_out_2"][0])
    d["ws"] = i["gm_w_spatial_2"][0].transpose(2, 0, 1)
    d["gm_b"] = i["gm_b_spatial_2"][0].reshape(1, -1)
    d["const"] = constants()
    dist = 255 - np.arange(384)
    ok = (dist >= 0) & (dist < P)
    hot = np.zeros((32, 384), np.float32)
    hot[bucket(dist[ok]), np.arange(384)[ok]] = 1.0
    d["hot"] = hot
    d["outside"] = np.broadcast_to(np.where(ok, 0.0, MASKED).astype(np.float32), (QH, 384))
    d["rel"] = i["rel_bias_2"]
    return {k: np.ascontiguousarray(v) for k, v in d.items()}


def kernel(**inputs):
    import concourse.bacc as bacc
    from concourse.bass_utils import run_bass_kernel_spmd

    nc = bacc.Bacc("TRN2", target_bir_lowering=False, num_devices=1)
    arrays = layout(inputs)
    a = {n: nc.dram_tensor(f"in_{n}", x.shape, mybir.dt.from_np(x.dtype), kind="ExternalInput").ap() for n, x in arrays.items()}
    a["out"] = nc.dram_tensor("out", (P, DT, L), F32, kind="ExternalOutput").ap()
    build(nc, a)
    r = run_bass_kernel_spmd(nc, [{f"in_{n}": x for n, x in arrays.items()}], core_ids=[0])
    out = r.results[0]["out"]
    return np.ascontiguousarray(out.transpose(2, 1, 0)).reshape(1, L, D)
```

```python
from contextlib import ExitStack

import numpy as np

import concourse.bass as bass
from concourse import mybir

F32 = mybir.dt.float32
ALU = mybir.AluOpType
ACT = mybir.ActivationFunctionType
AX = mybir.AxisListType

P = 128
D = 1024
L = 256
DT = D // P
LT = L // P
HEADS, DV = 8, 256
TAPS = 31
HALO = TAPS // 2
RING = 3
BLK = 4096
LN_EPS, RMS_EPS = 1e-5, 1e-6
KSCALE = 128 ** -0.5
ALPHA = 2.0 ** 0.25
GROUPS = 4
EXPERTS = (32, 16)
SLOTS = 64
QH, HD = 8, 64
MASKED = -1e30


def columns(*parts):
    at, out = 0, {}
    for name, n in parts:
        out[name] = at
        at += n
    return out, at


VCOLS, NV = columns(("b_ada", 48), ("b_q", 8), ("b_k", 8), ("b_za", 8), ("b_zb", 8), ("b_gates", 16),
                    ("conv_b", 8), ("conv_g", 8), ("conv_lb", 8), ("b_conv", 8), ("b_mix", 8), ("ln1_g", 8),
                    ("ln1_b", 8), ("ln2_g", 8), ("ln2_b", 8), ("attn_g", 8), ("ffn_g", 8), ("final_g", 8),
                    ("taps", 8 * TAPS))
RCOLS, NR = columns(("decay", 16), ("rb0", 36), ("rb1", 20), ("sinks", 8), ("gm_g", 512))
CCOLS, NC = columns(("ident", 128), ("ones", 128), ("rot", 128), ("cos", 256), ("sin", 256), ("dpos", 512),
                    ("dneg", 512), ("ln2", 512), ("nfb", 512), ("mctx", 4), ("causal", 128), ("iota", 16), ("tri", 128), ("pcol", 1),
                    ("slot", 65))


def make_jobs():
    jobs, srcs = [], []
    for src, n, kinds in (("ada", 12, ["ada"]), ("glu", 4, ["cm8"]), ("k", 2, ["cm8", "tm8c"]),
                          ("v", 4, ["tm8", "tm8c"]), ("q", 2, ["cm8"]), ("g", 4, ["tm8"]), ("gates", 4, ["cm8"]),
                          ("ret", 4, ["cm16"]), ("cout", 2, ["cm8"]), ("mix", 2, ["cm8"]),
                          ("u2", 1, ["cm8"]), ("v2", 1, ["tm8"]), ("q2", 1, ["cm8"]), ("kv2", 1, ["kv"]),
                          ("gates2", 4, ["cm8"]), ("pa", 1, ["cm4", "cm4"]), ("pb", 1, ["cm4", "cm4"]),
                          ("out2", 2, ["cm8"])):
        for b in range(n):
            for half, kind in enumerate(kinds):
                i = len(jobs)
                jobs.append(dict(src=src, b=b, kind=kind, half=half, w=len(srcs), i=i, pair=i % 2, use=i // 2))
            srcs.append((src, b))
    last_of = {j["w"]: j["i"] for j in jobs}
    return jobs, {(j["src"], j["b"], j["half"]): j for j in jobs}, srcs, last_of


def build(nc, a):
    jobs, J, srcs, last_of = make_jobs()
    moe_w = [srcs.index(("u2", 0)), len(srcs)]
    with ExitStack() as ctx:
        def sb(name, shape):
            return ctx.enter_context(nc.sbuf_tensor(name, shape, F32))

        def sem(name):
            return ctx.enter_context(nc.semaphore(name))

        ring = sb("ring", [P, RING, BLK])
        const = sb("const", [P, NC])
        vec = sb("vec", [P, NV])
        row = sb("row", [P, NR])
        wr = [sb("wr0", [P, DT, 36]), sb("wr1", [P, DT, 20])]
        hT = sb("hT", [P, DT, L])
        uT = sb("uT", [P, DT, L])
        RA = sb("RA", [P, 2 * DT, L])
        kT = sb("kT", [P, DT, L])
        qT = sb("qT", [P, DT, L])
        Kc = sb("Kc", [P, DT, L])
        Vc = sb("Vc", [P, 2 * DT, L])
        V = sb("V", [P, 2 * DT, L])
        biasr = sb("biasr", [P, 2, 512])
        zpad = sb("zpad", [P, DT, L + 2 * HALO])
        conv = sb("conv", [P, DT, L])
        raw = sb("raw", [P, 4, L])
        Eqd = sb("Eqd", [P, 4, L])
        qd = sb("qd", [P, 4, L])
        Ddec = sb("Ddec", [P, 4, L])
        kw = sb("kw", [P, 4, L])
        S0s = sb("S0s", [P, 4, L])
        Ph = sb("Ph", [P, 4, L])
        adaS = sb("adaS", [P, 2, P])
        modT = sb("modT", [P, 2, 48])
        sT = sb("sT", [P, DT, 32])
        cin = sb("cin", [P, DT, 2])
        lgs = sb("lgs", [P, 6, 16])
        wctx = sb("wctx", [P, LT, 2, 8])
        mv = sb("mv", [P, LT, HEADS, 2])
        rstd = sb("rstd", [P, LT * HEADS])
        bst = sb("bst", [P, LT, 6])
        rs = sb("rs", [P, L])
        rt = biasr[:, :, :].rearrange("p a n -> p (a n)")

        def flat(t):
            return t[:, :, :].rearrange("p a n -> p (a n)")
        xg = flat(raw)[:, 0:512]
        xts = flat(qd)[:, 0:512].rearrange("p (c m) -> p c m", c=4)
        hid, sg = qd[:, 2, :], Eqd[:, 0, :]
        hts = qd[:, 3, :].rearrange("p (c m) -> p c m", c=2)
        mw = flat(V)
        ys, S = mw[:, 0:512], mw[:, 512:768]
        Sk = mw[:, 768:1280].rearrange("p (k n) -> p k n", k=2)
        placer = mw[:, 1280:1792].rearrange("p (k n) -> p k n", k=2)
        weightr = mw[:, 1792:2304].rearrange("p (k n) -> p k n", k=2)
        diag = mw[:, 2304:3328].rearrange("p (v q n) -> p v q n", v=2, q=4)
        Ek = mw[:, 3328:3584].rearrange("p (q n) -> p q n", q=4)
        G = mw[:, 3584:3712].rearrange("p (t n) -> p t n", t=LT)
        slotno = mw[:, 3712:3777]
        hot, rel = flat(Vc)[0:32, 0:384], flat(Vc)[0:32, 512:512 + QH]
        outside, relb = flat(Vc)[0:QH, 1024:1408], flat(Vc)[0:QH, 1536:1920]
        pT = flat(zpad)
        gu, aT, bT = conv[:, 0:4, :], conv[:, 4:8, :], Eqd
        q2, k2, v2 = RA[:, 0:4, :], RA[:, 4, :], RA[:, 5, :]
        ws = flat(S0s).rearrange("p (g t) -> p g t", g=8)
        tab = adaS[:, :, :].rearrange("p a n -> p (a n)").bitcast(mybir.dt.int32)
        ctxT, ucT = RA[:, 0:DT], RA[:, DT:2 * DT]
        Kct = flat(Kc).rearrange("p (a n) -> p a n", a=LT)
        Vct = flat(Vc).rearrange("p (a n) -> p a n", a=LT)
        Vt = flat(V).rearrange("p (a n) -> p a n", a=LT)
        On = flat(RA).rearrange("p (a n) -> p a n", a=LT)
        retT, gT, mT, SQ = Vc, V, kT, qT
        raw2 = flat(raw).rearrange("p (a n) -> p a n", a=LT)
        PP = [ctx.enter_context(nc.psum_tensor(f"PP{i}", [P, 4, L], F32)) for i in range(2)]
        MB = [ctx.enter_context(nc.psum_tensor(f"MB{i}", [P, 2, L], F32)) for i in range(4)]
        bank = [flat(PP[i // 2])[:, 512 * (i % 2):512 * (i % 2 + 1)] for i in range(4)]
        PPt = [p[:, :, :].rearrange("p a n -> p (a n)").rearrange("p (a n) -> p a n", a=LT) for p in PP]

        relb_d = nc.dram_tensor("relb_d", [QH, P, 384], F32, kind="Internal")

        RT, _ = columns(("lt", 72), ("gd", 8), ("e2", 2), ("gm", 2), ("gw", 2), ("cm", 2), ("eq", 16), ("c", 16), ("hg", 8),
                        ("ml", 16), ("m1", 2), ("m2", 2), ("h1", 16), ("h2", 16), ("w1", 2), ("w2", 2), ("tmp", 64),
                        ("A1", 64), ("A2", 64), ("M", 64), ("rank", 64), ("Sa", 96), ("Sb", 96),
                        ("vx", 64), ("item", 1), ("pos", 4), ("mx", 8), ("sk", 8), ("den", 8))
        assert _ <= 1024
        widths = dict(zip(list(RT), [b - c for c, b in zip(list(RT.values()), list(RT.values())[1:] + [_])]))

        def r_(name):
            return rt[:, RT[name]:RT[name] + widths[name]]

        def cst(name, n):
            return const[:, CCOLS[name]:CCOLS[name] + n]

        def col(name, t):
            return vec[:, VCOLS[name] + t:VCOLS[name] + t + 1]

        def rowc(name, n):
            return row[:, RCOLS[name]:RCOLS[name] + n]
        ident, ones, rotm = cst("ident", P), cst("ones", P), cst("rot", P)
        lg = lgs[:, 5, :]

        ld_c, ld_small, ld_x = sem("ld_c"), sem("ld_small"), sem("ld_x")
        w_full = [sem(f"w_full{i}") for i in range(RING)]
        job_done = sem("job_done")
        pair_free = [sem("pair_free0"), sem("pair_free1")]
        dve_own, act_own = sem("dve_own"), sem("act_own")
        zeroed, silu_c, ada_turned, mod_part, u_mod, u_ready = (sem(n) for n in (
            "zeroed", "silu_c", "ada_turned", "mod_part", "u_mod", "u_ready"))
        lg_abs, lg_exp, lg_ready, wctx_exp = (sem(n) for n in ("lg_abs", "lg_exp", "lg_ready", "wctx_exp"))
        sig_ready, raw_rot, rope_done = sem("sig_ready"), sem("raw_rot"), sem("rope_done")
        bias_full = [sem("bias_full0"), sem("bias_full1")]
        dec_arg, dec_ready, prep, s0_ps, sc_ps, s0_sb, p_sb, o_ps, o_kept, o_stat = (sem(n) for n in (
            "dec_arg", "dec_ready", "head_prep", "s0_ps", "sc_ps", "s0_sb", "p_sb", "o_ps", "o_kept", "o_stat"))
        var_ready, std_ready, g_silu, ret_ready, ret_turned, ret_kept = (sem(n) for n in (
            "var_ready", "std_ready", "g_silu", "ret_ready", "ret_turned", "ret_kept"))
        conv_ready, mix_in, h_mid, h_ready = sem("conv_ready"), sem("mix_in"), sem("h_mid"), sem("h_ready")
        ln_pe, ln_dve, ln_act = sem("ln_pe"), sem("ln_dve"), sem("ln_act")
        out_done = sem("out_done")
        moe = []
        for n in range(2):
            moe.append({k: sem(f"{k}{n}") for k in (
                "uf_ready", "logits", "gexp_in", "eexp_in", "gexp_out", "eexp_out", "hot_ready", "ranks", "items_in",
                "items_ps", "items_ready", "u_turned", "u_rows", "diag_ready", "bc_ps", "bc_kept", "wg_full", "wu_full",
                "wd_full", "g_ready", "gathered", "xg_kept", "xt_ps", "xts_ready", "gate_done", "up_done", "down_done",
                "sg_ready", "hid_ready", "ht_ps", "ht_ready", "y_kept", "s_ready", "scattered", "acc_done", "step")})
        b2 = {k: sem(f"b2_{k}") for k in ("ld", "relb_ps", "relb_sb", "relb_dram", "relb_full", "gelu_u", "gelu_v", "vvar",
                                          "vstd", "v_ready", "qk_ready", "v2_ready", "ws_ready", "sp_ps", "a_ready",
                                          "sc_ps", "sc_sb", "p_exp", "p_ready", "p_turned", "p_kept", "b_ps", "b_ready",
                                          "m_ready")}

        LNS, tot = {}, [0, 0, 0]
        for name, mean in (("conv", 1), ("ln1", 1), ("ln2", 1), ("attn", 0), ("ffn", 0), ("final", 0)):
            LNS[name] = dict(mean=mean, pe=tot[0], dve=tot[1], act=tot[2])
            tot = [tot[0] + 1 + mean, tot[1] + 2 + mean, tot[2] + 3]
            LNS[name]["end"] = tot[2]

        def w_wait(eng, w):
            eng.wait_ge(w_full[w % RING], 16 * (w // RING + 1))

        def job_wait(eng, j):
            eng.wait_ge(job_done, j["i"] + 1)

        class Own:

            def __init__(self, eng, sem_):
                self.eng, self.sem, self.n = eng, sem_, 0

            def link(self, ins):
                self.n += 1
                ins.then_inc(self.sem, 1)
                self.eng.wait_ge(self.sem, self.n)

        def say(eng, ins, sem_, value):
            ins.then_inc(sem_, 1)
            eng.wait_ge(sem_, value)

        block = ctx.enter_context(nc.Block())

        @block.sync
        def _(sp):
            def load(w):
                src, b = srcs[w]
                if w >= RING and not moe_w[0] <= w < moe_w[0] + RING:
                    sp.wait_ge(job_done, last_of[w - RING] + 1)
                s = a["w_" + src]
                sp.dma_start(ring[:, w % RING, 0:s.shape[2]], s[b]).then_inc(w_full[w % RING], 16)

            def experts(n):
                m, s = moe[n], a[f"w_moe{n}"]
                part = (("wg_full", "gate_done"), ("wu_full", "up_done"), ("wd_full", "down_done"))
                for q in range(3):
                    sp.wait_ge(job_done, last_of[max(w for w in range(moe_w[n]) if w % RING == q)] + 1)
                    sp.dma_start(ring[:, q, :], s[q]).then_inc(m[part[q][0]], 16)
                sp.wait_ge(m["items_ready"], 1)
                T = sp.value_load(tab[0:1, 64:65], min_val=EXPERTS[n], max_val=EXPERTS[n] + 8)
                with sp.Fori(1, T) as i:
                    e = sp.value_load(tab[0:1, bass.ds(i, 1)], min_val=0, max_val=EXPERTS[n] - 1)
                    for q in range(3):
                        sp.wait_ge(m[part[q][1]], i)
                        sp.dma_start(ring[:, q, :], s[bass.ds(3 * e + q, 1)].rearrange("a p n -> p (a n)")
                                     ).then_inc(m[part[q][0]], 16)
                return [(m[x[1]], T) for x in part]

            for w in range(moe_w[0]):
                load(w)
            used = experts(0)
            for w in range(moe_w[0], moe_w[1]):
                if w < moe_w[0] + RING:
                    sp.wait_ge(*used[w % RING])
                load(w)
            experts(1)
            sp.wait_ge(ln_act, LNS["final"]["end"])
            sp.dma_start(a["out"], uT[:, :, :]).then_inc(out_done, 16)
            sp.wait_ge(out_done, 16)
        @block.gpsimd
        def _(pool):
            nc.gpsimd.memset(sT[:, :, :], 0.0).then_inc(zeroed, 1)
            nc.gpsimd.memset(zpad[:, :, 0:HALO], 0.0).then_inc(zeroed, 1)
            nc.gpsimd.memset(zpad[:, :, L + HALO:L + 2 * HALO], 0.0).then_inc(zeroed, 1)
            for n in range(10):
                if n >= 2:
                    src, b = (("k", n - 2), ("v", n - 4), ("v", n - 4), ("g", n - 8))[min((n - 2) // 2, 3)]
                    j = J[src, b, 0 if src == "g" else 1]
                    pool.wait_ge(pair_free[j["pair"]], j["use"] + 1)
                pool.dma_start(biasr[:, n % 2, :], a["bias_rows"][:, n * 512:(n + 1) * 512].partition_broadcast(P)
                               ).then_inc(bias_full[n % 2], 16)
            pool.wait_ge(moe[0]["uf_ready"], 1)
            pool.dma_start(flat(S0s), a["ws"].rearrange("s g t -> s (g t)")).then_inc(b2["ld"], 16)
            for g in range(8):
                pool.dma_start(flat(Ph)[64 * (g % 2):64 * (g % 2) + 64, (g // 2) * P:(g // 2 + 1) * P],
                               a["gm_b"][:, g * P:(g + 1) * P].partition_broadcast(64)).then_inc(b2["ld"], 16)
            pool.dma_start(hot, a["hot"]).then_inc(b2["ld"], 16)
            pool.dma_start(rel, a["rel"]).then_inc(b2["ld"], 16)
            pool.dma_start(outside, a["outside"]).then_inc(b2["ld"], 16)
            pool.wait_ge(b2["relb_dram"], 16)
            for h in range(QH):
                pool.dma_start(RA[:, DT + h, :], bass.AP(tensor=relb_d, offset=h * P * 384 + 127, ap=[[383, P], [1, L]])
                               ).then_inc(b2["relb_full"], 16)

        @block.scalar
        def _(act):
            own = Own(act, act_own)
            act.dma_start(cin[:, :, :], a["cT"]).then_inc(ld_c, 16)
            act.dma_start(vec[:, :], a["vec"]).then_inc(ld_small, 16)
            act.dma_start(const[:, :], a["const"]).then_inc(ld_small, 16)
            act.dma_start(row[:, :], a["rows"].partition_broadcast(P)).then_inc(ld_small, 16)
            act.dma_start(wr[0][:, :, :], a["wr0"]).then_inc(ld_small, 16)
            act.dma_start(wr[1][:, :, :], a["wr1"]).then_inc(ld_small, 16)
            act.dma_start(hT[:, :, :], a["xT"]).then_inc(ld_x, 16)
            act.dma_start(ctxT, a["ctxT"]).then_inc(ld_x, 16)
            act.wait_ge(ld_c, 16)
            act.wait_ge(zeroed, 1)
            nc.scalar.activation(sT[:, :, 0:2], cin[:, :, :], ACT.Silu).then_inc(silu_c, 1)
            act.wait_ge(lg_abs, 1)
            nc.scalar.activation(lgs[:, 1, :], lgs[:, 0, :], ACT.Exp, scale=-1.0).then_inc(lg_exp, 1)
            act.wait_ge(lg_ready, 1)
            nc.scalar.activation(wctx[:, :, :, :], wctx[:, :, :, :], ACT.Exp).then_inc(wctx_exp, 1)
            act.wait_ge(ld_x, 32)
            act.wait_ge(u_mod, 1)
            for r, (src, dst) in enumerate(((hT, uT), (ctxT, ucT))):
                for t in range(DT):
                    ins = nc.scalar.activation(dst[:, t, :], src[:, t, :], ACT.Identity, bias=modT[:, r, t:t + 1],
                                               scale=modT[:, r, 8 + t:9 + t])
                ins.then_inc(u_ready, 1)
            for b in range(4):
                j = J["glu", b, 0]
                job_wait(act, j)
                for i in range(2):
                    ins = nc.scalar.activation(raw[:, 2 * (b % 2) + i, :], PP[j["pair"]][:, 2 + i, :], ACT.Sigmoid,
                                               bias=col("b_zb", 2 * b + i))
                ins.then_inc(sig_ready, 1)

            def raw_copy(r, src, b, bias):
                j = J[src, b, 0]
                job_wait(act, j)
                if r:
                    act.wait_ge(rope_done, r)
                else:
                    act.wait_ge(pair_free[1], J["glu", 3, 0]["use"] + 1)
                for i in range(4):
                    ins = nc.scalar.activation(raw[:, i, :], PP[j["pair"]][:, i, :], ACT.Identity,
                                               bias=col(bias, 4 * b + i))
                ins.then_inc(pair_free[j["pair"]], 1)
            for r, (src, b, bias) in enumerate((("k", 0, "b_k"), ("k", 1, "b_k"), ("q", 0, "b_q"), ("q", 1, "b_q"))):
                raw_copy(r, src, b, bias)
            nfb = cst("nfb", 512)

            def exps(h):
                act.wait_ge(lg_ready, 1)
                act.wait_ge(rope_done, 4)
                if h >= 2:
                    act.wait_ge(prep, h - 1)
                for d in range(2):
                    nc.scalar.activation(Eqd[:, 2 * (h % 2) + d, :], nfb[:, d * L:(d + 1) * L], ACT.Exp,
                                         scale=lg[:, 8 * d + h:8 * d + h + 1])
                act.wait_ge(dec_arg, h + 1)
                dd = Ddec[:, 2 * (h % 2):2 * (h % 2) + 2, :]
                nc.scalar.activation(dd, dd, ACT.Exp).then_inc(dec_ready, 1)

            def s0_copy(h):
                act.wait_ge(s0_ps, h + 1)
                if h >= 2:
                    act.wait_ge(o_ps, h - 1)
                nc.scalar.activation(S0s[:, 2 * (h % 2):2 * (h % 2) + 2, :], MB[0][:, :, :], ACT.Copy).then_inc(s0_sb, 1)

            def o_copy(h):
                act.wait_ge(o_ps, h + 1)
                nc.scalar.activation(On[:, :, h * DV:(h + 1) * DV], MB[2 + h % 2][:, :, :], ACT.Copy).then_inc(o_kept, 1)
            exps(0)
            for h in range(HEADS):
                if h + 1 < HEADS:
                    exps(h + 1)
                s0_copy(h)
                if h:
                    o_copy(h - 1)
            o_copy(HEADS - 1)
            act.wait_ge(var_ready, 1)
            nc.scalar.activation(rstd[:, :], rstd[:, :], ACT.Sqrt).then_inc(std_ready, 1)

            def turned_copy(b):
                act.wait_ge(ret_turned, b + 1)
                for q in range(2):
                    ins = nc.scalar.activation(retT[:, 4 * b + 2 * q:4 * b + 2 * q + 2, :], MB[2 * (b % 2) + q][:, :, :],
                                               ACT.Copy)
                ins.then_inc(ret_kept, 1)
            for b in range(4):
                j = J["g", b, 0]
                act.wait_ge(pair_free[j["pair"]], j["use"] + 1)
                nc.scalar.activation(raw[:, :, :], raw[:, :, :], ACT.Silu).then_inc(g_silu, 1)
                if b:
                    turned_copy(b - 1)
            turned_copy(3)
            for b in range(4):
                j = J["gates", b, 0]
                job_wait(act, j)
                for i in range(4):
                    ins = nc.scalar.activation(gT[:, 4 * b + i, :], PP[j["pair"]][:, i, :], ACT.Sigmoid,
                                               bias=col("b_gates", 4 * b + i))
                ins.then_inc(pair_free[j["pair"]], 1)

            def norm(name, src, dst, func, g, b):
                n = LNS[name]
                m = n["mean"]
                act.wait_ge(ln_dve, n["dve"] + m) if n["dve"] + m else None
                if name == "attn":
                    act.wait_ge(ln_act, LNS["ln2"]["end"])
                if name in ("ffn", "final") and not m:
                    act.wait_ge(h_ready, 2 if name == "ffn" else 3)
                say(act, nc.scalar.activation(SQ[:, :, :], dst[:, :, :] if m else src[:, :, :], ACT.Square), ln_act,
                    n["act"] + 1)
                act.wait_ge(ln_dve, n["dve"] + m + 1)
                nc.scalar.activation(rs[:, :], rs[:, :], ACT.Sqrt).then_inc(ln_act, 1)
                act.wait_ge(ln_dve, n["dve"] + m + 2)
                for t in range(DT):
                    ins = nc.scalar.activation(dst[:, t, :], dst[:, t, :], func, scale=col(g, t), bias=col(b, t) if b else 0.0)
                say(act, ins, ln_act, n["act"] + 3)
            norm("conv", conv, conv, ACT.Silu, "conv_g", "conv_lb")
            norm("ln1", hT, hT, ACT.Identity, "ln1_g", "ln1_b")
            act.wait_ge(u_mod, 2)
            for t in range(DT):
                ins = nc.scalar.activation(uT[:, t, :], hT[:, t, :], ACT.Identity, bias=modT[:, 0, 24 + t:25 + t],
                                           scale=modT[:, 0, 32 + t:33 + t])
            ins.then_inc(moe[0]["uf_ready"], 1)

            def route_and_experts(n):
                m = moe[n]
                for t in range(LT):
                    act.wait_ge(m["u_turned"], t + 1)
                    ins = nc.scalar.activation(Kct[:, t, :], flat(PP[t]), ACT.Copy)
                ins.then_inc(m["u_rows"], 1)
                act.wait_ge(m["gexp_in"], 1)
                nc.scalar.activation(r_("gd"), r_("gd"), ACT.Exp).then_inc(m["gexp_out"], 1)
                act.wait_ge(m["eexp_in"], 1)
                nc.scalar.activation(r_("e2"), r_("e2"), ACT.Exp).then_inc(m["eexp_out"], 1)

                def keep(done, value, out, src, ready, **kw):
                    act.wait_ge(m[done], value)
                    nc.scalar.activation(out, src, ACT.Copy, **kw).then_inc(m[ready], 1)

                def keep_rows(value):
                    keep("gathered", value, xg, bank[3], "xg_kept")

                def keep_turned(value):
                    keep("xt_ps", value, xts, bank[0].rearrange("p (c m) -> p c m", c=4), "xts_ready")
                keep_rows(1)
                act.wait_ge(m["bc_ps"], 1)
                nc.scalar.activation(placer, bank[1].rearrange("p (k n) -> p k n", k=2), ACT.Copy, scale=float(D))
                nc.scalar.activation(weightr, bank[2].rearrange("p (k n) -> p k n", k=2), ACT.Copy, scale=float(D)
                                     ).then_inc(m["bc_kept"], 1)
                keep_turned(1)
                act.wait_ge(m["items_ready"], 1)
                T = act.value_load(tab[0:1, 64:65], min_val=EXPERTS[n], max_val=EXPERTS[n] + 8)
                with act.Fori(0, T) as i:
                    act.wait_ge(m["gate_done"], i + 1)
                    act.wait_ge(m["hid_ready"], i + 1)
                    nc.scalar.activation(sg, bank[0][:, 0:L], ACT.Silu).then_inc(m["sg_ready"], 1)
                    keep_rows(i + 2)
                    keep_turned(i + 2)
                    keep("ht_ps", i + 1, hts, bank[1][:, L:2 * L].rearrange("p (c m) -> p c m", c=2), "ht_ready")
            route_and_experts(0)
            norm("ln2", hT, hT, ACT.Identity, "ln2_g", "ln2_b")
            norm("attn", hT, uT, ACT.Identity, "attn_g", None)
            act.wait_ge(b2["relb_sb"], 1)
            act.dma_start(relb_d.ap(), relb[:, None, :].broadcast_to([QH, P, 384])).then_inc(b2["relb_dram"], 16)

            def copy_job(src, out, func, b=0, **kw):
                j = J[src, b, 0]
                job_wait(act, j)
                say(act, nc.scalar.activation(out, PP[j["pair"]][:, :, :], func, **kw), pair_free[j["pair"]], j["use"] + 1)
            copy_job("u2", gu, ACT.Gelu_apprx_tanh)
            copy_job("v2", raw[:, :, :], ACT.Gelu_apprx_tanh)
            copy_job("q2", q2, ACT.Copy)
            act.wait_ge(b2["vvar"], 1)
            nc.scalar.activation(rs[:, 0:2], rs[:, 0:2], ACT.Sqrt).then_inc(b2["vstd"], 1)
            j = J["kv2", 0, 0]
            job_wait(act, j)
            nc.scalar.activation(k2, PP[j["pair"]][:, 0, :], ACT.Copy, scale=HD ** -0.5)
            say(act, nc.scalar.activation(v2, PP[j["pair"]][:, 2, :], ACT.Copy), pair_free[j["pair"]], j["use"] + 1)
            copy_job("gates2", gT[:, 0:4, :], ACT.Sigmoid, 0)
            for qb in range(2):
                act.wait_ge(b2["sc_sb"], qb + 1)
                w0 = 0 if qb else P
                nc.scalar.activation(Kc[:, :, w0:L], Kc[:, :, w0:L], ACT.Exp)
                nc.scalar.activation(r_("sk"), r_("sk"), ACT.Exp).then_inc(b2["p_exp"], 1)
                copy_job("gates2", gT[:, 4 + 8 * qb:8 + 8 * qb, :], ACT.Sigmoid, 1 + 2 * qb)
                act.wait_ge(b2["p_turned"], qb + 1)
                for q in range(4 if qb else 2):
                    ins = nc.scalar.activation(pT[:, q * 512:(q + 1) * 512], flat(MB[q]), ACT.Copy)
                ins.then_inc(b2["p_kept"], 1)
                if not qb:
                    copy_job("gates2", gT[:, 8:12, :], ACT.Sigmoid, 2)
            norm("ffn", hT, uT, ACT.Identity, "ffn_g", None)
            route_and_experts(1)
            norm("final", hT, uT, ACT.Identity, "final_g", None)

        @block.tensor
        def _(pe):
            def job(j):
                w_wait(pe, j["w"])
                if j["use"]:
                    pe.wait_ge(pair_free[j["pair"]], j["use"])
                W, out, kind = ring[:, j["w"] % RING, :], PP[j["pair"]], j["kind"]
                if kind == "ada":
                    for k in range(DT):
                        for c in range(4):
                            ins = pe.matmul(out[32 * c:32 * c + 32, 0, 0:P], sT[:, k, :],
                                            W[:, k * 512 + c * P:k * 512 + (c + 1) * P], start=k == 0, stop=k == DT - 1,
                                            tile_position=(0, 32 * c))
                elif kind in ("cm8", "cm4", "cm16"):
                    K = int(kind[2:])
                    X = {"cm8": {"mix": mT, "cout": conv, "out2": mT}.get(j["src"], uT), "cm16": retT,
                         "cm4": {"pa": conv[:, 4:8], "pb": Eqd}.get(j["src"])}[kind]
                    width = 4096 // K
                    for c in range(2 if K == 16 else 4):
                        at = c * P + (512 * j["half"] if K == 4 else 0)
                        for k in range(K):
                            ins = pe.matmul(out[:, c, :], W[:, k * width + at:k * width + at + P], X[:, k, :],
                                            start=k == 0, stop=k == K - 1)
                elif kind in ("tm8", "tm8c"):
                    X = ucT if kind == "tm8c" else uT
                    for t in range(LT):
                        for k in range(DT):
                            ins = pe.matmul(out[:, 2 * t:2 * t + 2, :].rearrange("p a n -> p (a n)"),
                                            X[:, k, t * P:(t + 1) * P], W[:, k * 512:(k + 1) * 512], start=k == 0,
                                            stop=k == DT - 1)
                elif kind == "kv":
                    for k in range(DT):
                        pe.matmul(out[:, 0, :], W[:, k * 256:k * 256 + P], uT[:, k, :], start=k == 0, stop=k == DT - 1)
                    for t in range(LT):
                        for k in range(DT):
                            ins = pe.matmul(out[:, 2, t * P:(t + 1) * P], uT[:, k, t * P:(t + 1) * P],
                                            W[:, k * 256 + P:(k + 1) * 256], start=k == 0, stop=k == DT - 1)
                ins.then_inc(job_done, 1)

            def turn_ada(b):
                j = J["ada", b, 0]
                pe.wait_ge(pair_free[j["pair"]], j["use"] + 1)
                if b >= 2:
                    pe.wait_ge(mod_part, b - 1)
                pe.transpose(MB[b % 2][:, 0, 0:P], adaS[:, b % 2, :], ident).then_inc(ada_turned, 1)
            pe.wait_ge(silu_c, 1)
            pe.wait_ge(ld_small, 80)
            for b in range(12):
                job(J["ada", b, 0])
                if b:
                    turn_ada(b - 1)
            turn_ada(11)
            pe.wait_ge(u_ready, 2)
            for b in range(4):
                job(J["glu", b, 0])

            def rotate(r):
                j = J["kq"[r // 2], r % 2, 0]
                pe.wait_ge(pair_free[j["pair"]], j["use"] + 1)
                pe.wait_ge(rope_done, r) if r else pe.wait_ge(mod_part, 12)
                for q in range(2):
                    ins = pe.matmul(MB[q][:, :, :].rearrange("p a n -> p (a n)"), rotm,
                                    raw[:, 2 * q:2 * q + 2, :].rearrange("p a n -> p (a n)"), start=True, stop=True)
                ins.then_inc(raw_rot, 1)
            for b in range(2):
                job(J["k", b, 0])
                job(J["k", b, 1])
                rotate(b)
            for b in range(4):
                job(J["v", b, 0])
                job(J["v", b, 1])
            job(J["q", 0, 0])
            rotate(2)
            job(J["q", 1, 0])
            rotate(3)

            def scores(h):
                pe.wait_ge(prep, h + 1)
                if h:
                    pe.wait_ge(s0_sb, h)
                else:
                    pe.wait_ge(rope_done, 4)
                k4 = kw[:, :, :].rearrange("p a n -> p (a n)").rearrange("p (a n) -> p a n", n=P)
                for d in range(2):
                    for m in range(LT):
                        ins = pe.matmul(MB[0][:, d, :], k4[:, 4 * (h % 2) + 2 * d + m, :], Vct[:, m, h * DV:(h + 1) * DV],
                                        start=m == 0, stop=m == LT - 1)
                ins.then_inc(s0_ps, 1)
                if h:
                    pe.wait_ge(p_sb, h)
                for m in range(LT):
                    ins = pe.matmul(MB[1][:, m, :], kT[:, h, m * P:(m + 1) * P], qT[:, h, :], start=True, stop=True)
                ins.then_inc(sc_ps, 1)

            def mix_head(h):
                pe.wait_ge(s0_sb, h + 1)
                pe.wait_ge(p_sb, h + 1)
                if h >= 2:
                    pe.wait_ge(o_kept, h - 1)
                o, q = MB[2 + h % 2], 2 * (h % 2)
                for t in range(LT):
                    for m in range(LT):
                        pe.matmul(o[:, t, :], Ph[:, q + m, t * P:(t + 1) * P], Vt[:, m, h * DV:(h + 1) * DV],
                                  start=m == 0, stop=False)
                    for d in range(2):
                        ins = pe.matmul(o[:, t, :], qd[:, q + d, t * P:(t + 1) * P], S0s[:, q + d, :], start=False,
                                        stop=d == 1)
                ins.then_inc(o_ps, 1)
            scores(0)
            for h in range(HEADS):
                if h + 1 < HEADS:
                    scores(h + 1)
                mix_head(h)

            def turn_ret(b):
                pe.wait_ge(ret_ready, b + 1)
                if b >= 2:
                    pe.wait_ge(ret_kept, b - 1)
                for i in range(4):
                    for t in range(LT):
                        ins = pe.transpose(MB[2 * (b % 2) + i // 2][:, i % 2, t * P:(t + 1) * P],
                                           On[:, t, b * 512 + i * P:b * 512 + (i + 1) * P], ident)
                ins.then_inc(ret_turned, 1)
            for b in range(4):
                job(J["g", b, 0])
                if b:
                    turn_ret(b - 1)
            job(J["gates", 0, 0])
            turn_ret(3)
            for b in range(1, 4):
                job(J["gates", b, 0])

            def sums(name, src, out, first):
                n = LNS[name]
                for k in range(DT):
                    ins = pe.matmul(out[:, 0, :], ones, src[:, k, :], start=k == 0, stop=k == DT - 1)
                ins.then_inc(ln_pe, 1)

            def norm(name, src):
                n = LNS[name]
                if n["mean"]:
                    sums(name, src, MB[0], True)
                pe.wait_ge(ln_act, n["act"] + 1)
                sums(name, SQ, MB[1], False)
            pe.wait_ge(ret_kept, 4)
            pe.wait_ge(conv_ready, 1)
            sums("conv", conv, MB[0], True)
            job(J["ret", 0, 0])
            job(J["ret", 1, 0])
            pe.wait_ge(ln_act, LNS["conv"]["act"] + 1)
            sums("conv", SQ, MB[1], False)
            job(J["ret", 2, 0])
            job(J["ret", 3, 0])
            pe.wait_ge(ln_act, LNS["conv"]["end"])
            for b in range(2):
                job(J["cout", b, 0])
            pe.wait_ge(mix_in, 2)
            for b in range(2):
                job(J["mix", b, 0])
            pe.wait_ge(h_mid, 2)
            norm("ln1", hT)

            def route_and_experts(n):
                m, E = moe[n], EXPERTS[n]
                cols = GROUPS + E
                for t in range(LT):
                    for k in range(DT):
                        ins = pe.matmul(MB[2][:, 0, t * 64:t * 64 + cols], uT[:, k, t * P:(t + 1) * P], wr[n][:, k, :],
                                        start=k == 0, stop=k == DT - 1)
                ins.then_inc(m["logits"], 1)
                for t in range(LT):
                    pe.wait_ge(pair_free[t], J_uses[n][t])
                    for k in range(DT):
                        ins = pe.transpose(flat(PP[t])[:, k * P:(k + 1) * P], uT[:, k, t * P:(t + 1) * P], ident)
                    ins.then_inc(m["u_turned"], 1)
                pe.wait_ge(m["hot_ready"], 1)
                M, tri = r_("M"), cst("tri", P)
                pe.matmul(MB[3][:, 0, 0:E], tri, M[:, 0:E], start=True, stop=True)
                pe.matmul(MB[3][:, 0, E:2 * E], tri, M[:, E:2 * E], start=True, stop=False)
                pe.matmul(MB[3][:, 0, E:2 * E], ones, M[:, 0:E], start=False, stop=True)
                for t in range(LT):
                    ins = pe.matmul(MB[3][:, 0, 2 * E:3 * E], ones, M[:, t * E:(t + 1) * E], start=t == 0, stop=t == 1)
                ins.then_inc(m["ranks"], 1)
                pe.wait_ge(m["items_in"], 1)
                pe.transpose(MB[3][0:1, 1, 0:P], r_("item"), ident).then_inc(m["items_ps"], 1)

                def gather():
                    for t in range(LT):
                        for g in range(2):
                            ins = pe.matmul(bank[3][SLOTS * g:SLOTS * (g + 1), :], G[:, t, :], Kct[:, t, g * 512:(g + 1) * 512],
                                            start=t == 0, stop=t == 1, tile_position=(0, SLOTS * g))
                    ins.then_inc(m["gathered"], 1)

                def turn_rows():
                    for c in range(4):
                        ins = pe.transpose(bank[0][:, c * P:(c + 1) * P], xg[:, c * P:(c + 1) * P], ident)
                    ins.then_inc(m["xt_ps"], 1)

                def scatter(ks, done=None):
                    for k in ks:
                        g = slice(SLOTS * (k // 4), SLOTS * (k // 4 + 1))
                        ins = pe.matmul(MB[k // 2][:, k % 2, :], ys[g, (k % 4) * P:(k % 4 + 1) * P], S[g, :], start=False,
                                        stop=done == "acc_done" and k % 2 == 1, tile_position=(SLOTS * (k // 4), 0))
                        if done is not None and k in ks[-2:]:
                            ins.then_inc(m[done], 1)
                pe.wait_ge(m["u_rows"], 1)
                pe.wait_ge(m["g_ready"], 1)
                gather()
                pe.wait_ge(m["diag_ready"], 1)
                for v in range(2):
                    ins = pe.matmul(bank[1 + v], ones, diag[:, v].rearrange("p q n -> p (q n)"), start=True, stop=True)
                ins.then_inc(m["bc_ps"], 1)
                pe.wait_ge(m["xg_kept"], 1)
                turn_rows()
                pe.wait_ge(m["y_kept"], 1)
                pe.wait_ge(m["s_ready"], 1)
                pe.wait_ge(m["items_ready"], 1)
                for q in range(4):
                    pe.matmul(flat(MB[q]), ys[:, 0:P], ys, start=True, stop=False)
                pe.wait_ge(m["bc_kept"], 1)
                T = pe.value_load(tab[0:1, 64:65], min_val=EXPERTS[n], max_val=EXPERTS[n] + 8)
                with pe.Fori(0, T) as i:
                    def gate_or_up(q, done):
                        for k in range(DT):
                            for g in range(2):
                                ins = pe.matmul(bank[q][SLOTS * g:SLOTS * (g + 1), 0:L],
                                                xts[:, k % 4, SLOTS * (k // 4):SLOTS * (k // 4 + 1)],
                                                ring[:, q, k * 512 + g * 256:k * 512 + (g + 1) * 256], start=k == 0,
                                                stop=k == DT - 1, tile_position=(0, SLOTS * g))
                        ins.then_inc(m[done], 1)
                    pe.wait_ge(m["xts_ready"], i + 1)
                    pe.wait_ge(m["wg_full"], i * 16 + 16)
                    gate_or_up(0, "gate_done")
                    pe.wait_ge(m["g_ready"], i + 2)
                    gather()
                    pe.wait_ge(m["wu_full"], i * 16 + 16)
                    gate_or_up(1, "up_done")
                    pe.wait_ge(m["xg_kept"], i + 2)
                    pe.wait_ge(m["sg_ready"], i + 1)
                    turn_rows()
                    pe.wait_ge(m["y_kept"], i + 1)
                    pe.wait_ge(m["s_ready"], i + 1)
                    scatter((0, 4, 1, 5))
                    pe.wait_ge(m["hid_ready"], i + 2)
                    for c in range(2):
                        ins = pe.transpose(bank[1][:, L + c * P:L + (c + 1) * P], hid[:, c * P:(c + 1) * P], ident)
                    ins.then_inc(m["ht_ps"], 1)
                    scatter((2, 6, 3, 7), "scattered")
                    pe.wait_ge(m["wd_full"], i * 16 + 16)
                    pe.wait_ge(m["ht_ready"], i + 1)
                    for k in range(4):
                        for g in range(2):
                            ins = pe.matmul(bank[2][SLOTS * g:SLOTS * (g + 1), :],
                                            hts[:, k % 2, SLOTS * (k // 2):SLOTS * (k // 2 + 1)],
                                            ring[:, 2, k * D + g * 512:k * D + (g + 1) * 512], start=k == 0, stop=k == 3,
                                            tile_position=(0, SLOTS * g))
                    ins.then_inc(m["down_done"], 1)
                pe.wait_ge(m["y_kept"], T + 1)
                pe.wait_ge(m["s_ready"], T + 1)
                scatter((0, 4, 1, 5, 2, 6, 3, 7), "acc_done")
            J_uses = [[0, 0], [0, 0]]
            for n in range(2):
                for j in jobs:
                    if j["w"] < moe_w[n]:
                        J_uses[n][j["pair"]] = j["use"] + 1
            pe.wait_ge(moe[0]["uf_ready"], 1)
            route_and_experts(0)
            pe.wait_ge(h_ready, 1)
            norm("ln2", hT)
            norm("attn", hT)
            pe.wait_ge(b2["ld"], 16 * 12)
            pe.matmul(flat(MB[2])[0:QH, 0:384], rel, hot, start=True, stop=True).then_inc(b2["relb_ps"], 1)
            pe.wait_ge(ln_act, LNS["attn"]["end"])
            for n in ("u2", "v2", "q2", "kv2", "gates2"):
                job(J[n, 0, 0])
            pe.wait_ge(b2["v_ready"], 1)
            pe.wait_ge(b2["ws_ready"], 1)
            for g in range(8):
                for c in range(LT):
                    ins = pe.matmul(MB[g // 4][64 * (g % 2):64 * (g % 2) + 64, (g // 2) % 2, c * P:(c + 1) * P],
                                    raw2[:, c, g * 64:(g + 1) * 64], ws[:, g, :], start=True, stop=True,
                                    tile_position=(0, 64 * (g % 2)))
            ins.then_inc(b2["sp_ps"], 1)

            def attn_scores(qb):
                if qb:
                    pe.wait_ge(b2["b_ready"], 1)
                else:
                    pe.wait_ge(b2["a_ready"], 1)
                    j = J["kv2", 0, 0]
                    pe.wait_ge(pair_free[j["pair"]], j["use"] + 1)
                per = 2 if qb else 4
                for h in range(QH):
                    at = 64 * (h // 4)
                    ins = pe.matmul(flat(MB[h // per])[:, (h % per) * (512 // per):(h % per + 1) * (512 // per)],
                                    q2[at:at + 64, h % 4, qb * P:(qb + 1) * P], k2[at:at + 64, 0:(qb + 1) * P],
                                    start=True, stop=True, tile_position=(at, 0))
                ins.then_inc(b2["sc_ps"], 1)

            def attn_turn(qb):
                pe.wait_ge(b2["p_ready"], qb + 1)
                i = 0
                for h in range(QH):
                    for kb in range(0 if qb else 1, 2):
                        ins = pe.transpose(flat(MB[i // 4])[:, (i % 4) * P:(i % 4 + 1) * P], Kc[:, h, kb * P:(kb + 1) * P], ident)
                        i += 1
                ins.then_inc(b2["p_turned"], 1)

            def attn_out(qb):
                pe.wait_ge(b2["p_kept"], qb + 1)
                n = qb + 1
                for h in range(QH):
                    for kb in range(n):
                        ins = pe.matmul(flat(MB[0])[64 * (h % 2):64 * (h % 2) + 64, (h // 2) * P:(h // 2 + 1) * P],
                                        v2[:, kb * P + 64 * (h // 4):kb * P + 64 * (h // 4) + 64],
                                        pT[:, (h * n + kb) * P:(h * n + kb + 1) * P], start=kb == 0, stop=kb == n - 1,
                                        tile_position=(0, 64 * (h % 2)))
                ins.then_inc(b2["b_ps"], 1)
            attn_scores(0)
            job(J["gates2", 1, 0])
            attn_turn(0)
            job(J["gates2", 2, 0])
            attn_out(0)
            attn_scores(1)
            job(J["gates2", 3, 0])
            attn_turn(1)
            job(J["pa", 0, 0])
            job(J["pa", 0, 1])
            attn_out(1)
            pe.wait_ge(b2["b_ready"], 2)
            job(J["pb", 0, 0])
            job(J["pb", 0, 1])
            pe.wait_ge(b2["m_ready"], 2)
            for b in range(2):
                job(J["out2", b, 0])
            norm("ffn", hT)
            pe.wait_ge(ln_act, LNS["ffn"]["end"])
            route_and_experts(1)
            norm("final", hT)

        @block.vector
        def _(dve):
            V_ = nc.vector
            own = Own(dve, dve_own)
            link = own.link

            def evac(j, ins):
                say(dve, ins, pair_free[j["pair"]], j["use"] + 1)
            dve.wait_ge(ld_small, 80)
            x = rowc("decay", 16)
            say(dve, V_.scalar_tensor_tensor(lgs[:, 0, :], x, -1.0, x, ALU.mult, ALU.max), lg_abs, 1)
            dve.wait_ge(lg_exp, 1)
            link(V_.tensor_scalar(lgs[:, 2, :], lgs[:, 1, :], 2.0, None, ALU.add))
            link(V_.reciprocal(lgs[:, 2, :], lgs[:, 2, :]))
            link(V_.tensor_tensor(lgs[:, 1, :], lgs[:, 1, :], lgs[:, 2, :], ALU.mult))
            link(V_.tensor_tensor(lgs[:, 2, :], lgs[:, 1, :], lgs[:, 1, :], ALU.mult))
            link(V_.tensor_scalar(lgs[:, 3, :], lgs[:, 2, :], 1 / 17, None, ALU.mult))
            for c in (15, 13, 11, 9, 7, 5, 3):
                link(V_.scalar_tensor_tensor(lgs[:, 3, :], lgs[:, 3, :], 1 / c, lgs[:, 2, :], ALU.add, ALU.mult))
            link(V_.scalar_tensor_tensor(lgs[:, 3, :], lgs[:, 3, :], 1.0, lgs[:, 1, :], ALU.add, ALU.mult))
            link(V_.tensor_scalar(lgs[:, 4, :], x, 0.0, None, ALU.min))
            link(V_.scalar_tensor_tensor(lg, lgs[:, 3, :], -2.0, lgs[:, 4, :], ALU.mult, ALU.add))
            for m in range(LT):
                for d in range(2):
                    ins = V_.tensor_scalar(wctx[:, m, d, :], lg[:, 8 * d:8 * d + 8], cst("mctx", 4)[:, 2 * m + d:2 * m + d + 1],
                                           None, ALU.mult)
            say(dve, ins, lg_ready, 1)

            def modulation(b):
                dve.wait_ge(ada_turned, b + 1)
                T = MB[b % 2][:, 0, 0:P].rearrange("p (c r) -> p c r", r=32)
                for r in range(2):
                    ins = V_.tensor_tensor(modT[:, r, 4 * b:4 * b + 4], T[:, :, r], vec[:, 4 * b:4 * b + 4], ALU.add)
                say(dve, ins, mod_part, b + 1)
                if b == 3:
                    say(dve, V_.tensor_scalar(modT[:, :, 8:16], modT[:, :, 8:16], 1.0, None, ALU.add), u_mod, 1)
                if b == 11:
                    say(dve, V_.tensor_scalar(modT[:, 0, 32:40], modT[:, 0, 32:40], 1.0, None, ALU.add), u_mod, 2)
            for b in range(12):
                j = J["ada", b, 0]
                job_wait(dve, j)
                if b >= 2:
                    dve.wait_ge(ada_turned, b - 1)
                evac(j, V_.tensor_copy(adaS[:, b % 2, :], PP[j["pair"]][:, 0, 0:P]))
                if b:
                    modulation(b - 1)
            modulation(11)
            dve.wait_ge(zeroed, 3)
            for b in range(4):
                j = J["glu", b, 0]
                dve.wait_ge(sig_ready, b + 1)
                for i in range(2):
                    ins = V_.scalar_tensor_tensor(zpad[:, 2 * b + i, HALO:HALO + L], PP[j["pair"]][:, i, :],
                                                  col("b_za", 2 * b + i), raw[:, 2 * (b % 2) + i, :], ALU.add, ALU.mult)
                evac(j, ins)

            def rope(r):
                dst = (kT, qT)[r // 2][:, 4 * (r % 2):4 * (r % 2) + 4, :]
                cos4, sin2 = (cst(n, L).unsqueeze(1).to_broadcast([P, k, L]) for n, k in (("cos", 4), ("sin", 2)))
                dve.wait_ge(raw_rot, r + 1)
                V_.tensor_tensor(Eqd[:, :, :], raw[:, :, :], cos4, ALU.mult)
                for q in range(2):
                    ins = V_.tensor_tensor(dst[:, 2 * q:2 * q + 2, :], MB[q][:, :, :], sin2, ALU.mult)
                link(ins)
                say(dve, V_.tensor_tensor(dst, dst, Eqd[:, :, :], ALU.add), rope_done, r + 1)

            def with_bias(j, n, dst):
                job_wait(dve, j)
                dve.wait_ge(bias_full[n % 2], 16 * (n // 2 + 1))
                evac(j, V_.tensor_tensor(dst, PPt[j["pair"]], biasr[:, n % 2, :].unsqueeze(1).to_broadcast([P, LT, 512]), ALU.add))

            def convolve(t):
                tap = [col("taps", t * TAPS + k) for k in range(TAPS)]
                link(V_.tensor_scalar(conv[:, t, :], zpad[:, t, 0:L], tap[0], col("conv_b", t), ALU.mult, ALU.add))
                for k in range(1, TAPS):
                    ins = V_.scalar_tensor_tensor(conv[:, t, :], zpad[:, t, k:k + L], tap[k], conv[:, t, :], ALU.mult, ALU.add)
                    if k < TAPS - 1 or t < DT - 1:
                        link(ins)
                    else:
                        say(dve, ins, conv_ready, 1)
            for b in range(2):
                with_bias(J["k", b, 1], b, Kct[:, :, b * 512:(b + 1) * 512])
                rope(b)
            for b in range(4):
                with_bias(J["v", b, 0], 2 + b, Vt[:, :, b * 512:(b + 1) * 512])
                convolve(2 * b)
                with_bias(J["v", b, 1], 2 + b, Vct[:, :, b * 512:(b + 1) * 512])
                convolve(2 * b + 1)
            rope(2)
            rope(3)
            k4 = kw[:, :, :].rearrange("p a n -> p (a n)").rearrange("p (a n) -> p a n", n=P)

            def prepare(h):
                q = 2 * (h % 2)
                f = Ddec[:, q:q + 2, :].rearrange("p a n -> p (a n)")
                link(V_.scalar_tensor_tensor(f, cst("dpos", 512), lg[:, h:h + 1], cst("ln2", 512), ALU.mult, ALU.add))
                say(dve, V_.scalar_tensor_tensor(f, cst("dneg", 512), lg[:, 8 + h:9 + h], f, ALU.mult, ALU.add), dec_arg, h + 1)
                dve.wait_ge(wctx_exp, 1)
                if h >= 2:
                    dve.wait_ge(s0_ps, h - 1)
                    dve.wait_ge(o_ps, h - 1)
                for d in range(2):
                    for m in range(LT):
                        V_.tensor_scalar(k4[:, 4 * (h % 2) + 2 * d + m, :], Kct[:, m, h * P:(h + 1) * P], wctx[:, m, d, h:h + 1],
                                         KSCALE, ALU.mult, ALU.mult)
                dve.wait_ge(dec_ready, h + 1)
                say(dve, V_.tensor_tensor(qd[:, q:q + 2, :], Eqd[:, q:q + 2, :], qT[:, h, :].unsqueeze(1).to_broadcast([P, 2, L]),
                                          ALU.mult), prep, h + 1)

            def stats(h):
                dve.wait_ge(o_kept, h + 1)
                for t in range(LT):
                    ins = V_.bn_stats(bst[:, t, :], On[:, t, h * DV:(h + 1) * DV])
                link(ins)
                for t in range(LT):
                    ins = V_.bn_aggr(mv[:, t, h, :], bst[:, t, :])
                say(dve, ins, o_stat, h + 1)
            prepare(0)
            for h in range(HEADS):
                if h + 1 < HEADS:
                    prepare(h + 1)
                dve.wait_ge(sc_ps, h + 1)
                q = 2 * (h % 2)
                say(dve, V_.scalar_tensor_tensor(Ph[:, q:q + 2, :], MB[1][:, :, :], KSCALE, Ddec[:, q:q + 2, :], ALU.mult,
                                                 ALU.mult), p_sb, h + 1)
                if h:
                    stats(h - 1)
            stats(HEADS - 1)
            say(dve, V_.tensor_scalar(rstd[:, :].rearrange("p (t h) -> p t h", t=LT), mv[:, :, :, 1], LN_EPS, None, ALU.add),
                var_ready, 1)
            dve.wait_ge(std_ready, 1)
            link(V_.reciprocal(rstd[:, :], rstd[:, :]))
            for t in range(LT):
                for h in range(HEADS):
                    o = On[:, t, h * DV:(h + 1) * DV]
                    ins = V_.tensor_scalar(o, o, mv[:, t, h, 0:1], rstd[:, t * HEADS + h:t * HEADS + h + 1], ALU.subtract, ALU.mult)
            link(ins)
            for b in range(4):
                with_bias(J["g", b, 0], 6 + b, raw2)
                dve.wait_ge(g_silu, b + 1)
                o = On[:, :, b * 512:(b + 1) * 512]
                say(dve, V_.tensor_tensor(o, o, raw2, ALU.mult), ret_ready, b + 1)

            def centre(name, src, dst):
                n = LNS[name]
                dve.wait_ge(ln_pe, n["pe"] + 1)
                say(dve, V_.tensor_tensor(dst[:, :, :], src[:, :, :], MB[0][:, 0:1, :].to_broadcast([P, DT, L]), ALU.subtract),
                    ln_dve, n["dve"] + 1)

            def scale(name, src, dst, eps):
                n = LNS[name]
                m = n["mean"]
                dve.wait_ge(ln_pe, n["pe"] + m + 1)
                say(dve, V_.tensor_scalar(rs[:, :], MB[1][:, 0, :], eps, None, ALU.add), ln_dve, n["dve"] + m + 1)
                dve.wait_ge(ln_act, n["act"] + 2)
                link(V_.reciprocal(rs[:, :], rs[:, :]))
                say(dve, V_.tensor_tensor(dst[:, :, :], src[:, :, :], rs[:, :].unsqueeze(1).to_broadcast([P, DT, L]), ALU.mult),
                    ln_dve, n["dve"] + m + 2)

            def ret(b):
                j = J["ret", b, 0]
                job_wait(dve, j)
                g3 = J["gates", 3, 0]
                dve.wait_ge(pair_free[g3["pair"]], g3["use"] + 1)
                evac(j, V_.tensor_tensor(mT[:, 2 * b:2 * b + 2, :], PP[j["pair"]][:, 0:2, :], gT[:, 2 * b:2 * b + 2, :], ALU.mult))
            centre("conv", conv, conv)
            ret(0)
            ret(1)
            scale("conv", conv, conv, LN_EPS)
            ret(2)
            ret(3)
            for b in range(2):
                j = J["cout", b, 0]
                job_wait(dve, j)
                for i in range(4):
                    ins = V_.scalar_tensor_tensor(raw[:, i, :], PP[j["pair"]][:, i, :], col("b_conv", 4 * b + i),
                                                  gT[:, 8 + 4 * b + i, :], ALU.add, ALU.mult)
                evac(j, ins)
                m4 = mT[:, 4 * b:4 * b + 4, :]
                say(dve, V_.tensor_tensor(m4, m4, raw[:, :, :], ALU.add), mix_in, b + 1)
            for b in range(2):
                j = J["mix", b, 0]
                job_wait(dve, j)
                for i in range(4):
                    ins = V_.tensor_scalar(raw[:, i, :], PP[j["pair"]][:, i, :], col("b_mix", 4 * b + i),
                                           modT[:, 0, 16 + 4 * b + i:17 + 4 * b + i], ALU.add, ALU.mult)
                evac(j, ins)
                h4 = hT[:, 4 * b:4 * b + 4, :]
                say(dve, V_.scalar_tensor_tensor(h4, h4, ALPHA, raw[:, :, :], ALU.mult, ALU.add), h_mid, b + 1)
            def first_of(out, val, top, n):
                eq, c = (r_(x).rearrange("p (t n) -> p t n", t=LT)[:, :, 0:n] for x in ("eq", "c"))
                link(V_.tensor_tensor(eq, val, top.unsqueeze(2).to_broadcast([P, LT, n]), ALU.is_equal))
                link(V_.scalar_tensor_tensor(c, eq, -64.0, cst("iota", n).unsqueeze(1).to_broadcast([P, LT, n]), ALU.mult, ALU.add))
                link(V_.tensor_reduce(r_("cm"), c, AX.X, ALU.min))
                link(V_.tensor_tensor(out, c, r_("cm").unsqueeze(2).to_broadcast([P, LT, n]), ALU.is_equal))

            def route(n):
                m, E = moe[n], EXPERTS[n]
                EG = E // GROUPS
                t2 = lambda x, w: r_(x)[:, 0:LT * w].rearrange("p (t n) -> p t n", t=LT)
                t4 = lambda x: r_(x)[:, 0:LT * E].rearrange("p (t g n) -> p t g n", t=LT, g=GROUPS)
                V_.memset(ys, 0.0).then_inc(m["y_kept"], 1)
                V_.memset(S, 0.0).then_inc(m["s_ready"], 1)
                V_.tensor_copy(slotno, cst("slot", SLOTS + 1))
                dve.wait_ge(m["logits"], 1)
                lt = t2("lt", GROUPS + E)
                link(V_.tensor_tensor(lt, MB[2][:, 0, 0:128].rearrange("p (t c) -> p t c", t=LT)[:, :, 0:GROUPS + E],
                                      rowc(f"rb{n}", GROUPS + E).unsqueeze(1).to_broadcast([P, LT, GROUPS + E]), ALU.add))
                link(V_.tensor_reduce(r_("gm"), lt[:, :, 0:GROUPS], AX.X, ALU.max))
                say(dve, V_.tensor_tensor(t2("gd", GROUPS), lt[:, :, 0:GROUPS], r_("gm").unsqueeze(2).to_broadcast([P, LT, GROUPS]),
                                          ALU.subtract), m["gexp_in"], 1)
                first_of(t2("hg", GROUPS), lt[:, :, 0:GROUPS], r_("gm"), GROUPS)
                hg = t2("hg", GROUPS).unsqueeze(3).to_broadcast([P, LT, GROUPS, EG])
                tmp = r_("tmp")[:, 0:LT * E].rearrange("p (t g n) -> p t g n", t=LT, g=GROUPS)
                le = lt[:, :, GROUPS:GROUPS + E].rearrange("p t (g n) -> p t g n", g=GROUPS)
                link(V_.tensor_tensor(tmp, le, hg, ALU.mult))
                ml = t2("ml", EG)
                link(V_.tensor_reduce(ml, tmp.rearrange("p t g n -> p t n g"), AX.X, ALU.add))
                link(V_.tensor_reduce(r_("m1"), ml, AX.X, ALU.max))
                first_of(t2("h1", EG), ml, r_("m1"), EG)
                link(V_.scalar_tensor_tensor(ml, t2("h1", EG), MASKED, ml, ALU.mult, ALU.add))
                link(V_.tensor_reduce(r_("m2"), ml, AX.X, ALU.max))
                say(dve, V_.tensor_tensor(r_("e2"), r_("m2"), r_("m1"), ALU.subtract), m["eexp_in"], 1)
                first_of(t2("h2", EG), ml, r_("m2"), EG)
                for A, h in (("A1", "h1"), ("A2", "h2")):
                    link(V_.tensor_tensor(t4(A), t2(h, EG).unsqueeze(2).to_broadcast([P, LT, GROUPS, EG]), hg, ALU.mult))
                say(dve, V_.tensor_tensor(r_("M")[:, 0:2 * E], r_("A1")[:, 0:2 * E], r_("A2")[:, 0:2 * E], ALU.add), m["hot_ready"], 1)
                dve.wait_ge(m["gexp_out"], 1)
                link(V_.tensor_reduce(r_("gw"), t2("gd", GROUPS), AX.X, ALU.add))
                dve.wait_ge(m["eexp_out"], 1)
                link(V_.scalar_tensor_tensor(r_("w1"), r_("e2"), 1.0, r_("gw"), ALU.add, ALU.mult))
                link(V_.reciprocal(r_("w1"), r_("w1")))
                link(V_.tensor_tensor(r_("w2"), r_("w1"), r_("e2"), ALU.mult))
                Sa, Sb = (r_(x).rearrange("p (t n) -> p t n", t=2) for x in ("Sa", "Sb"))
                V_.memset(r_("Sa"), 0.0)
                link(V_.memset(r_("Sb"), 0.0))
                dve.wait_ge(m["ranks"], 1)
                cnt, items = Sa[:, 0, 16:16 + E], Sa[:, 1, 16:16 + E]
                link(V_.tensor_scalar(cnt, MB[3][:, 0, 2 * E:3 * E], float(D), None, ALU.mult))
                link(V_.tensor_scalar(r_("rank")[:, 0:2 * E], MB[3][:, 0, 0:2 * E], float(D), None, ALU.mult))
                link(V_.tensor_scalar(items, cnt, float(SLOTS), 1.0, ALU.is_gt, ALU.add))
                for c in (2, 3):
                    link(V_.scalar_tensor_tensor(items, cnt, float(c * SLOTS), items, ALU.is_gt, ALU.add))
                A, B, step = Sa, Sb, 1
                while step < E:
                    link(V_.tensor_tensor(B[:, :, 16:16 + E], A[:, :, 16:16 + E], A[:, :, 16 - step:16 + E - step], ALU.add))
                    A, B, step = B, A, 2 * step
                first, total = A[:, 1, 15:15 + E], A[:, 1, 15 + E:16 + E]
                link(V_.tensor_scalar(r_("vx")[:, 0:E], first, cst("pcol", 1), None, ALU.is_le))
                link(V_.tensor_reduce(r_("item"), r_("vx")[:, 0:E], AX.X, ALU.add))
                say(dve, V_.tensor_scalar(r_("item"), r_("item"), -1.0, None, ALU.add), m["items_in"], 1)
                vx, rank, pos = t2("vx", E), t2("rank", E), r_("pos")
                link(V_.scalar_tensor_tensor(vx, first.unsqueeze(1).to_broadcast([P, LT, E]), float(SLOTS), rank, ALU.mult, ALU.add))
                for k, A_ in enumerate(("A1", "A2")):
                    link(V_.tensor_tensor(t2("tmp", E), t2(A_, E), vx, ALU.mult))
                    link(V_.tensor_reduce(pos[:, 2 * k:2 * k + 2], t2("tmp", E), AX.X, ALU.add))

                def rows_of_item(linked):
                    linked(V_.tensor_tensor(Ek, slotno[:, 0:SLOTS].unsqueeze(1).to_broadcast([P, 4, SLOTS]),
                                            pos.unsqueeze(2).to_broadcast([P, 4, SLOTS]), ALU.is_equal))
                    V_.tensor_tensor(G, Ek[:, 0:2], Ek[:, 2:4], ALU.add).then_inc(m["g_ready"], 1)
                rows_of_item(link)
                for v, x in ((0, pos), (1, rt[:, RT["w1"]:RT["w1"] + 4])):
                    ins = V_.tensor_tensor(diag[:, v], ident.unsqueeze(1).to_broadcast([P, 4, P]),
                                           x.unsqueeze(2).to_broadcast([P, 4, P]), ALU.mult)
                ins.then_inc(m["diag_ready"], 1)
                link(V_.tensor_scalar(slotno, slotno, float(SLOTS), None, ALU.add))
                dve.wait_ge(m["items_ps"], 1)
                V_.tensor_copy(tab[0:1, 64:65], total[0:1])
                say(dve, V_.tensor_copy(tab[0:1, 0:64], MB[3][0:1, 1, 0:64]), m["items_ready"], 1)
                dve.wait_ge(m["gathered"], 1)
                rows_of_item(link)
                dve.sem_inc(m["hid_ready"], 1)
                dve.wait_ge(m["bc_kept"], 1)
                T = dve.value_load(tab[0:1, 64:65], min_val=E, max_val=E + 8)
                with dve.Fori(0, T) as i:
                    steps = [0]

                    def linked(ins):
                        steps[0] += 1
                        ins.then_inc(m["step"], 1)
                        dve.wait_ge(m["step"], i * 4 + steps[0])
                    linked(V_.tensor_scalar(slotno, slotno, float(SLOTS), None, ALU.add))
                    dve.wait_ge(m["gathered"], i + 2)
                    rows_of_item(linked)
                    dve.wait_ge(m["sg_ready"], i + 1)
                    dve.wait_ge(m["up_done"], i + 1)
                    V_.tensor_tensor(hid, bank[1][:, 0:L], sg, ALU.mult).then_inc(m["hid_ready"], 1)
                    dve.wait_ge(m["scattered"], i * 2 + 2)
                    for k in range(2):
                        linked(V_.scalar_tensor_tensor(Sk[:, k], placer[:, k], slotno[:, SLOTS:SLOTS + 1], weightr[:, k],
                                                       ALU.is_equal, ALU.mult))
                    V_.tensor_tensor(S, Sk[:, 0], Sk[:, 1], ALU.add).then_inc(m["s_ready"], 1)
                    dve.wait_ge(m["down_done"], i + 1)
                    V_.tensor_copy(ys, bank[2]).then_inc(m["y_kept"], 1)
                if n == 0:
                    link(V_.tensor_scalar(hT[:, :, :], hT[:, :, :], ALPHA, None, ALU.mult))
                dve.wait_ge(m["acc_done"], 2)
                for k in range(DT):
                    if n == 0:
                        ins = V_.scalar_tensor_tensor(hT[:, k, :], MB[k // 2][:, k % 2, :], modT[:, 0, 40 + k:41 + k], hT[:, k, :],
                                                      ALU.mult, ALU.add)
                    else:
                        ins = V_.tensor_tensor(hT[:, k, :], MB[k // 2][:, k % 2, :], hT[:, k, :], ALU.add)
                say(dve, ins, h_ready, 1 + 2 * n)
            centre("ln1", hT, hT)
            scale("ln1", hT, hT, LN_EPS)
            route(0)
            centre("ln2", hT, hT)
            scale("ln2", hT, hT, LN_EPS)
            scale("attn", hT, uT, RMS_EPS)
            dve.wait_ge(b2["relb_ps"], 1)
            dve.wait_ge(b2["ld"], 16 * 12)
            say(dve, V_.tensor_tensor(relb, flat(MB[2])[0:QH, 0:384], outside, ALU.add), b2["relb_sb"], 1)
            say(dve, V_.tensor_tensor(ws, ws, cst("causal", P).unsqueeze(1).to_broadcast([P, 8, P]), ALU.mult), b2["ws_ready"], 1)
            j = J["v2", 0, 0]
            dve.wait_ge(pair_free[j["pair"]], j["use"] + 1)
            for t in range(LT):
                ins = V_.bn_stats(bst[:, t, :], raw2[:, t, :])
            link(ins)
            for t in range(LT):
                ins = V_.bn_aggr(mv[:, t, 0, :], bst[:, t, :])
            link(ins)
            dve.wait_ge(ln_act, LNS["attn"]["end"])
            say(dve, V_.tensor_scalar(rs[:, 0:2], mv[:, :, 0, 1], RMS_EPS, None, ALU.add), b2["vvar"], 1)
            dve.wait_ge(b2["vstd"], 1)
            link(V_.reciprocal(rs[:, 0:2], rs[:, 0:2]))
            for t in range(LT):
                ins = V_.tensor_scalar(raw2[:, t, :], raw2[:, t, :], mv[:, t, 0, 0:1], rs[:, t:t + 1], ALU.subtract, ALU.mult)
            link(ins)
            say(dve, V_.tensor_tensor(raw2, raw2, rowc("gm_g", 512).unsqueeze(1).to_broadcast([P, LT, 512]), ALU.mult),
                b2["v_ready"], 1)
            dve.wait_ge(b2["sp_ps"], 1)
            for q in range(2):
                bias = flat(Ph)[:, 0:512].rearrange("p (a t) -> p a t", a=4)[:, 2 * q:2 * q + 2, :]
                ins = V_.tensor_tensor(aT[:, 2 * q:2 * q + 2, :].rearrange("p a (c t) -> p a c t", c=2),
                                       MB[q][:, :, :].rearrange("p a (c t) -> p a c t", c=2),
                                       bias.unsqueeze(2).to_broadcast([P, 2, LT, P]), ALU.add)
            link(ins)
            say(dve, V_.tensor_tensor(aT, aT, gu, ALU.mult), b2["a_ready"], 1)
            dve.wait_ge(b2["relb_full"], 16 * QH)
            for qb in range(2):
                dve.wait_ge(b2["sc_ps"], qb + 1)
                if qb:
                    dve.wait_ge(b2["p_turned"], 1)
                w0, per = (0, 2) if qb else (P, 4)
                sc = Kc[:, :, w0:L]
                for q in range(QH // per):
                    h = slice(q * per, (q + 1) * per)
                    ins = V_.tensor_tensor(Kc[:, h, w0:L], flat(MB[q]).rearrange("p (a n) -> p a n", a=per),
                                           RA[:, DT + q * per:DT + (q + 1) * per, w0:L], ALU.add)
                link(ins)
                link(V_.tensor_reduce(r_("mx"), sc, AX.X, ALU.max))
                link(V_.tensor_tensor(r_("mx"), r_("mx"), rowc("sinks", QH), ALU.max))
                V_.tensor_tensor(r_("sk"), rowc("sinks", QH), r_("mx"), ALU.subtract)
                say(dve, V_.tensor_tensor(sc, sc, r_("mx").unsqueeze(2).to_broadcast([P, QH, L - w0]), ALU.subtract),
                    b2["sc_sb"], qb + 1)
                dve.wait_ge(b2["p_exp"], qb + 1)
                link(V_.tensor_reduce(r_("den"), sc, AX.X, ALU.add))
                link(V_.tensor_tensor(r_("den"), r_("den"), r_("sk"), ALU.add))
                link(V_.reciprocal(r_("den"), r_("den")))
                say(dve, V_.tensor_tensor(sc, sc, r_("den").unsqueeze(2).to_broadcast([P, QH, L - w0]), ALU.mult),
                    b2["p_ready"], qb + 1)
                dve.wait_ge(b2["b_ps"], qb + 1)
                say(dve, V_.tensor_copy(bT[:, :, qb * P:(qb + 1) * P], flat(MB[0]).rearrange("p (a n) -> p a n", a=4)),
                    b2["b_ready"], qb + 1)
            g3 = J["gates2", 3, 0]
            dve.wait_ge(pair_free[g3["pair"]], g3["use"] + 1)
            for half in range(2):
                j = J["pa", 0, half]
                job_wait(dve, j)
                evac(j, V_.tensor_tensor(mT[:, 4 * half:4 * half + 4, :], PP[j["pair"]][:, :, :],
                                         gT[:, 4 * half:4 * half + 4, :], ALU.mult))
            for half in range(2):
                j = J["pb", 0, half]
                job_wait(dve, j)
                evac(j, V_.tensor_tensor(raw[:, :, :], PP[j["pair"]][:, :, :], gT[:, 8 + 4 * half:12 + 4 * half, :], ALU.mult))
                m4 = mT[:, 4 * half:4 * half + 4, :]
                say(dve, V_.tensor_tensor(m4, m4, raw[:, :, :], ALU.add), b2["m_ready"], half + 1)
            for b in range(2):
                j = J["out2", b, 0]
                job_wait(dve, j)
                h4 = hT[:, 4 * b:4 * b + 4, :]
                evac(j, V_.tensor_tensor(h4, PP[j["pair"]][:, :, :], h4, ALU.add))
            dve.sem_inc(h_ready, 1)
            scale("ffn", hT, uT, RMS_EPS)
            route(1)
            scale("final", hT, uT, RMS_EPS)


def blocks(w, width=512):
    K, N = w.shape
    return np.ascontiguousarray(w.reshape(K // P, P, N // width, width).transpose(2, 1, 0, 3)).reshape(N // width, P, -1)


def tiles(x):
    n = x.shape[-1] // P
    return np.ascontiguousarray(np.moveaxis(x.reshape(-1, n, P), (0, 1, 2), (2, 1, 0)))


def bucket(dist):
    large = 16 + (np.log(np.maximum(dist, 1).astype(np.float32) / np.float32(16)) / np.float32(np.log(8.0)) * np.float32(16)).astype(np.int32)
    return np.where(dist < 16, dist, np.minimum(large, 31))


def constants():
    f = np.float32
    c = np.zeros((P, NC), f)

    def put(name, value):
        value = np.asarray(value, f).reshape(P, -1)
        c[:, CCOLS[name]:CCOLS[name] + value.shape[1]] = value
    p = np.arange(P)
    put("ident", np.eye(P))
    put("ones", np.full((P, P), 1.0 / D))
    rot = np.zeros((P, P))
    rot[p[64:], p[:64]] = -1.0
    rot[p[:64], p[64:]] = 1.0
    put("rot", rot)
    pos = np.arange(L)
    inv = (f(10000.0) ** (-np.arange(32, dtype=f) / f(32))).astype(f)
    ang = np.concatenate([(pos // 64).astype(f)[:, None] * inv, (pos % 64).astype(f)[:, None] * inv], axis=1).astype(f)
    ang = np.concatenate([ang, ang], axis=1)
    put("cos", np.cos(ang).T)
    put("sin", np.sin(ang).T)
    m = p[:, None, None] + P * np.arange(LT)[None, :, None]
    n = pos[None, None, :]
    put("dpos", np.maximum(n - m, 0))
    put("dneg", np.maximum(m - n, 0))
    put("ln2", (m == n) * np.log(2.0))
    put("nfb", np.broadcast_to(np.concatenate([pos + 1, L - pos]), (P, 2 * L)))
    put("mctx", np.stack([L - 1 - m[:, :, 0], m[:, :, 0]], axis=2))
    put("causal", p[:, None] <= p[None, :])
    put("iota", np.broadcast_to(np.arange(16) + 64, (P, 16)))
    put("tri", (p[:, None] < p[None, :]) / D)
    put("pcol", p)
    put("slot", np.concatenate([np.broadcast_to(np.arange(SLOTS), (P, SLOTS)), (p % SLOTS - 2 * SLOTS)[:, None]], axis=1))
    return c


def layout(i):
    i = {k: np.asarray(v) for k, v in i.items()}
    d = {}
    w_in, b_in = i["w_in"][0], i["b_in"][0]
    cut = np.cumsum([0, 1024, 1024, 2048, 2048, 1024, 1024, 2048])
    q, k, v, g, za, zb, gates = (slice(cut[n], cut[n + 1]) for n in range(7))
    d["w_ada"] = blocks(i["w_ada"][0])
    d["w_q"], d["w_k"], d["w_v"], d["w_g"], d["w_gates"] = (blocks(w_in[:, s]) for s in (q, k, v, g, gates))
    d["w_glu"] = blocks(np.stack([w_in[:, za].reshape(D, 4, 256), w_in[:, zb].reshape(D, 4, 256)], axis=2).reshape(D, 2 * D))
    d["w_ret"] = blocks(i["w_ret_out"][0], 256)
    d["w_cout"], d["w_mix"] = blocks(i["w_conv_out"][0]), blocks(i["w_mix_out"][0])
    vecs = [i["b_ada"][0], b_in[q], b_in[k], b_in[za], b_in[zb], b_in[gates], i["conv_dw_b"][0], i["conv_ln_g"][0],
            i["conv_ln_b"][0], i["b_conv_out"][0], i["b_mix_out"][0], i["ln1_g"][0], i["ln1_b"][0], i["ln2_g"][0],
            i["ln2_b"][0], i["attn_norm_g_2"][0], i["ffn_norm_g_2"][0], i["final_norm_g_2"]]
    taps = i["conv_dw"][0].reshape(TAPS, DT, P).transpose(2, 1, 0).reshape(P, -1)
    d["vec"] = np.concatenate([tiles(x)[:, :, 0] for x in vecs] + [taps], axis=1)
    d["rows"] = np.concatenate([i["ret_decay_fwd"][0], i["ret_decay_bwd"][0], i["b_router_grp"][0], i["b_router_exp"][0],
                                i["router_group_b_2"][0], i["router_expert_b_2"][0].ravel(), i["attn_sinks_2"][0],
                                i["gm_v_norm_g_2"][0]])[None]
    d["bias_rows"] = np.concatenate([b_in[k], b_in[v], b_in[g]])[None]
    d["wr0"] = np.concatenate([i["w_router_grp"][0], i["w_router_exp"][0]], axis=1).reshape(DT, P, 36).transpose(1, 0, 2)
    d["wr1"] = np.concatenate([i["router_group_w_2"][0], i["router_expert_w_2"][0].transpose(1, 0, 2).reshape(D, 16)],
                              axis=1).reshape(DT, P, 20).transpose(1, 0, 2)
    d["xT"], d["ctxT"] = tiles(i["x"][0]), tiles(i["ctx"][0])
    d["cT"] = np.concatenate([tiles(i["c"]), tiles(i["c_ctx"][None])], axis=2)
    for n, (x, y, z) in enumerate((("w_exp_gate", "w_exp_up", "w_exp_down"), ("expert_w_gate_2", "expert_w_up_2", "expert_w_down_2"))):
        E = EXPERTS[n]
        s = np.empty((E, 3, P, BLK), np.float32)
        s[:, 0] = i[x][0].reshape(E, DT, P, 512).transpose(0, 2, 1, 3).reshape(E, P, BLK)
        s[:, 1] = i[y][0].reshape(E, DT, P, 512).transpose(0, 2, 1, 3).reshape(E, P, BLK)
        s[:, 2] = i[z][0].reshape(E, 4, P, D).transpose(0, 2, 1, 3).reshape(E, P, BLK)
        d[f"w_moe{n}"] = s.reshape(3 * E, P, BLK)
    w2 = i["w_in_2"][0]
    d["w_u2"], d["w_v2"] = blocks(w2[:, 0:512]), blocks(w2[:, 512:1024])
    d["w_q2"] = blocks(w2[:, 1024:1536].reshape(D, 2, 4, HD).transpose(0, 2, 1, 3).reshape(D, 512))
    d["w_kv2"] = blocks(w2[:, 1536:1792], 256)
    d["w_gates2"] = blocks(w2[:, 1792:3840])
    d["w_pa"], d["w_pb"] = blocks(i["w_proj_a_2"][0], 1024), blocks(i["w_proj_b_2"][0], 1024)
    d["w_out2"] = blocks(i["w_out_2"][0])
    d["ws"] = i["gm_w_spatial_2"][0].transpose(2, 0, 1)
    d["gm_b"] = i["gm_b_spatial_2"][0].reshape(1, -1)
    d["const"] = constants()
    dist = 255 - np.arange(384)
    ok = (dist >= 0) & (dist < P)
    hot = np.zeros((32, 384), np.float32)
    hot[bucket(dist[ok]), np.arange(384)[ok]] = 1.0
    d["hot"] = hot
    d["outside"] = np.broadcast_to(np.where(ok, 0.0, MASKED).astype(np.float32), (QH, 384))
    d["rel"] = i["rel_bias_2"]
    return {k: np.ascontiguousarray(v) for k, v in d.items()}


def kernel(**inputs):
    import concourse.bacc as bacc
    from concourse.bass_utils import run_bass_kernel_spmd

    nc = bacc.Bacc("TRN2", target_bir_lowering=False, num_devices=1)
    arrays = layout(inputs)
    a = {n: nc.dram_tensor(f"in_{n}", x.shape, mybir.dt.from_np(x.dtype), kind="ExternalInput").ap() for n, x in arrays.items()}
    a["out"] = nc.dram_tensor("out", (P, DT, L), F32, kind="ExternalOutput").ap()
    build(nc, a)
    r = run_bass_kernel_spmd(nc, [{f"in_{n}": x for n, x in arrays.items()}], core_ids=[0])
    out = r.results[0]["out"]
    return np.ascontiguousarray(out.transpose(2, 1, 0)).reshape(1, L, D)
```

```python
from contextlib import ExitStack

import numpy as np

import concourse.bass as bass
from concourse import mybir

F32 = mybir.dt.float32
ALU = mybir.AluOpType
ACT = mybir.ActivationFunctionType
AX = mybir.AxisListType

P = 128
D = 1024
L = 256
DT = D // P
LT = L // P
HEADS, DV = 8, 256
TAPS = 31
HALO = TAPS // 2
RING = 3
BLK = 4096
LN_EPS, RMS_EPS = 1e-5, 1e-6
A_JOB = 16
KSCALE = 128 ** -0.5
ALPHA = 2.0 ** 0.25
GROUPS = 4
EXPERTS = (32, 16)
MEAN_WAIT, SQUARE_WAIT, GAIN_WAIT, ATTN_WAIT = 7, 9, 24, 24
MEAN = ("conv", "ln1", "ln2")
SLOTS = 64
QH, HD = 8, 64
MASKED = -1e30


def columns(*parts):
    at, out = 0, {}
    for name, n in parts:
        out[name] = at
        at += n
    return out, at


VCOLS, NV = columns(("b_ada", 48), ("b_q", 8), ("b_k", 8), ("b_za", 8), ("b_zb", 8), ("b_gates", 16),
                    ("conv_b", 8), ("conv_g", 8), ("conv_lb", 8), ("b_conv", 8), ("b_mix", 8), ("ln1_g", 8),
                    ("ln1_b", 8), ("ln2_g", 8), ("ln2_b", 8), ("attn_g", 8), ("ffn_g", 8), ("final_g", 8),
                    ("taps", 8 * TAPS))
RCOLS, NR = columns(("decay", 16), ("rb0", 36), ("rb1", 20), ("sinks", 8), ("gm_g", 512))
CCOLS, NC = columns(("ident", 128), ("ones", 128), ("rot", 128), ("pick", 2), ("cos", 256), ("sin", 256), ("dpos", 512),
                    ("dneg", 512), ("ln2", 512), ("nfb", 512), ("mctx", 4), ("causal", 128), ("tri", 128), ("pcol", 1),
                    ("slot", 65), ("eps", 2))


def make_jobs():
    jobs, srcs = [], []
    for src, n, kinds in (("ada", 4, ["ada"]), ("glu", 4, ["cm8"]), ("k", 2, ["cm8", "tm8c"]),
                          ("q", 2, ["cm8"]), ("v", 4, ["tm8", "tm8c"]), ("ada", 8, ["ada"]), ("g", 4, ["tm8"]), ("gates", 4, ["cm8"]),
                          ("ret", 4, ["cm16"]), ("cout", 2, ["cm8"]), ("mix", 2, ["cm8"]),
                          ("u2", 1, ["cm8"]), ("v2", 1, ["tm8"]), ("q2", 1, ["cm8"]), ("kv2", 1, ["kv"]),
                          ("gates2", 4, ["cm8"]), ("pa", 1, ["cm4", "cm4"]), ("pb", 1, ["cm4", "cm4"]),
                          ("out2", 2, ["cm8"])):
        first = sum(x[0] == src for x in srcs)
        for b in range(first, first + n):
            for half, kind in enumerate(kinds):
                i = len(jobs)
                jobs.append(dict(src=src, b=b, kind=kind, half=half, w=len(srcs), i=i, pair=i % 2, use=i // 2))
            srcs.append((src, b))
    last_of = {j["w"]: j["i"] for j in jobs}
    return jobs, {(j["src"], j["b"], j["half"]): j for j in jobs}, srcs, last_of


def build(nc, a):
    jobs, J, srcs, last_of = make_jobs()
    moe_w = [srcs.index(("u2", 0)), len(srcs)]
    with ExitStack() as ctx:
        def sb(name, shape):
            return ctx.enter_context(nc.sbuf_tensor(name, shape, F32))

        def sem(name):
            return ctx.enter_context(nc.semaphore(name))

        ring = sb("ring", [P, RING, BLK])
        const = sb("const", [P, NC])
        vec = sb("vec", [P, NV])
        row = sb("row", [P, NR])
        wr = [sb("wr0", [P, DT, 36]), sb("wr1", [P, DT, 20])]
        hT = sb("hT", [P, DT, L])
        uT = sb("uT", [P, DT, L])
        RA = sb("RA", [P, 2 * DT, L])
        kT = sb("kT", [P, DT, L])
        qT = sb("qT", [P, DT, L])
        Kc = sb("Kc", [P, DT, L])
        Vc = sb("Vc", [P, 2 * DT, L])
        V = sb("V", [P, 2 * DT, L])
        biasr = sb("biasr", [P, 2, 512])
        zpad = sb("zpad", [P, DT, L + 2 * HALO])
        conv = sb("conv", [P, DT, L])
        raw = sb("raw", [P, 4, L])
        Eqd = sb("Eqd", [P, 4, L])
        qd = sb("qd", [P, 4, L])
        Ddec = sb("Ddec", [P, 4, L])
        kw = sb("kw", [P, 4, L])
        S0s = sb("S0s", [P, 4, L])
        Ph = sb("Ph", [P, 4, L])
        table = sb("table", [P, P])
        modT = sb("modT", [P, 2, 48])
        fold = sb("fold", [P, 5, DT])
        sT = sb("sT", [P, DT, 32])
        cin = sb("cin", [P, DT, 2])
        lgs = sb("lgs", [P, 6, 16])
        wctx = sb("wctx", [P, LT, 2, 8])
        mv = sb("mv", [P, LT, HEADS, 2])
        rstd = sb("rstd", [P, LT * HEADS])
        bst = sb("bst", [P, LT, 6])
        rs = sb("rs", [P, L])
        rt = biasr[:, :, :].rearrange("p a n -> p (a n)")

        def flat(t):
            return t[:, :, :].rearrange("p a n -> p (a n)")
        xg = flat(raw)[:, 0:512]
        xts = flat(qd)[:, 0:512].rearrange("p (c m) -> p c m", c=4)
        hid, sg = qd[:, 2, :], Eqd[:, 0, :]
        hts = qd[:, 3, :].rearrange("p (c m) -> p c m", c=2)
        mw = flat(V)
        ys, S = mw[:, 0:512], mw[:, 512:768]
        Sk = mw[:, 768:1280].rearrange("p (k n) -> p k n", k=2)
        placer = mw[:, 1280:1792].rearrange("p (k n) -> p k n", k=2)
        weightr = mw[:, 1792:2304].rearrange("p (k n) -> p k n", k=2)
        diag = mw[:, 2304:3328].rearrange("p (v q n) -> p v q n", v=2, q=4)
        Ek = mw[:, 3328:3584].rearrange("p (q n) -> p q n", q=4)
        G = mw[:, 3584:3712].rearrange("p (t n) -> p t n", t=LT)
        slotno = mw[:, 3712:3777]
        lgT = mw[:, 3780:4036]
        hot, rel = flat(Vc)[0:32, 0:384], flat(Vc)[0:32, 512:512 + QH]
        outside, relb = flat(Vc)[0:QH, 1024:1408], flat(Vc)[0:QH, 1536:1920]
        pT = flat(zpad)
        gu, aT, bT = conv[:, 0:4, :], conv[:, 4:8, :], Eqd
        q2, k2, v2 = RA[:, 0:4, :], RA[:, 4, :], RA[:, 5, :]
        ws = flat(S0s).rearrange("p (g t) -> p g t", g=8)
        warm = table[:, P - 1:P]
        tab = table[:, :].bitcast(mybir.dt.int32)
        ctxT, ucT = RA[:, 0:DT], RA[:, DT:2 * DT]
        Kct = flat(Kc).rearrange("p (a n) -> p a n", a=LT)
        Vct = flat(Vc).rearrange("p (a n) -> p a n", a=LT)
        Vt = flat(V).rearrange("p (a n) -> p a n", a=LT)
        On = flat(RA).rearrange("p (a n) -> p a n", a=LT)
        adaR = flat(raw).rearrange("p (a n) -> p a n", a=2)
        retT, gT, mT, SQ = Vc, V, kT, qT
        raw2 = flat(raw).rearrange("p (a n) -> p a n", a=LT)
        PP = [ctx.enter_context(nc.psum_tensor(f"PP{i}", [P, 4, L], F32)) for i in range(2)]
        MB = [ctx.enter_context(nc.psum_tensor(f"MB{i}", [P, 2, L], F32)) for i in range(4)]
        bank = [flat(PP[i // 2])[:, 512 * (i % 2):512 * (i % 2 + 1)] for i in range(4)]
        PPt = [p[:, :, :].rearrange("p a n -> p (a n)").rearrange("p (a n) -> p a n", a=LT) for p in PP]

        relb_d = nc.dram_tensor("relb_d", [QH, P, 384], F32, kind="Internal")

        RT, end = columns(("lt", 72), ("gd", 8), ("e2", 2), ("gm", 2), ("gw", 2), ("cm", 2), ("eq", 16), ("c", 16), ("hg", 8),
                        ("ml", 16), ("m1", 2), ("m2", 2), ("h1", 16), ("h2", 16), ("w1", 2), ("w2", 2), ("tmp", 64),
                        ("A1", 64), ("A2", 64), ("M", 64), ("rank", 64), ("Sa", 96), ("Sb", 96),
                        ("vx", 64), ("item", 1), ("pos", 4), ("mx", 8), ("sk", 8), ("den", 8))
        assert end <= 1024
        widths = dict(zip(list(RT), [b - c for c, b in zip(list(RT.values()), list(RT.values())[1:] + [end])]))

        def r_(name):
            return rt[:, RT[name]:RT[name] + widths[name]]

        def cst(name, n):
            return const[:, CCOLS[name]:CCOLS[name] + n]

        def col(name, t):
            return vec[:, VCOLS[name] + t:VCOLS[name] + t + 1]

        def rowc(name, n):
            return row[:, RCOLS[name]:RCOLS[name] + n]
        ident, ones, rotm = cst("ident", P), cst("ones", P), cst("rot", P)
        lg = lgs[:, 5, :]

        ld_c, ld_first, ld_rest, ld_x, ld_ctx, ld_wr = (sem(n) for n in ("ld_c", "ld_first", "ld_rest", "ld_x", "ld_ctx", "ld_wr"))
        w_full = [sem(f"w_full{i}") for i in range(RING)]
        job_done = sem("job_done")
        pair_free = [sem("pair_free0"), sem("pair_free1")]
        dve_own, act_own = sem("dve_own"), sem("act_own")
        zeroed, silu_c, ada_kept, ada_turned, u_mod, u_ready, u_second = (sem(n) for n in (
            "zeroed", "silu_c", "ada_kept", "ada_turned", "u_mod", "u_ready", "u_second"))
        lg_abs, lg_exp, lg_ready, wctx_exp = (sem(n) for n in ("lg_abs", "lg_exp", "lg_ready", "wctx_exp"))
        sig_ready, raw_rot, rope_done = sem("sig_ready"), sem("raw_rot"), sem("rope_done")
        bias_full = [sem("bias_full0"), sem("bias_full1")]
        dec_arg, dec_ready, eq_ready, k_decayed, q_decayed, s0_ps, sc_ps, s0_sb, p_sb, o_ps, o_kept, o_stat = (sem(n) for n in (
            "dec_arg", "dec_ready", "eq_ready", "k_decayed", "q_decayed", "s0_ps", "sc_ps", "s0_sb", "p_sb", "o_ps", "o_kept", "o_stat"))
        var_ready, std_ready, g_silu, ret_ready, ret_turned, ret_kept = (sem(n) for n in (
            "var_ready", "std_ready", "g_silu", "ret_ready", "ret_turned", "ret_kept"))
        mix_in, h_scaled = sem("mix_in"), sem("h_scaled")
        LN = {k: sem(f"ln_{k}") for k in ("in", "mean", "centred", "squared", "summed", "rooted", "divided", "out_a", "out_v")}
        STEPS = {"in": 2, "mean": 1, "centred": 2, "squared": 2, "summed": 1, "rooted": 1, "divided": 2, "out_a": 1, "out_v": 1}
        LN_BASE, done = {}, dict.fromkeys(STEPS, 0)
        for name in ("conv", "ln1", "ln2", "attn", "ffn", "final"):
            LN_BASE[name] = dict(done)
            for k, steps in STEPS.items():
                if (k not in ("mean", "centred") or name in MEAN) and (k, name) != ("in", "attn"):
                    done[k] += steps

        def ln_wait(eng, name, step, value):
            eng.wait_ge(LN[step], LN_BASE[name][step] + value)

        out_done = sem("out_done")
        moe = []
        for n in range(2):
            moe.append({k: sem(f"{k}{n}") for k in (
                "logits", "logits_kept", "logits_turned", "gexp_in", "eexp_in", "gexp_out", "eexp_out", "hot_ready", "ranks", "items_in",
                "items_ps", "items_ready", "u_turned", "u_rows", "diag_ready", "bc_ps", "bc_kept", "wg_full", "wu_full",
                "wd_full", "g_ready", "gathered", "xg_kept", "xt_ps", "xts_ready", "gate_done", "up_done", "down_done",
                "sg_ready", "hid_ready", "ht_ps", "ht_ready", "y_kept", "s_ready", "scattered", "acc_done", "step")})
        b2 = {k: sem(f"b2_{k}") for k in ("ld", "relb_ps", "relb_sb", "relb_dram", "relb_full", "vvar",
                                          "vstd", "v_ready", "ws_ready", "sp_ps", "a_ready",
                                          "sc_ps", "sc_sb", "p_exp", "p_ready", "p_turned", "p_kept", "b_ps", "b_ready",
                                          "m_ready")}

        def out_wait(eng, name):
            ln_wait(eng, name, "out_a", 1)
            ln_wait(eng, name, "out_v", 1)

        def half_in(eng, name, half):
            if name == "attn":
                ln_wait(eng, "ln2", ("out_a", "out_v")[half], 1)
            else:
                ln_wait(eng, name, "in", half + 1)

        def ln_say(eng, ins, name, step, value):
            ins.then_inc(LN[step], 1)
            ln_wait(eng, name, step, value)

        def w_wait(eng, w):
            eng.wait_ge(w_full[w % RING], 16 * (w // RING + 1))

        def job_wait(eng, j):
            eng.wait_ge(job_done, j["i"] + 1)

        class Own:

            def __init__(self, eng, sem_):
                self.eng, self.sem, self.n = eng, sem_, 0

            def link(self, ins):
                self.n += 1
                ins.then_inc(self.sem, 1)
                self.eng.wait_ge(self.sem, self.n)

        def say(eng, ins, sem_, value):
            ins.then_inc(sem_, 1)
            eng.wait_ge(sem_, value)

        block = ctx.enter_context(nc.Block())

        @block.sync
        def _(sp):
            def load(w):
                src, b = srcs[w]
                if w >= RING and not moe_w[0] <= w < moe_w[0] + RING:
                    sp.wait_ge(job_done, last_of[w - RING] + 1)
                s = a["w_" + src]
                sp.dma_start(ring[:, w % RING, 0:s.shape[2]], s[b]).then_inc(w_full[w % RING], 16)

            def experts(n):
                m, s = moe[n], a[f"w_moe{n}"]
                part = (("wg_full", "gate_done"), ("wu_full", "up_done"), ("wd_full", "down_done"))
                for q in range(3):
                    sp.wait_ge(job_done, last_of[max(w for w in range(moe_w[n]) if w % RING == q)] + 1)
                    sp.dma_start(ring[:, q, :], s[q]).then_inc(m[part[q][0]], 16)
                sp.wait_ge(m["items_ready"], 1)
                T = sp.value_load(tab[0:1, 64:65], min_val=EXPERTS[n], max_val=EXPERTS[n] + 8)
                with sp.Fori(1, T) as i:
                    e = sp.value_load(tab[0:1, bass.ds(i, 1)], min_val=0, max_val=EXPERTS[n] - 1)
                    for q in range(3):
                        sp.wait_ge(m[part[q][1]], i)
                        sp.dma_start(ring[:, q, :], s[bass.ds(3 * e + q, 1)].rearrange("a p n -> p (a n)")
                                     ).then_inc(m[part[q][0]], 16)
                return [(m[x[1]], T) for x in part]

            for w in range(moe_w[0]):
                load(w)
            used = experts(0)
            for w in range(moe_w[0], moe_w[1]):
                if w < moe_w[0] + RING:
                    sp.wait_ge(*used[w % RING])
                load(w)
            experts(1)
            for half, out in enumerate(("out_a", "out_v")):
                ln_wait(sp, "final", out, 1)
                sp.dma_start(a["out"][:, 4 * half:4 * half + 4], uT[:, 4 * half:4 * half + 4, :]).then_inc(out_done, 16)
            sp.wait_ge(out_done, 32)

        @block.gpsimd
        def _(pool):
            nc.gpsimd.memset(sT[:, :, :], 0.0).then_inc(zeroed, 1)
            nc.gpsimd.memset(zpad[:, :, 0:HALO], 0.0).then_inc(zeroed, 1)
            nc.gpsimd.memset(zpad[:, :, L + HALO:L + 2 * HALO], 0.0).then_inc(zeroed, 1)
            for n in range(10):
                if n >= 2:
                    src, b = (("k", n - 2), ("v", n - 4), ("v", n - 4), ("g", n - 8))[min((n - 2) // 2, 3)]
                    j = J[src, b, 0 if src == "g" else 1]
                    pool.wait_ge(pair_free[j["pair"]], j["use"] + 1)
                pool.dma_start(biasr[:, n % 2, :], a["bias_rows"][:, n * 512:(n + 1) * 512].partition_broadcast(P)
                               ).then_inc(bias_full[n % 2], 16)
            pool.wait_ge(moe[0]["logits"], 1)
            pool.dma_start(flat(S0s), a["ws"].rearrange("s g t -> s (g t)")).then_inc(b2["ld"], 16)
            for g in range(8):
                pool.dma_start(flat(Ph)[64 * (g % 2):64 * (g % 2) + 64, (g // 2) * P:(g // 2 + 1) * P],
                               a["gm_b"][:, g * P:(g + 1) * P].partition_broadcast(64)).then_inc(b2["ld"], 16)
            pool.dma_start(hot, a["hot"]).then_inc(b2["ld"], 16)
            pool.dma_start(rel, a["rel"]).then_inc(b2["ld"], 16)
            pool.dma_start(outside, a["outside"]).then_inc(b2["ld"], 16)
            pool.wait_ge(b2["relb_dram"], 16)
            for h in range(QH):
                pool.dma_start(RA[:, DT + h, :], bass.AP(tensor=relb_d, offset=h * P * 384 + 127, ap=[[383, P], [1, L]])
                               ).then_inc(b2["relb_full"], 16)

        @block.scalar
        def _(act):
            own = Own(act, act_own)
            act.dma_start(cin[:, :, :], a["cT"]).then_inc(ld_c, 16)
            early = CCOLS["cos"]
            act.dma_start(const[:, 0:early], a["const"][:, 0:early]).then_inc(ld_first, 16)
            act.dma_start(vec[:, :], a["vec"]).then_inc(ld_first, 16)
            act.dma_start(hT[:, :, :], a["xT"]).then_inc(ld_x, 16)
            act.wait_ge(ld_c, 16)
            act.wait_ge(zeroed, 1)
            nc.scalar.activation(sT[:, :, 0:2], cin[:, :, :], ACT.Silu).then_inc(silu_c, 1)
            job_wait(act, J["ada", 1, 0])
            act.dma_start(const[:, early:], a["const"][:, early:]).then_inc(ld_rest, 16)
            act.dma_start(row[:, :], a["rows"].partition_broadcast(P)).then_inc(ld_rest, 16)
            act.dma_start(ctxT, a["ctxT"]).then_inc(ld_ctx, 16)
            act.dma_start(wr[0][:, :, :], a["wr0"]).then_inc(ld_wr, 16)
            act.dma_start(wr[1][:, :, :], a["wr1"]).then_inc(ld_wr, 16)

            def modulate(r, tiles, src, dst):
                for t in tiles:
                    ins = nc.scalar.activation(dst[:, t, :], src[:, t, :], ACT.Identity, bias=modT[:, r, t:t + 1],
                                               scale=modT[:, r, 8 + t:9 + t])
                ins.then_inc(u_ready, 1)
            act.wait_ge(u_mod, 1)
            act.wait_ge(ld_x, 16)
            modulate(0, range(4), hT, uT)
            act.wait_ge(lg_abs, 1)
            nc.scalar.activation(lgs[:, 1, :], lgs[:, 0, :], ACT.Exp, scale=-1.0).then_inc(lg_exp, 1)
            act.wait_ge(lg_ready, 1)
            nc.scalar.activation(wctx[:, :, :, :], wctx[:, :, :, :], ACT.Exp).then_inc(wctx_exp, 1)
            act.wait_ge(ld_ctx, 16)
            modulate(1, range(DT), ctxT, ucT)
            for b in range(4):
                j = J["glu", b, 0]
                job_wait(act, j)
                for i in range(2):
                    ins = nc.scalar.activation(raw[:, 2 * (b % 2) + i, :], PP[j["pair"]][:, 2 + i, :], ACT.Sigmoid,
                                               bias=col("b_zb", 2 * b + i))
                ins.then_inc(sig_ready, 1)

            def raw_copy(r, src, b, bias):
                j = J[src, b, 0]
                job_wait(act, j)
                if r:
                    act.wait_ge(rope_done, r)
                else:
                    act.wait_ge(pair_free[1], J["glu", 3, 0]["use"] + 1)
                for i in range(4):
                    ins = nc.scalar.activation(raw[:, i, :], PP[j["pair"]][:, i, :], ACT.Identity,
                                               bias=col(bias, 4 * b + i))
                ins.then_inc(pair_free[j["pair"]], 1)
            for r, (src, b, bias) in enumerate((("k", 0, "b_k"), ("k", 1, "b_k"), ("q", 0, "b_q"), ("q", 1, "b_q"))):
                raw_copy(r, src, b, bias)
            nfb = cst("nfb", 512)

            def decays(h):
                act.wait_ge(dec_arg, h + 1)
                dd = Ddec[:, 2 * (h % 2):2 * (h % 2) + 2, :]
                nc.scalar.activation(dd, dd, ACT.Exp).then_inc(dec_ready, 1)

            def q_exps(h):
                if h >= 2:
                    act.wait_ge(q_decayed, h - 1)
                else:
                    act.wait_ge(rope_done, 4)
                for d in range(2):
                    ins = nc.scalar.activation(Eqd[:, 2 * (h % 2) + d, :], nfb[:, d * L:(d + 1) * L], ACT.Exp,
                                               scale=lg[:, 8 * d + h:8 * d + h + 1])
                ins.then_inc(eq_ready, 1)

            def s0_copy(h):
                act.wait_ge(s0_ps, h + 1)
                if h >= 2:
                    act.wait_ge(o_ps, h - 1)
                nc.scalar.activation(S0s[:, 2 * (h % 2):2 * (h % 2) + 2, :], MB[0][:, :, :], ACT.Copy).then_inc(s0_sb, 1)

            def o_copy(h):
                act.wait_ge(o_ps, h + 1)
                nc.scalar.activation(On[:, :, h * DV:(h + 1) * DV], MB[2 + h % 2][:, :, :], ACT.Copy).then_inc(o_kept, 1)
            for h in range(2):
                q_exps(h)
                decays(h)
            for h in range(HEADS):
                s0_copy(h)
                if h:
                    o_copy(h - 1)
                if h + 2 < HEADS:
                    decays(h + 2)
                    q_exps(h + 2)
            o_copy(HEADS - 1)
            act.wait_ge(var_ready, 1)
            nc.scalar.activation(rstd[:, :], rstd[:, :], ACT.Sqrt).then_inc(std_ready, 1)

            def turned_copy(b):
                act.wait_ge(ret_turned, b + 1)
                for q in range(2):
                    ins = nc.scalar.activation(retT[:, 4 * b + 2 * q:4 * b + 2 * q + 2, :], MB[2 * (b % 2) + q][:, :, :],
                                               ACT.Copy)
                ins.then_inc(ret_kept, 1)
            for b in range(4):
                j = J["g", b, 0]
                act.wait_ge(pair_free[j["pair"]], j["use"] + 1)
                nc.scalar.activation(raw[:, :, :], raw[:, :, :], ACT.Silu).then_inc(g_silu, 1)
                if b:
                    turned_copy(b - 1)
            turned_copy(3)
            for b in range(4):
                j = J["gates", b, 0]
                job_wait(act, j)
                for i in range(4):
                    ins = nc.scalar.activation(gT[:, 4 * b + i, :], PP[j["pair"]][:, i, :], ACT.Sigmoid,
                                               bias=col("b_gates", 4 * b + i))
                ins.then_inc(pair_free[j["pair"]], 1)

            def squares(name, src):
                eps = 0 if name in MEAN else 1
                for half in range(2):
                    if name in MEAN:
                        ln_wait(act, name, "centred", half + 1)
                    else:
                        half_in(act, name, half)
                    h = slice(4 * half, 4 * half + 4)
                    nc.scalar.activation(SQ[:, h, :], src[:, h, :], ACT.Square).then_inc(LN["squared"], 1)
                nc.scalar.activation(warm, cst("eps", 1), ACT.Sqrt)
                ln_wait(act, name, "summed", 1)
                nc.scalar.activation(rs[:, :], MB[1][:, 0, :], ACT.Sqrt, bias=cst("eps", 2)[:, eps:eps + 1]).then_inc(LN["rooted"], 1)

            def gains(name, dst, scale, bias):
                ln_wait(act, name, "divided", 1)
                for t in range(4):
                    ins = nc.scalar.activation(dst[:, t, :], dst[:, t, :], ACT.Identity, scale=scale(t), bias=bias(t))
                ln_say(act, ins, name, "out_a", 1)
            squares("conv", conv)
            for half, out in enumerate(("out_a", "out_v")):
                ln_wait(act, "conv", "divided", half + 1)
                for t in range(4 * half, 4 * half + 4):
                    ins = nc.scalar.activation(conv[:, t, :], conv[:, t, :], ACT.Silu, scale=col("conv_g", t), bias=col("conv_lb", t))
                ln_say(act, ins, "conv", out, 1)
            squares("ln1", hT)
            ln_wait(act, "ln1", "divided", 1)
            for t in range(4):
                ins = nc.scalar.activation(uT[:, t, :], hT[:, t, :], ACT.Identity, bias=fold[:, 1, t:t + 1],
                                           scale=fold[:, 0, t:t + 1])
            ins.then_inc(LN["out_a"], 1)

            def route_and_experts(n):
                m = moe[n]
                cols = GROUPS + EXPERTS[n]
                act.wait_ge(m["logits"], 1)
                act.wait_ge(m["y_kept"], 1)
                nc.scalar.activation(lgT[0:cols, :], MB[2][0:cols, 0, :], ACT.Copy).then_inc(m["logits_kept"], 1)
                for t in range(LT):
                    act.wait_ge(m["u_turned"], t + 1)
                    ins = nc.scalar.activation(Kct[:, t, :], flat(PP[t]), ACT.Copy)
                ins.then_inc(m["u_rows"], 1)
                act.wait_ge(m["gexp_in"], 1)
                nc.scalar.activation(r_("gd"), r_("gd"), ACT.Exp).then_inc(m["gexp_out"], 1)
                act.wait_ge(m["eexp_in"], 1)
                nc.scalar.activation(r_("e2"), r_("e2"), ACT.Exp).then_inc(m["eexp_out"], 1)

                def keep(done, value, out, src, ready, **kw):
                    act.wait_ge(m[done], value)
                    nc.scalar.activation(out, src, ACT.Copy, **kw).then_inc(m[ready], 1)

                def keep_rows(value):
                    keep("gathered", value, xg, bank[3], "xg_kept")

                def keep_turned(value):
                    keep("xt_ps", value, xts, bank[0].rearrange("p (c m) -> p c m", c=4), "xts_ready")
                keep_rows(1)
                act.wait_ge(m["bc_ps"], 1)
                nc.scalar.activation(placer, bank[1].rearrange("p (k n) -> p k n", k=2), ACT.Copy, scale=float(D))
                nc.scalar.activation(weightr, bank[2].rearrange("p (k n) -> p k n", k=2), ACT.Copy, scale=float(D)
                                     ).then_inc(m["bc_kept"], 1)
                keep_turned(1)
                act.wait_ge(m["items_ready"], 1)
                T = act.value_load(tab[0:1, 64:65], min_val=EXPERTS[n], max_val=EXPERTS[n] + 8)
                with act.Fori(0, T) as i:
                    act.wait_ge(m["gate_done"], i + 1)
                    act.wait_ge(m["hid_ready"], i + 1)
                    nc.scalar.activation(sg, bank[0][:, 0:L], ACT.Silu).then_inc(m["sg_ready"], 1)
                    keep_rows(i + 2)
                    keep_turned(i + 2)
                    keep("ht_ps", i + 1, hts, bank[1][:, L:2 * L].rearrange("p (c m) -> p c m", c=2), "ht_ready")
            route_and_experts(0)
            squares("ln2", hT)
            gains("ln2", hT, lambda t: col("ln2_g", t), lambda t: col("ln2_b", t))
            squares("attn", hT)
            gains("attn", uT, lambda t: col("attn_g", t), lambda t: 0.0)
            act.wait_ge(b2["relb_sb"], 1)
            act.dma_start(relb_d.ap(), relb[:, None, :].broadcast_to([QH, P, 384])).then_inc(b2["relb_dram"], 16)

            def copy_job(src, out, func, b=0, **kw):
                j = J[src, b, 0]
                job_wait(act, j)
                say(act, nc.scalar.activation(out, PP[j["pair"]][:, :, :], func, **kw), pair_free[j["pair"]], j["use"] + 1)
            copy_job("u2", gu, ACT.Gelu_apprx_tanh)
            copy_job("v2", raw[:, :, :], ACT.Gelu_apprx_tanh)
            copy_job("q2", q2, ACT.Copy)
            act.wait_ge(b2["vvar"], 1)
            nc.scalar.activation(rs[:, 0:2], rs[:, 0:2], ACT.Sqrt).then_inc(b2["vstd"], 1)
            j = J["kv2", 0, 0]
            job_wait(act, j)
            nc.scalar.activation(k2, PP[j["pair"]][:, 0, :], ACT.Copy, scale=HD ** -0.5)
            say(act, nc.scalar.activation(v2, PP[j["pair"]][:, 2, :], ACT.Copy), pair_free[j["pair"]], j["use"] + 1)
            copy_job("gates2", gT[:, 0:4, :], ACT.Sigmoid, 0)
            for qb in range(2):
                act.wait_ge(b2["sc_sb"], qb + 1)
                w0 = 0 if qb else P
                nc.scalar.activation(Kc[:, :, w0:L], Kc[:, :, w0:L], ACT.Exp)
                nc.scalar.activation(r_("sk"), r_("sk"), ACT.Exp).then_inc(b2["p_exp"], 1)
                copy_job("gates2", gT[:, 4 + 8 * qb:8 + 8 * qb, :], ACT.Sigmoid, 1 + 2 * qb)
                act.wait_ge(b2["p_turned"], qb + 1)
                for q in range(4 if qb else 2):
                    ins = nc.scalar.activation(pT[:, q * 512:(q + 1) * 512], flat(MB[q]), ACT.Copy)
                ins.then_inc(b2["p_kept"], 1)
                if not qb:
                    copy_job("gates2", gT[:, 8:12, :], ACT.Sigmoid, 2)
            squares("ffn", hT)
            gains("ffn", uT, lambda t: col("ffn_g", t), lambda t: 0.0)
            route_and_experts(1)
            squares("final", hT)
            gains("final", uT, lambda t: col("final_g", t), lambda t: 0.0)

        @block.tensor
        def _(pe):
            def job(j):
                w_wait(pe, j["w"])
                if j["use"]:
                    pe.wait_ge(pair_free[j["pair"]], j["use"])
                W, out, kind = ring[:, j["w"] % RING, :], PP[j["pair"]], j["kind"]
                if kind == "ada":
                    for k in range(DT):
                        at = 32 * (k % 4)
                        ins = pe.matmul(out[at:at + 32, 0:2, :].rearrange("p a n -> p (a n)"), sT[:, k, :],
                                        W[:, k * 512:(k + 1) * 512], start=k < 4, stop=k >= 4, tile_position=(0, at))
                elif kind in ("cm8", "cm4", "cm16"):
                    K = int(kind[2:])
                    X = {"cm8": {"mix": mT, "cout": conv, "out2": mT}.get(j["src"], uT), "cm16": retT,
                         "cm4": {"pa": conv[:, 4:8], "pb": Eqd}.get(j["src"])}[kind]
                    width = 4096 // K
                    for c in range(2 if K == 16 else 4):
                        at = c * P + (512 * j["half"] if K == 4 else 0)
                        for k in range(K):
                            ins = pe.matmul(out[:, c, :], W[:, k * width + at:k * width + at + P], X[:, k, :],
                                            start=k == 0, stop=k == K - 1)
                elif kind in ("tm8", "tm8c"):
                    X = ucT if kind == "tm8c" else uT
                    for t in range(LT):
                        for k in range(DT):
                            ins = pe.matmul(out[:, 2 * t:2 * t + 2, :].rearrange("p a n -> p (a n)"),
                                            X[:, k, t * P:(t + 1) * P], W[:, k * 512:(k + 1) * 512], start=k == 0,
                                            stop=k == DT - 1)
                elif kind == "kv":
                    for k in range(DT):
                        pe.matmul(out[:, 0, :], W[:, k * 256:k * 256 + P], uT[:, k, :], start=k == 0, stop=k == DT - 1)
                    for t in range(LT):
                        for k in range(DT):
                            ins = pe.matmul(out[:, 2, t * P:(t + 1) * P], uT[:, k, t * P:(t + 1) * P],
                                            W[:, k * 256 + P:(k + 1) * 256], start=k == 0, stop=k == DT - 1)
                ins.then_inc(job_done, 1)

            def turn_ada(b):
                pe.wait_ge(ada_kept, b + 1)
                for c in range(4):
                    ins = pe.matmul(PP[J["ada", b, 0]["pair"]][:, 2, 2 * c:2 * c + 2], adaR[:, b % 2, c * P:(c + 1) * P],
                                    cst("pick", 2), start=True, stop=True)
                ins.then_inc(ada_turned, 1)
            pe.wait_ge(silu_c, 1)
            for b in range(4):
                job(J["ada", b, 0])
                if b == 1:
                    pe.wait_ge(ld_first, 32)
                if b:
                    turn_ada(b - 1)
            turn_ada(3)
            pe.wait_ge(u_ready, 1)
            pe.wait_ge(u_second, 1)
            for b in range(4):
                job(J["glu", b, 0])

            def rotate(r):
                j = J["kq"[r // 2], r % 2, 0]
                pe.wait_ge(pair_free[j["pair"]], j["use"] + 1)
                if r:
                    pe.wait_ge(rope_done, r)
                for q in range(2):
                    ins = pe.matmul(MB[q][:, :, :].rearrange("p a n -> p (a n)"), rotm,
                                    raw[:, 2 * q:2 * q + 2, :].rearrange("p a n -> p (a n)"), start=True, stop=True)
                ins.then_inc(raw_rot, 1)
            for b in range(2):
                job(J["k", b, 0])
                pe.wait_ge(u_ready, 2)
                job(J["k", b, 1])
                rotate(b)
            job(J["q", 0, 0])
            job(J["q", 1, 0])
            rotate(2)
            for b in range(4):
                job(J["v", b, 0])
                if b == 0:
                    rotate(3)
                job(J["v", b, 1])

            def scores(h):
                pe.wait_ge(k_decayed, h + 1)
                if h:
                    pe.wait_ge(s0_sb, h)
                else:
                    pe.wait_ge(rope_done, 4)
                    j = J["v", 3, 1]
                    pe.wait_ge(pair_free[j["pair"]], j["use"] + 1)
                k4 = kw[:, :, :].rearrange("p a n -> p (a n)").rearrange("p (a n) -> p a n", n=P)
                for d in range(2):
                    for m in range(LT):
                        ins = pe.matmul(MB[0][:, d, :], k4[:, 4 * (h % 2) + 2 * d + m, :], Vct[:, m, h * DV:(h + 1) * DV],
                                        start=m == 0, stop=m == LT - 1)
                ins.then_inc(s0_ps, 1)
                if h:
                    pe.wait_ge(p_sb, h)
                for m in range(LT):
                    ins = pe.matmul(MB[1][:, m, :], kT[:, h, m * P:(m + 1) * P], qT[:, h, :], start=True, stop=True)
                ins.then_inc(sc_ps, 1)

            def mix_head(h):
                pe.wait_ge(s0_sb, h + 1)
                pe.wait_ge(p_sb, h + 1)
                pe.wait_ge(q_decayed, h + 1)
                if h >= 2:
                    pe.wait_ge(o_kept, h - 1)
                o, q = MB[2 + h % 2], 2 * (h % 2)
                for t in range(LT):
                    for m in range(LT):
                        pe.matmul(o[:, t, :], Ph[:, q + m, t * P:(t + 1) * P], Vt[:, m, h * DV:(h + 1) * DV],
                                  start=m == 0, stop=False)
                    for d in range(2):
                        ins = pe.matmul(o[:, t, :], qd[:, q + d, t * P:(t + 1) * P], S0s[:, q + d, :], start=False,
                                        stop=d == 1)
                ins.then_inc(o_ps, 1)
            scores(0)
            for h in range(HEADS):
                if h + 1 < HEADS:
                    scores(h + 1)
                job(J["ada", 4 + h, 0])
                mix_head(h)
                turn_ada(4 + h)

            def turn_ret(b):
                pe.wait_ge(ret_ready, b + 1)
                if b >= 2:
                    pe.wait_ge(ret_kept, b - 1)
                for i in range(4):
                    for t in range(LT):
                        ins = pe.transpose(MB[2 * (b % 2) + i // 2][:, i % 2, t * P:(t + 1) * P],
                                           On[:, t, b * 512 + i * P:b * 512 + (i + 1) * P], ident)
                ins.then_inc(ret_turned, 1)
            for b in range(4):
                job(J["g", b, 0])
                if b:
                    turn_ret(b - 1)
            job(J["gates", 0, 0])
            turn_ret(3)
            for b in range(1, 4):
                job(J["gates", b, 0])

            def keep_clock(n, spare):
                for _ in range(n):
                    pe.matmul(spare[:, 0:P], ident, ones, start=True, stop=True)

            SPARE = {"ln1": flat(MB[3]), "ffn": flat(MB[3]), "ln2": bank[0], "attn": bank[0], "final": bank[0]}

            def mean_sums(name, src):
                if name != "conv":
                    keep_clock(MEAN_WAIT, SPARE[name])
                for k in range(DT):
                    if k % 4 == 0:
                        half_in(pe, name, k // 4)
                    ins = pe.matmul(MB[0][:, 0, :], ones, src[:, k, :], start=k == 0, stop=k == DT - 1)
                ins.then_inc(LN["mean"], 1)

            def square_sums(name):
                if name != "conv":
                    keep_clock({"attn": ATTN_WAIT}.get(name, SQUARE_WAIT), SPARE[name])
                for k in range(DT):
                    if k % 4 == 0:
                        ln_wait(pe, name, "squared", k // 4 + 1)
                    ins = pe.matmul(MB[1][:, 0, :], ones, SQ[:, k, :], start=k == 0, stop=k == DT - 1)
                ins.then_inc(LN["summed"], 1)
            pe.wait_ge(ret_kept, 4)
            mean_sums("conv", conv)
            job(J["ret", 0, 0])
            job(J["ret", 1, 0])
            square_sums("conv")
            job(J["ret", 2, 0])
            job(J["ret", 3, 0])
            out_wait(pe, "conv")
            for b in range(2):
                job(J["cout", b, 0])
            pe.wait_ge(mix_in, 2)
            for b in range(2):
                job(J["mix", b, 0])
            mean_sums("ln1", hT)
            square_sums("ln1")

            def route_and_experts(n):
                m, E = moe[n], EXPERTS[n]
                cols = GROUPS + E
                keep_clock(GAIN_WAIT, flat(MB[3]))
                pe.wait_ge(ld_wr, 32)
                for k in range(DT):
                    if k % 4 == 0:
                        ln_wait(pe, ("ln1", "ffn")[n], ("out_a", "out_v")[k // 4], 1)
                    at = 64 * (k % 2)
                    ins = pe.matmul(MB[2][at:at + cols, 0, :], wr[n][:, k, :], uT[:, k, :], start=k < 2, stop=k >= DT - 2,
                                    tile_position=(0, at))
                ins.then_inc(m["logits"], 1)

                def turn_u(t):
                    pe.wait_ge(pair_free[t], J_uses[n][t])
                    for k in range(DT):
                        ins = pe.transpose(flat(PP[t])[:, k * P:(k + 1) * P], uT[:, k, t * P:(t + 1) * P], ident)
                    ins.then_inc(m["u_turned"], 1)
                pe.wait_ge(m["logits_kept"], 2)
                for t in range(LT):
                    ins = pe.transpose(MB[2][:, 1, t * P:(t + 1) * P], lgT[:, t * P:(t + 1) * P], ident)
                ins.then_inc(m["logits_turned"], 1)
                turn_u(0)
                turn_u(1)
                keep_clock(14, flat(MB[0]))
                pe.wait_ge(m["hot_ready"], 1)
                M, tri = r_("M"), cst("tri", P)
                pe.matmul(MB[3][:, 0, 0:E], tri, M[:, 0:E], start=True, stop=True)
                pe.matmul(MB[3][:, 0, E:2 * E], tri, M[:, E:2 * E], start=True, stop=False)
                pe.matmul(MB[3][:, 0, E:2 * E], ones, M[:, 0:E], start=False, stop=True)
                for t in range(LT):
                    ins = pe.matmul(MB[3][:, 0, 2 * E:3 * E], ones, M[:, t * E:(t + 1) * E], start=t == 0, stop=t == 1)
                ins.then_inc(m["ranks"], 1)
                pe.wait_ge(m["y_kept"], 1)
                for q in range(3):
                    pe.matmul(flat(MB[q]), ys[:, 0:P], ys, start=True, stop=False)
                pe.wait_ge(m["items_in"], 1)
                pe.transpose(MB[3][0:1, 1, 0:P], r_("item"), ident).then_inc(m["items_ps"], 1)

                def gather():
                    for t in range(LT):
                        for g in range(2):
                            ins = pe.matmul(bank[3][SLOTS * g:SLOTS * (g + 1), :], G[:, t, :], Kct[:, t, g * 512:(g + 1) * 512],
                                            start=t == 0, stop=t == 1, tile_position=(0, SLOTS * g))
                    ins.then_inc(m["gathered"], 1)

                def turn_rows():
                    for c in range(4):
                        ins = pe.transpose(bank[0][:, c * P:(c + 1) * P], xg[:, c * P:(c + 1) * P], ident)
                    ins.then_inc(m["xt_ps"], 1)

                def scatter(ks, done=None):
                    for k in ks:
                        g = slice(SLOTS * (k // 4), SLOTS * (k // 4 + 1))
                        ins = pe.matmul(MB[k // 2][:, k % 2, :], ys[g, (k % 4) * P:(k % 4 + 1) * P], S[g, :], start=False,
                                        stop=done == "acc_done" and k % 2 == 1, tile_position=(SLOTS * (k // 4), 0))
                        if done is not None and k in ks[-2:]:
                            ins.then_inc(m[done], 1)
                pe.wait_ge(m["u_rows"], 1)
                keep_clock(6, bank[3])
                pe.wait_ge(m["g_ready"], 1)
                gather()
                pe.wait_ge(m["diag_ready"], 1)
                for v in range(2):
                    ins = pe.matmul(bank[1 + v], ones, diag[:, v].rearrange("p q n -> p (q n)"), start=True, stop=True)
                ins.then_inc(m["bc_ps"], 1)
                pe.wait_ge(m["xg_kept"], 1)
                turn_rows()
                pe.wait_ge(m["s_ready"], 1)
                pe.wait_ge(m["items_ready"], 1)
                pe.matmul(flat(MB[3]), ys[:, 0:P], ys, start=True, stop=False)
                pe.wait_ge(m["bc_kept"], 1)
                T = pe.value_load(tab[0:1, 64:65], min_val=EXPERTS[n], max_val=EXPERTS[n] + 8)
                with pe.Fori(0, T) as i:
                    def gate_or_up(q, done):
                        for k in range(DT):
                            for g in range(2):
                                ins = pe.matmul(bank[q][SLOTS * g:SLOTS * (g + 1), 0:L],
                                                xts[:, k % 4, SLOTS * (k // 4):SLOTS * (k // 4 + 1)],
                                                ring[:, q, k * 512 + g * 256:k * 512 + (g + 1) * 256], start=k == 0,
                                                stop=k == DT - 1, tile_position=(0, SLOTS * g))
                        ins.then_inc(m[done], 1)
                    pe.wait_ge(m["xts_ready"], i + 1)
                    pe.wait_ge(m["wg_full"], i * 16 + 16)
                    gate_or_up(0, "gate_done")
                    pe.wait_ge(m["g_ready"], i + 2)
                    gather()
                    pe.wait_ge(m["wu_full"], i * 16 + 16)
                    gate_or_up(1, "up_done")
                    pe.wait_ge(m["xg_kept"], i + 2)
                    pe.wait_ge(m["sg_ready"], i + 1)
                    turn_rows()
                    pe.wait_ge(m["y_kept"], i + 1)
                    pe.wait_ge(m["s_ready"], i + 1)
                    scatter((0, 4, 1, 5))
                    pe.wait_ge(m["hid_ready"], i + 2)
                    for c in range(2):
                        ins = pe.transpose(bank[1][:, L + c * P:L + (c + 1) * P], hid[:, c * P:(c + 1) * P], ident)
                    ins.then_inc(m["ht_ps"], 1)
                    scatter((2, 6, 3, 7), "scattered")
                    pe.wait_ge(m["wd_full"], i * 16 + 16)
                    pe.wait_ge(m["ht_ready"], i + 1)
                    for k in range(4):
                        for g in range(2):
                            ins = pe.matmul(bank[2][SLOTS * g:SLOTS * (g + 1), :],
                                            hts[:, k % 2, SLOTS * (k // 2):SLOTS * (k // 2 + 1)],
                                            ring[:, 2, k * D + g * 512:k * D + (g + 1) * 512], start=k == 0, stop=k == 3,
                                            tile_position=(0, SLOTS * g))
                    ins.then_inc(m["down_done"], 1)
                pe.wait_ge(m["y_kept"], T + 1)
                pe.wait_ge(m["s_ready"], T + 1)
                scatter((0, 4, 1, 5, 2, 6, 3, 7), "acc_done")
                pe.wait_ge(m["xts_ready"], T + 1)
            J_uses = [[0, 0], [0, 0]]
            for n in range(2):
                for j in jobs:
                    if j["w"] < moe_w[n]:
                        J_uses[n][j["pair"]] = j["use"] + 1
            route_and_experts(0)
            mean_sums("ln2", hT)
            square_sums("ln2")
            square_sums("attn")
            pe.wait_ge(b2["ld"], 16 * 12)
            keep_clock(GAIN_WAIT - 4, bank[0])
            pe.matmul(flat(MB[2])[0:QH, 0:384], rel, hot, start=True, stop=True).then_inc(b2["relb_ps"], 1)
            out_wait(pe, "attn")
            for n in ("u2", "v2", "q2", "kv2", "gates2"):
                job(J[n, 0, 0])
            pe.wait_ge(b2["v_ready"], 1)
            pe.wait_ge(b2["ws_ready"], 1)
            for g in range(8):
                for c in range(LT):
                    ins = pe.matmul(MB[g // 4][64 * (g % 2):64 * (g % 2) + 64, (g // 2) % 2, c * P:(c + 1) * P],
                                    raw2[:, c, g * 64:(g + 1) * 64], ws[:, g, :], start=True, stop=True,
                                    tile_position=(0, 64 * (g % 2)))
            ins.then_inc(b2["sp_ps"], 1)

            def attn_scores(qb):
                if qb:
                    pe.wait_ge(b2["b_ready"], 1)
                else:
                    pe.wait_ge(b2["a_ready"], 1)
                    j = J["kv2", 0, 0]
                    pe.wait_ge(pair_free[j["pair"]], j["use"] + 1)
                per = 2 if qb else 4
                for h in range(QH):
                    at = 64 * (h // 4)
                    ins = pe.matmul(flat(MB[h // per])[:, (h % per) * (512 // per):(h % per + 1) * (512 // per)],
                                    q2[at:at + 64, h % 4, qb * P:(qb + 1) * P], k2[at:at + 64, 0:(qb + 1) * P],
                                    start=True, stop=True, tile_position=(at, 0))
                ins.then_inc(b2["sc_ps"], 1)

            def attn_turn(qb):
                pe.wait_ge(b2["p_ready"], qb + 1)
                i = 0
                for h in range(QH):
                    for kb in range(0 if qb else 1, 2):
                        ins = pe.transpose(flat(MB[i // 4])[:, (i % 4) * P:(i % 4 + 1) * P], Kc[:, h, kb * P:(kb + 1) * P], ident)
                        i += 1
                ins.then_inc(b2["p_turned"], 1)

            def attn_out(qb):
                pe.wait_ge(b2["p_kept"], qb + 1)
                n = qb + 1
                for h in range(QH):
                    for kb in range(n):
                        ins = pe.matmul(flat(MB[0])[64 * (h % 2):64 * (h % 2) + 64, (h // 2) * P:(h // 2 + 1) * P],
                                        v2[:, kb * P + 64 * (h // 4):kb * P + 64 * (h // 4) + 64],
                                        pT[:, (h * n + kb) * P:(h * n + kb + 1) * P], start=kb == 0, stop=kb == n - 1,
                                        tile_position=(0, 64 * (h % 2)))
                ins.then_inc(b2["b_ps"], 1)
            attn_scores(0)
            job(J["gates2", 1, 0])
            attn_turn(0)
            job(J["gates2", 2, 0])
            attn_out(0)
            attn_scores(1)
            job(J["gates2", 3, 0])
            attn_turn(1)
            job(J["pa", 0, 0])
            job(J["pa", 0, 1])
            attn_out(1)
            pe.wait_ge(b2["b_ready"], 2)
            job(J["pb", 0, 0])
            job(J["pb", 0, 1])
            pe.wait_ge(b2["m_ready"], 2)
            for b in range(2):
                job(J["out2", b, 0])
            square_sums("ffn")
            route_and_experts(1)
            square_sums("final")

        @block.vector
        def _(dve):
            V_ = nc.vector
            own = Own(dve, dve_own)
            link = own.link

            def evac(j, ins):
                say(dve, ins, pair_free[j["pair"]], j["use"] + 1)
            dve.wait_ge(ld_first, 32)

            def modulation(b):
                dve.wait_ge(ada_turned, b + 1)
                j = J["ada", b, 0]
                T = PP[j["pair"]][:, 2, 0:8].rearrange("p (c r) -> p c r", r=2)
                for r in range(2):
                    ins = V_.tensor_tensor(modT[:, r, 4 * b:4 * b + 4], T[:, :, r], vec[:, 4 * b:4 * b + 4], ALU.add)
                evac(j, ins)
                if b == 3:
                    say(dve, V_.tensor_scalar(modT[:, :, 8:16], modT[:, :, 8:16], 1.0, None, ALU.add), u_mod, 1)
                if b == 11:
                    link(V_.tensor_scalar(modT[:, 0, 32:40], modT[:, 0, 32:40], 1.0, None, ALU.add))
                    g, b_ = (vec[:, VCOLS[x]:VCOLS[x] + DT] for x in ("ln1_g", "ln1_b"))
                    link(V_.tensor_tensor(fold[:, 0, :], g, modT[:, 0, 32:40], ALU.mult))
                    link(V_.tensor_tensor(fold[:, 1, :], b_, modT[:, 0, 32:40], ALU.mult))
                    link(V_.tensor_tensor(fold[:, 1, :], fold[:, 1, :], modT[:, 0, 24:32], ALU.add))
                    link(V_.tensor_scalar(fold[:, 2, :], g, ALPHA, None, ALU.mult))
                    link(V_.tensor_scalar(fold[:, 3, :], b_, ALPHA, None, ALU.mult))
                    say(dve, V_.tensor_tensor(fold[:, 4, :], vec[:, VCOLS["b_mix"]:VCOLS["b_mix"] + DT], modT[:, 0, 16:24], ALU.mult), u_mod, 2)

            def keep_ada(b):
                job_wait(dve, J["ada", b, 0])
                if b >= 2:
                    dve.wait_ge(ada_turned, b - 1)
                say(dve, V_.tensor_copy(adaR[:, b % 2, :], PPt[J["ada", b, 0]["pair"]][:, 0, :]), ada_kept, b + 1)
            for b in range(4):
                keep_ada(b)
                if b:
                    modulation(b - 1)
            modulation(3)
            dve.wait_ge(ld_x, 16)
            for t in range(4, DT):
                ins = V_.tensor_scalar(uT[:, t, :], hT[:, t, :], modT[:, 0, 8 + t:9 + t], modT[:, 0, t:t + 1], ALU.mult, ALU.add)
            ins.then_inc(u_second, 1)
            dve.wait_ge(ld_rest, 32)
            x = rowc("decay", 16)
            say(dve, V_.scalar_tensor_tensor(lgs[:, 0, :], x, -1.0, x, ALU.mult, ALU.max), lg_abs, 1)
            dve.wait_ge(lg_exp, 1)
            link(V_.tensor_scalar(lgs[:, 2, :], lgs[:, 1, :], 2.0, None, ALU.add))
            link(V_.reciprocal(lgs[:, 2, :], lgs[:, 2, :]))
            link(V_.tensor_tensor(lgs[:, 1, :], lgs[:, 1, :], lgs[:, 2, :], ALU.mult))
            link(V_.tensor_tensor(lgs[:, 2, :], lgs[:, 1, :], lgs[:, 1, :], ALU.mult))
            link(V_.tensor_scalar(lgs[:, 3, :], lgs[:, 2, :], 1 / 17, None, ALU.mult))
            for c in (15, 13, 11, 9, 7, 5, 3):
                link(V_.scalar_tensor_tensor(lgs[:, 3, :], lgs[:, 3, :], 1 / c, lgs[:, 2, :], ALU.add, ALU.mult))
            link(V_.scalar_tensor_tensor(lgs[:, 3, :], lgs[:, 3, :], 1.0, lgs[:, 1, :], ALU.add, ALU.mult))
            link(V_.tensor_scalar(lgs[:, 4, :], x, 0.0, None, ALU.min))
            link(V_.scalar_tensor_tensor(lg, lgs[:, 3, :], -2.0, lgs[:, 4, :], ALU.mult, ALU.add))
            for m in range(LT):
                for d in range(2):
                    ins = V_.tensor_scalar(wctx[:, m, d, :], lg[:, 8 * d:8 * d + 8], cst("mctx", 4)[:, 2 * m + d:2 * m + d + 1],
                                           None, ALU.mult)
            say(dve, ins, lg_ready, 1)

            def convolve(first, last):
                for step in range(first, min(last, DT * TAPS)):
                    t, k = step // TAPS, step % TAPS
                    tap = col("taps", step)
                    if k == 0:
                        ins = V_.tensor_scalar(conv[:, t, :], zpad[:, t, 0:L], tap, col("conv_b", t), ALU.mult, ALU.add)
                    else:
                        ins = V_.scalar_tensor_tensor(conv[:, t, :], zpad[:, t, k:k + L], tap, conv[:, t, :], ALU.mult, ALU.add)
                    if step < DT * TAPS - 1:
                        link(ins)
                    else:
                        ln_say(dve, ins, "conv", "in", 1)
                        dve.sem_inc(LN["in"], 1)
            dve.wait_ge(zeroed, 3)
            for b in range(4):
                j = J["glu", b, 0]
                dve.wait_ge(sig_ready, b + 1)
                for i in range(2):
                    ins = V_.scalar_tensor_tensor(zpad[:, 2 * b + i, HALO:HALO + L], PP[j["pair"]][:, i, :],
                                                  col("b_za", 2 * b + i), raw[:, 2 * (b % 2) + i, :], ALU.add, ALU.mult)
                evac(j, ins)
                convolve(b * A_JOB, (b + 1) * A_JOB)

            def rope(r):
                dst = (kT, qT)[r // 2][:, 4 * (r % 2):4 * (r % 2) + 4, :]
                cos4, sin2 = (cst(n, L).unsqueeze(1).to_broadcast([P, k, L]) for n, k in (("cos", 4), ("sin", 2)))
                dve.wait_ge(raw_rot, r + 1)
                V_.tensor_tensor(Eqd[:, :, :], raw[:, :, :], cos4, ALU.mult)
                for q in range(2):
                    ins = V_.tensor_tensor(dst[:, 2 * q:2 * q + 2, :], MB[q][:, :, :], sin2, ALU.mult)
                link(ins)
                say(dve, V_.tensor_tensor(dst, dst, Eqd[:, :, :], ALU.add), rope_done, r + 1)

            def with_bias(j, n, dst):
                job_wait(dve, j)
                dve.wait_ge(bias_full[n % 2], 16 * (n // 2 + 1))
                evac(j, V_.tensor_tensor(dst, PPt[j["pair"]], biasr[:, n % 2, :].unsqueeze(1).to_broadcast([P, LT, 512]), ALU.add))

            for b in range(2):
                with_bias(J["k", b, 1], b, Kct[:, :, b * 512:(b + 1) * 512])
                rope(b)
                convolve(4 * A_JOB + 2 * b * A_JOB, 4 * A_JOB + 2 * (b + 1) * A_JOB)
            rope(2)
            convolve(8 * A_JOB, 9 * A_JOB)
            rope(3)
            k4 = kw[:, :, :].rearrange("p a n -> p (a n)").rearrange("p (a n) -> p a n", n=P)

            def decay(h):
                q = 2 * (h % 2)
                f = Ddec[:, q:q + 2, :].rearrange("p a n -> p (a n)")
                link(V_.scalar_tensor_tensor(f, cst("dpos", 512), lg[:, h:h + 1], cst("ln2", 512), ALU.mult, ALU.add))
                say(dve, V_.scalar_tensor_tensor(f, cst("dneg", 512), lg[:, 8 + h:9 + h], f, ALU.mult, ALU.add), dec_arg, h + 1)

            def decay_k(h):
                if h >= 2:
                    dve.wait_ge(s0_ps, h - 1)
                for d in range(2):
                    for m in range(LT):
                        ins = V_.tensor_scalar(k4[:, 4 * (h % 2) + 2 * d + m, :], Kct[:, m, h * P:(h + 1) * P],
                                               wctx[:, m, d, h:h + 1], KSCALE, ALU.mult, ALU.mult)
                ins.then_inc(k_decayed, 1)

            def decay_q(h):
                q = 2 * (h % 2)
                if h >= 2:
                    dve.wait_ge(o_ps, h - 1)
                dve.wait_ge(eq_ready, h + 1)
                V_.tensor_tensor(qd[:, q:q + 2, :], Eqd[:, q:q + 2, :], qT[:, h, :].unsqueeze(1).to_broadcast([P, 2, L]),
                                 ALU.mult).then_inc(q_decayed, 1)
            dve.wait_ge(wctx_exp, 1)
            for h in range(2):
                decay(h)
                decay_k(h)
                decay_q(h)
            for b in range(4):
                with_bias(J["v", b, 0], 2 + b, Vt[:, :, b * 512:(b + 1) * 512])
                convolve((9 + 2 * b) * A_JOB, (10 + 2 * b) * A_JOB)
                with_bias(J["v", b, 1], 2 + b, Vct[:, :, b * 512:(b + 1) * 512])
                convolve((10 + 2 * b) * A_JOB, (11 + 2 * b) * A_JOB)
            def stats(h):
                dve.wait_ge(o_kept, h + 1)
                for t in range(LT):
                    ins = V_.bn_stats(bst[:, t, :], On[:, t, h * DV:(h + 1) * DV])
                link(ins)
                for t in range(LT):
                    ins = V_.bn_aggr(mv[:, t, h, :], bst[:, t, :])
                say(dve, ins, o_stat, h + 1)
            for h in range(HEADS):
                dve.wait_ge(dec_ready, h + 1)
                dve.wait_ge(sc_ps, h + 1)
                q = 2 * (h % 2)
                say(dve, V_.scalar_tensor_tensor(Ph[:, q:q + 2, :], MB[1][:, :, :], KSCALE, Ddec[:, q:q + 2, :], ALU.mult,
                                                 ALU.mult), p_sb, h + 1)
                if h + 2 < HEADS:
                    decay(h + 2)
                    decay_k(h + 2)
                keep_ada(4 + h)
                if h:
                    modulation(3 + h)
                    stats(h - 1)
                if h + 2 < HEADS:
                    decay_q(h + 2)
            modulation(11)
            stats(HEADS - 1)
            say(dve, V_.tensor_scalar(rstd[:, :].rearrange("p (t h) -> p t h", t=LT), mv[:, :, :, 1], LN_EPS, None, ALU.add),
                var_ready, 1)
            dve.wait_ge(std_ready, 1)
            link(V_.reciprocal(rstd[:, :], rstd[:, :]))
            for t in range(LT):
                for h in range(HEADS):
                    o = On[:, t, h * DV:(h + 1) * DV]
                    ins = V_.tensor_scalar(o, o, mv[:, t, h, 0:1], rstd[:, t * HEADS + h:t * HEADS + h + 1], ALU.subtract, ALU.mult)
            link(ins)
            for b in range(4):
                with_bias(J["g", b, 0], 6 + b, raw2)
                dve.wait_ge(g_silu, b + 1)
                o = On[:, :, b * 512:(b + 1) * 512]
                say(dve, V_.tensor_tensor(o, o, raw2, ALU.mult), ret_ready, b + 1)

            def centre(name, src):
                ln_wait(dve, name, "mean", 1)
                for half in range(2):
                    h = slice(4 * half, 4 * half + 4)
                    V_.tensor_tensor(src[:, h, :], src[:, h, :], MB[0][:, 0:1, :].to_broadcast([P, 4, L]), ALU.subtract
                                     ).then_inc(LN["centred"], 1)

            def divide(name, src, dst):
                ln_wait(dve, name, "rooted", 1)
                if name in MEAN:
                    ln_wait(dve, name, "centred", 2)
                link(V_.reciprocal(rs[:, :], rs[:, :]))
                for half in range(2):
                    h = slice(4 * half, 4 * half + 4)
                    ln_say(dve, V_.tensor_tensor(dst[:, h, :], src[:, h, :], rs[:, :].unsqueeze(1).to_broadcast([P, 4, L]),
                                                 ALU.mult), name, "divided", half + 1)

            def gains(name, src, dst, scale, bias):
                for t in range(4, DT):
                    if bias is None:
                        ins = V_.tensor_scalar(dst[:, t, :], src[:, t, :], scale(t), None, ALU.mult)
                    else:
                        ins = V_.tensor_scalar(dst[:, t, :], src[:, t, :], scale(t), bias(t), ALU.mult, ALU.add)
                ln_say(dve, ins, name, "out_v", 1)

            def ret(b):
                j = J["ret", b, 0]
                job_wait(dve, j)
                g3 = J["gates", 3, 0]
                dve.wait_ge(pair_free[g3["pair"]], g3["use"] + 1)
                evac(j, V_.tensor_tensor(mT[:, 2 * b:2 * b + 2, :], PP[j["pair"]][:, 0:2, :], gT[:, 2 * b:2 * b + 2, :], ALU.mult))
            centre("conv", conv)
            ret(0)
            ret(1)
            divide("conv", conv, conv)
            ret(2)
            ret(3)
            for t in range(DT):
                V_.tensor_scalar(hT[:, t, :], hT[:, t, :], ALPHA, fold[:, 4, t:t + 1], ALU.mult, ALU.add).then_inc(h_scaled, 1)
            for b in range(2):
                j = J["cout", b, 0]
                job_wait(dve, j)
                for i in range(4):
                    ins = V_.scalar_tensor_tensor(raw[:, i, :], PP[j["pair"]][:, i, :], col("b_conv", 4 * b + i),
                                                  gT[:, 8 + 4 * b + i, :], ALU.add, ALU.mult)
                evac(j, ins)
                m4 = mT[:, 4 * b:4 * b + 4, :]
                say(dve, V_.tensor_tensor(m4, m4, raw[:, :, :], ALU.add), mix_in, b + 1)
            dve.wait_ge(h_scaled, DT)
            for b in range(2):
                j = J["mix", b, 0]
                job_wait(dve, j)
                for i in range(4):
                    t = 4 * b + i
                    ins = V_.scalar_tensor_tensor(hT[:, t, :], PP[j["pair"]][:, i, :], modT[:, 0, 16 + t:17 + t], hT[:, t, :],
                                                  ALU.mult, ALU.add)
                ins.then_inc(pair_free[j["pair"]], 1)
                dve.wait_ge(pair_free[j["pair"]], j["use"] + 1)
                dve.sem_inc(LN["in"], 1)

            def first_of(out, val, top, n):
                eq, c = (r_(x).rearrange("p (t n) -> p t n", t=LT)[:, :, 0:n] for x in ("eq", "c"))
                link(V_.tensor_tensor(eq, val, top.unsqueeze(2).to_broadcast([P, LT, n]), ALU.is_equal))
                link(V_.scalar_tensor_tensor(c, eq, -64.0, cst("slot", n).unsqueeze(1).to_broadcast([P, LT, n]), ALU.mult, ALU.add))
                link(V_.tensor_reduce(r_("cm"), c, AX.X, ALU.min))
                link(V_.tensor_tensor(out, c, r_("cm").unsqueeze(2).to_broadcast([P, LT, n]), ALU.is_equal))

            def route(n):
                m, E = moe[n], EXPERTS[n]
                EG = E // GROUPS
                t2 = lambda x, w: r_(x)[:, 0:LT * w].rearrange("p (t n) -> p t n", t=LT)
                t4 = lambda x: r_(x)[:, 0:LT * E].rearrange("p (t g n) -> p t g n", t=LT, g=GROUPS)
                V_.memset(lgT, 0.0)
                V_.memset(ys, 0.0).then_inc(m["y_kept"], 1)
                V_.memset(S, 0.0).then_inc(m["s_ready"], 1)
                V_.tensor_copy(slotno, cst("slot", SLOTS + 1))
                dve.wait_ge(m["logits"], 1)
                cols = GROUPS + E
                dve.wait_ge(m["logits_kept"], 1)
                V_.tensor_copy(lgT[64:64 + cols, :], MB[2][64:64 + cols, 0, :]).then_inc(m["logits_kept"], 1)
                dve.wait_ge(m["logits_turned"], 1)
                lt = t2("lt", cols)
                turned = MB[2][:, 1, :].rearrange("p (t c) -> p t c", t=LT)
                link(V_.tensor_tensor(lt, turned[:, :, 0:cols], rowc(f"rb{n}", cols).unsqueeze(1).to_broadcast([P, LT, cols]), ALU.add))
                link(V_.tensor_tensor(lt, turned[:, :, 64:64 + cols], lt, ALU.add))
                link(V_.tensor_reduce(r_("gm"), lt[:, :, 0:GROUPS], AX.X, ALU.max))
                say(dve, V_.tensor_tensor(t2("gd", GROUPS), lt[:, :, 0:GROUPS], r_("gm").unsqueeze(2).to_broadcast([P, LT, GROUPS]),
                                          ALU.subtract), m["gexp_in"], 1)
                first_of(t2("hg", GROUPS), lt[:, :, 0:GROUPS], r_("gm"), GROUPS)
                hg = t2("hg", GROUPS).unsqueeze(3).to_broadcast([P, LT, GROUPS, EG])
                tmp = r_("tmp")[:, 0:LT * E].rearrange("p (t g n) -> p t g n", t=LT, g=GROUPS)
                le = lt[:, :, GROUPS:GROUPS + E].rearrange("p t (g n) -> p t g n", g=GROUPS)
                link(V_.tensor_tensor(tmp, le, hg, ALU.mult))
                ml = t2("ml", EG)
                link(V_.tensor_reduce(ml, tmp.rearrange("p t g n -> p t n g"), AX.X, ALU.add))
                link(V_.tensor_reduce(r_("m1"), ml, AX.X, ALU.max))
                first_of(t2("h1", EG), ml, r_("m1"), EG)
                link(V_.scalar_tensor_tensor(ml, t2("h1", EG), MASKED, ml, ALU.mult, ALU.add))
                link(V_.tensor_reduce(r_("m2"), ml, AX.X, ALU.max))
                say(dve, V_.tensor_tensor(r_("e2"), r_("m2"), r_("m1"), ALU.subtract), m["eexp_in"], 1)
                first_of(t2("h2", EG), ml, r_("m2"), EG)
                for A, h in (("A1", "h1"), ("A2", "h2")):
                    link(V_.tensor_tensor(t4(A), t2(h, EG).unsqueeze(2).to_broadcast([P, LT, GROUPS, EG]), hg, ALU.mult))
                say(dve, V_.tensor_tensor(r_("M")[:, 0:2 * E], r_("A1")[:, 0:2 * E], r_("A2")[:, 0:2 * E], ALU.add), m["hot_ready"], 1)
                dve.wait_ge(m["gexp_out"], 1)
                link(V_.tensor_reduce(r_("gw"), t2("gd", GROUPS), AX.X, ALU.add))
                dve.wait_ge(m["eexp_out"], 1)
                link(V_.scalar_tensor_tensor(r_("w1"), r_("e2"), 1.0, r_("gw"), ALU.add, ALU.mult))
                link(V_.reciprocal(r_("w1"), r_("w1")))
                link(V_.tensor_tensor(r_("w2"), r_("w1"), r_("e2"), ALU.mult))
                Sa, Sb = (r_(x).rearrange("p (t n) -> p t n", t=2) for x in ("Sa", "Sb"))
                V_.memset(r_("Sa"), 0.0)
                link(V_.memset(r_("Sb"), 0.0))
                dve.wait_ge(m["ranks"], 1)
                cnt, items = Sa[:, 0, 16:16 + E], Sa[:, 1, 16:16 + E]
                link(V_.tensor_scalar(cnt, MB[3][:, 0, 2 * E:3 * E], float(D), None, ALU.mult))
                link(V_.tensor_scalar(r_("rank")[:, 0:2 * E], MB[3][:, 0, 0:2 * E], float(D), None, ALU.mult))
                link(V_.tensor_scalar(items, cnt, float(SLOTS), 1.0, ALU.is_gt, ALU.add))
                for c in (2, 3):
                    link(V_.scalar_tensor_tensor(items, cnt, float(c * SLOTS), items, ALU.is_gt, ALU.add))
                A, B, step = Sa, Sb, 1
                while step < E:
                    link(V_.tensor_tensor(B[:, 1, 16:16 + E], A[:, 1, 16:16 + E], A[:, 1, 16 - step:16 + E - step], ALU.add))
                    A, B, step = B, A, 2 * step
                first, total = A[:, 1, 15:15 + E], A[:, 1, 15 + E:16 + E]
                link(V_.tensor_scalar(r_("vx")[:, 0:E], first, cst("pcol", 1), None, ALU.is_le))
                link(V_.tensor_reduce(r_("item"), r_("vx")[:, 0:E], AX.X, ALU.add))
                say(dve, V_.tensor_scalar(r_("item"), r_("item"), -1.0, None, ALU.add), m["items_in"], 1)
                vx, rank, pos = t2("vx", E), t2("rank", E), r_("pos")
                link(V_.scalar_tensor_tensor(vx, first.unsqueeze(1).to_broadcast([P, LT, E]), float(SLOTS), rank, ALU.mult, ALU.add))
                for k, A_ in enumerate(("A1", "A2")):
                    link(V_.tensor_tensor(t2("tmp", E), t2(A_, E), vx, ALU.mult))
                    link(V_.tensor_reduce(pos[:, 2 * k:2 * k + 2], t2("tmp", E), AX.X, ALU.add))

                def rows_of_item(linked):
                    linked(V_.tensor_tensor(Ek, slotno[:, 0:SLOTS].unsqueeze(1).to_broadcast([P, 4, SLOTS]),
                                            pos.unsqueeze(2).to_broadcast([P, 4, SLOTS]), ALU.is_equal))
                    V_.tensor_tensor(G, Ek[:, 0:2], Ek[:, 2:4], ALU.add).then_inc(m["g_ready"], 1)
                rows_of_item(link)
                for v, x in ((0, pos), (1, rt[:, RT["w1"]:RT["w1"] + 4])):
                    ins = V_.tensor_tensor(diag[:, v], ident.unsqueeze(1).to_broadcast([P, 4, P]),
                                           x.unsqueeze(2).to_broadcast([P, 4, P]), ALU.mult)
                ins.then_inc(m["diag_ready"], 1)
                link(V_.tensor_scalar(slotno, slotno, float(SLOTS), None, ALU.add))
                dve.wait_ge(m["items_ps"], 1)
                V_.tensor_copy(tab[0:1, 64:65], total[0:1])
                say(dve, V_.tensor_copy(tab[0:1, 0:64], MB[3][0:1, 1, 0:64]), m["items_ready"], 1)
                dve.wait_ge(m["gathered"], 1)
                rows_of_item(link)
                if n == 0:
                    for t in range(DT):
                        ins = V_.tensor_scalar(hT[:, t, :], hT[:, t, :], fold[:, 2, t:t + 1], fold[:, 3, t:t + 1], ALU.mult, ALU.add)
                    link(ins)
                dve.sem_inc(m["hid_ready"], 1)
                dve.wait_ge(m["bc_kept"], 1)
                T = dve.value_load(tab[0:1, 64:65], min_val=E, max_val=E + 8)
                with dve.Fori(0, T) as i:
                    steps = [0]

                    def linked(ins):
                        steps[0] += 1
                        ins.then_inc(m["step"], 1)
                        dve.wait_ge(m["step"], i * 4 + steps[0])
                    linked(V_.tensor_scalar(slotno, slotno, float(SLOTS), None, ALU.add))
                    dve.wait_ge(m["gathered"], i + 2)
                    rows_of_item(linked)
                    dve.wait_ge(m["sg_ready"], i + 1)
                    dve.wait_ge(m["up_done"], i + 1)
                    V_.tensor_tensor(hid, bank[1][:, 0:L], sg, ALU.mult).then_inc(m["hid_ready"], 1)
                    dve.wait_ge(m["scattered"], i * 2 + 2)
                    for k in range(2):
                        linked(V_.scalar_tensor_tensor(Sk[:, k], placer[:, k], slotno[:, SLOTS:SLOTS + 1], weightr[:, k],
                                                       ALU.is_equal, ALU.mult))
                    V_.tensor_tensor(S, Sk[:, 0], Sk[:, 1], ALU.add).then_inc(m["s_ready"], 1)
                    dve.wait_ge(m["down_done"], i + 1)
                    V_.tensor_copy(ys, bank[2]).then_inc(m["y_kept"], 1)
                dve.wait_ge(m["acc_done"], 2)
                for k in range(DT):
                    if n == 0:
                        ins = V_.scalar_tensor_tensor(hT[:, k, :], MB[k // 2][:, k % 2, :], modT[:, 0, 40 + k:41 + k], hT[:, k, :],
                                                      ALU.mult, ALU.add)
                    else:
                        ins = V_.tensor_tensor(hT[:, k, :], MB[k // 2][:, k % 2, :], hT[:, k, :], ALU.add)
                    if k % 4 == 3:
                        ln_say(dve, ins, ("ln2", "final")[n], "in", k // 4 + 1)
            centre("ln1", hT)
            divide("ln1", hT, hT)
            gains("ln1", hT, uT, lambda t: fold[:, 0, t:t + 1], lambda t: fold[:, 1, t:t + 1])
            route(0)
            centre("ln2", hT)
            divide("ln2", hT, hT)
            gains("ln2", hT, hT, lambda t: col("ln2_g", t), lambda t: col("ln2_b", t))
            divide("attn", hT, uT)
            gains("attn", uT, uT, lambda t: col("attn_g", t), None)
            dve.wait_ge(b2["relb_ps"], 1)
            dve.wait_ge(b2["ld"], 16 * 12)
            say(dve, V_.tensor_tensor(relb, flat(MB[2])[0:QH, 0:384], outside, ALU.add), b2["relb_sb"], 1)
            say(dve, V_.tensor_tensor(ws, ws, cst("causal", P).unsqueeze(1).to_broadcast([P, 8, P]), ALU.mult), b2["ws_ready"], 1)
            j = J["v2", 0, 0]
            dve.wait_ge(pair_free[j["pair"]], j["use"] + 1)
            for t in range(LT):
                ins = V_.bn_stats(bst[:, t, :], raw2[:, t, :])
            link(ins)
            for t in range(LT):
                ins = V_.bn_aggr(mv[:, t, 0, :], bst[:, t, :])
            link(ins)
            out_wait(dve, "attn")
            say(dve, V_.tensor_scalar(rs[:, 0:2], mv[:, :, 0, 1], RMS_EPS, None, ALU.add), b2["vvar"], 1)
            dve.wait_ge(b2["vstd"], 1)
            link(V_.reciprocal(rs[:, 0:2], rs[:, 0:2]))
            for t in range(LT):
                ins = V_.tensor_scalar(raw2[:, t, :], raw2[:, t, :], mv[:, t, 0, 0:1], rs[:, t:t + 1], ALU.subtract, ALU.mult)
            link(ins)
            say(dve, V_.tensor_tensor(raw2, raw2, rowc("gm_g", 512).unsqueeze(1).to_broadcast([P, LT, 512]), ALU.mult),
                b2["v_ready"], 1)
            dve.wait_ge(b2["sp_ps"], 1)
            for q in range(2):
                bias = flat(Ph)[:, 0:512].rearrange("p (a t) -> p a t", a=4)[:, 2 * q:2 * q + 2, :]
                ins = V_.tensor_tensor(aT[:, 2 * q:2 * q + 2, :].rearrange("p a (c t) -> p a c t", c=2),
                                       MB[q][:, :, :].rearrange("p a (c t) -> p a c t", c=2),
                                       bias.unsqueeze(2).to_broadcast([P, 2, LT, P]), ALU.add)
            link(ins)
            say(dve, V_.tensor_tensor(aT, aT, gu, ALU.mult), b2["a_ready"], 1)
            dve.wait_ge(b2["relb_full"], 16 * QH)
            for qb in range(2):
                dve.wait_ge(b2["sc_ps"], qb + 1)
                if qb:
                    dve.wait_ge(b2["p_turned"], 1)
                w0, per = (0, 2) if qb else (P, 4)
                sc = Kc[:, :, w0:L]
                for q in range(QH // per):
                    h = slice(q * per, (q + 1) * per)
                    ins = V_.tensor_tensor(Kc[:, h, w0:L], flat(MB[q]).rearrange("p (a n) -> p a n", a=per),
                                           RA[:, DT + q * per:DT + (q + 1) * per, w0:L], ALU.add)
                link(ins)
                link(V_.tensor_reduce(r_("mx"), sc, AX.X, ALU.max))
                link(V_.tensor_tensor(r_("mx"), r_("mx"), rowc("sinks", QH), ALU.max))
                V_.tensor_tensor(r_("sk"), rowc("sinks", QH), r_("mx"), ALU.subtract)
                say(dve, V_.tensor_tensor(sc, sc, r_("mx").unsqueeze(2).to_broadcast([P, QH, L - w0]), ALU.subtract),
                    b2["sc_sb"], qb + 1)
                dve.wait_ge(b2["p_exp"], qb + 1)
                link(V_.tensor_reduce(r_("den"), sc, AX.X, ALU.add))
                link(V_.tensor_tensor(r_("den"), r_("den"), r_("sk"), ALU.add))
                link(V_.reciprocal(r_("den"), r_("den")))
                say(dve, V_.tensor_tensor(sc, sc, r_("den").unsqueeze(2).to_broadcast([P, QH, L - w0]), ALU.mult),
                    b2["p_ready"], qb + 1)
                dve.wait_ge(b2["b_ps"], qb + 1)
                say(dve, V_.tensor_copy(bT[:, :, qb * P:(qb + 1) * P], flat(MB[0]).rearrange("p (a n) -> p a n", a=4)),
                    b2["b_ready"], qb + 1)
            g3 = J["gates2", 3, 0]
            dve.wait_ge(pair_free[g3["pair"]], g3["use"] + 1)
            for half in range(2):
                j = J["pa", 0, half]
                job_wait(dve, j)
                evac(j, V_.tensor_tensor(mT[:, 4 * half:4 * half + 4, :], PP[j["pair"]][:, :, :],
                                         gT[:, 4 * half:4 * half + 4, :], ALU.mult))
            for half in range(2):
                j = J["pb", 0, half]
                job_wait(dve, j)
                evac(j, V_.tensor_tensor(raw[:, :, :], PP[j["pair"]][:, :, :], gT[:, 8 + 4 * half:12 + 4 * half, :], ALU.mult))
                m4 = mT[:, 4 * half:4 * half + 4, :]
                say(dve, V_.tensor_tensor(m4, m4, raw[:, :, :], ALU.add), b2["m_ready"], half + 1)
            for b in range(2):
                j = J["out2", b, 0]
                job_wait(dve, j)
                h4 = hT[:, 4 * b:4 * b + 4, :]
                evac(j, V_.tensor_tensor(h4, PP[j["pair"]][:, :, :], h4, ALU.add))
                dve.sem_inc(LN["in"], 1)
            divide("ffn", hT, uT)
            gains("ffn", uT, uT, lambda t: col("ffn_g", t), None)
            route(1)
            divide("final", hT, uT)
            gains("final", uT, uT, lambda t: col("final_g", t), None)


def blocks(w, width=512):
    K, N = w.shape
    return np.ascontiguousarray(w.reshape(K // P, P, N // width, width).transpose(2, 1, 0, 3)).reshape(N // width, P, -1)


def tiles(x):
    n = x.shape[-1] // P
    return np.ascontiguousarray(np.moveaxis(x.reshape(-1, n, P), (0, 1, 2), (2, 1, 0)))


def bucket(dist):
    large = 16 + (np.log(np.maximum(dist, 1).astype(np.float32) / np.float32(16)) / np.float32(np.log(8.0)) * np.float32(16)).astype(np.int32)
    return np.where(dist < 16, dist, np.minimum(large, 31))


def constants():
    f = np.float32
    c = np.zeros((P, NC), f)

    def put(name, value):
        value = np.asarray(value, f).reshape(P, -1)
        c[:, CCOLS[name]:CCOLS[name] + value.shape[1]] = value
    p = np.arange(P)
    put("ident", np.eye(P))
    put("ones", np.full((P, P), 1.0 / D))
    rot = np.zeros((P, P))
    rot[p[64:], p[:64]] = -1.0
    rot[p[:64], p[64:]] = 1.0
    put("rot", rot)
    pos = np.arange(L)
    inv = (f(10000.0) ** (-np.arange(32, dtype=f) / f(32))).astype(f)
    ang = np.concatenate([(pos // 64).astype(f)[:, None] * inv, (pos % 64).astype(f)[:, None] * inv], axis=1).astype(f)
    ang = np.concatenate([ang, ang], axis=1)
    put("cos", np.cos(ang).T)
    put("sin", np.sin(ang).T)
    m = p[:, None, None] + P * np.arange(LT)[None, :, None]
    n = pos[None, None, :]
    put("dpos", np.maximum(n - m, 0))
    put("dneg", np.maximum(m - n, 0))
    put("ln2", (m == n) * np.log(2.0))
    put("nfb", np.broadcast_to(np.concatenate([pos + 1, L - pos]), (P, 2 * L)))
    put("mctx", np.stack([L - 1 - m[:, :, 0], m[:, :, 0]], axis=2))
    put("causal", p[:, None] <= p[None, :])
    put("tri", (p[:, None] < p[None, :]) / D)
    put("pcol", p)
    put("pick", p[:, None] % 32 == np.arange(2))
    put("eps", np.broadcast_to(np.array([LN_EPS, RMS_EPS]), (P, 2)))
    put("slot", np.concatenate([np.broadcast_to(np.arange(SLOTS), (P, SLOTS)), (p % SLOTS - 2 * SLOTS)[:, None]], axis=1))
    return c


def layout(i):
    i = {k: np.asarray(v) for k, v in i.items()}
    d = {}
    w_in, b_in = i["w_in"][0], i["b_in"][0]
    cut = np.cumsum([0, 1024, 1024, 2048, 2048, 1024, 1024, 2048])
    q, k, v, g, za, zb, gates = (slice(cut[n], cut[n + 1]) for n in range(7))
    d["w_ada"] = blocks(i["w_ada"][0])
    d["w_q"], d["w_k"], d["w_v"], d["w_g"], d["w_gates"] = (blocks(w_in[:, s]) for s in (q, k, v, g, gates))
    d["w_glu"] = blocks(np.stack([w_in[:, za].reshape(D, 4, 256), w_in[:, zb].reshape(D, 4, 256)], axis=2).reshape(D, 2 * D))
    d["w_ret"] = blocks(i["w_ret_out"][0], 256)
    d["w_cout"], d["w_mix"] = blocks(i["w_conv_out"][0]), blocks(i["w_mix_out"][0])
    vecs = [i["b_ada"][0], b_in[q], b_in[k], b_in[za], b_in[zb], b_in[gates], i["conv_dw_b"][0], i["conv_ln_g"][0],
            i["conv_ln_b"][0], i["b_conv_out"][0], i["b_mix_out"][0], i["ln1_g"][0], i["ln1_b"][0], i["ln2_g"][0],
            i["ln2_b"][0], i["attn_norm_g_2"][0], i["ffn_norm_g_2"][0], i["final_norm_g_2"]]
    taps = i["conv_dw"][0].reshape(TAPS, DT, P).transpose(2, 1, 0).reshape(P, -1)
    d["vec"] = np.concatenate([tiles(x)[:, :, 0] for x in vecs] + [taps], axis=1)
    d["rows"] = np.concatenate([i["ret_decay_fwd"][0], i["ret_decay_bwd"][0], i["b_router_grp"][0], i["b_router_exp"][0],
                                i["router_group_b_2"][0], i["router_expert_b_2"][0].ravel(), i["attn_sinks_2"][0],
                                i["gm_v_norm_g_2"][0]])[None]
    d["bias_rows"] = np.concatenate([b_in[k], b_in[v], b_in[g]])[None]
    d["wr0"] = np.concatenate([i["w_router_grp"][0], i["w_router_exp"][0]], axis=1).reshape(DT, P, 36).transpose(1, 0, 2)
    d["wr1"] = np.concatenate([i["router_group_w_2"][0], i["router_expert_w_2"][0].transpose(1, 0, 2).reshape(D, 16)],
                              axis=1).reshape(DT, P, 20).transpose(1, 0, 2)
    d["xT"], d["ctxT"] = tiles(i["x"][0]), tiles(i["ctx"][0])
    d["cT"] = np.concatenate([tiles(i["c"]), tiles(i["c_ctx"][None])], axis=2)
    for n, (x, y, z) in enumerate((("w_exp_gate", "w_exp_up", "w_exp_down"), ("expert_w_gate_2", "expert_w_up_2", "expert_w_down_2"))):
        E = EXPERTS[n]
        s = np.empty((E, 3, P, BLK), np.float32)
        s[:, 0] = i[x][0].reshape(E, DT, P, 512).transpose(0, 2, 1, 3).reshape(E, P, BLK)
        s[:, 1] = i[y][0].reshape(E, DT, P, 512).transpose(0, 2, 1, 3).reshape(E, P, BLK)
        s[:, 2] = i[z][0].reshape(E, 4, P, D).transpose(0, 2, 1, 3).reshape(E, P, BLK)
        d[f"w_moe{n}"] = s.reshape(3 * E, P, BLK)
    w2 = i["w_in_2"][0]
    d["w_u2"], d["w_v2"] = blocks(w2[:, 0:512]), blocks(w2[:, 512:1024])
    d["w_q2"] = blocks(w2[:, 1024:1536].reshape(D, 2, 4, HD).transpose(0, 2, 1, 3).reshape(D, 512))
    d["w_kv2"] = blocks(w2[:, 1536:1792], 256)
    d["w_gates2"] = blocks(w2[:, 1792:3840])
    d["w_pa"], d["w_pb"] = blocks(i["w_proj_a_2"][0], 1024), blocks(i["w_proj_b_2"][0], 1024)
    d["w_out2"] = blocks(i["w_out_2"][0])
    d["ws"] = i["gm_w_spatial_2"][0].transpose(2, 0, 1)
    d["gm_b"] = i["gm_b_spatial_2"][0].reshape(1, -1)
    d["const"] = constants()
    dist = 255 - np.arange(384)
    ok = (dist >= 0) & (dist < P)
    hot = np.zeros((32, 384), np.float32)
    hot[bucket(dist[ok]), np.arange(384)[ok]] = 1.0
    d["hot"] = hot
    d["outside"] = np.broadcast_to(np.where(ok, 0.0, MASKED).astype(np.float32), (QH, 384))
    d["rel"] = i["rel_bias_2"]
    return {k: np.ascontiguousarray(v) for k, v in d.items()}


def kernel(**inputs):
    import concourse.bacc as bacc
    from concourse.bass_utils import run_bass_kernel_spmd

    nc = bacc.Bacc("TRN2", target_bir_lowering=False, num_devices=1)
    arrays = layout(inputs)
    a = {n: nc.dram_tensor(f"in_{n}", x.shape, mybir.dt.from_np(x.dtype), kind="ExternalInput").ap() for n, x in arrays.items()}
    a["out"] = nc.dram_tensor("out", (P, DT, L), F32, kind="ExternalOutput").ap()
    build(nc, a)
    r = run_bass_kernel_spmd(nc, [{f"in_{n}": x for n, x in arrays.items()}], core_ids=[0])
    out = r.results[0]["out"]
    return np.ascontiguousarray(out.transpose(2, 1, 0)).reshape(1, L, D)
```
